# Optimizing a Trainium2 kernel written in Bass

```python
import math
import jax
import jax.numpy as jnp
from jax import lax
import numpy as np

D_MODEL = 1024
BATCH = 1
SEQ = 2048
DEPTH = 1

GRID_W = 64
CTX_LEN = 256
N_HEADS = 8
HEAD_DIM = 64
D_ATTN = N_HEADS * HEAD_DIM
D_HYENA = 512
HYENA_ORDER = 2
FILTER_HIDDEN = 64
POS_BANDS = 16
POS_FEATS = 1 + 2 * POS_BANDS
DECAY_TARGET = 1e-2
DECAY_FAST_PCT = 0.3
DECAY_SLOW_PCT = 1.5
D_FF = 2816
CONV_WIDTH = 3
WIN_ROWS = 8
WIN_COLS = 16
ROPE_BASE = 10000.0
RMS_EPS = 1e-6
N_BRANCHES = 2
N_MOD = 6
D_IN = 3 * D_ATTN + (HYENA_ORDER + 1) * D_HYENA + N_BRANCHES * D_MODEL

kernel_name = 'hybrid_na_hyena_convffn_dit_block'

def rmsnorm(x, g):
    xf = x.astype(jnp.float32)
    y = xf * lax.rsqrt(jnp.mean(xf * xf, axis=-1, keepdims=True) + RMS_EPS)
    return (y * g.astype(jnp.float32)).astype(x.dtype)

def adaln(cvec, w, b, n_chunks):
    m = (jax.nn.silu(cvec) @ w + b)[:, None, :]
    return jnp.split(m, n_chunks, axis=-1)

def modulate(x, shift, scale):
    return x * (1 + scale) + shift

def heads(t):
    return t.reshape(t.shape[0], t.shape[1], N_HEADS, HEAD_DIM)

def split_proj(p):
    q = p[..., :D_ATTN]
    k = p[..., D_ATTN:2 * D_ATTN]
    v = p[..., 2 * D_ATTN:3 * D_ATTN]
    hy = p[..., 3 * D_ATTN:3 * D_ATTN + (HYENA_ORDER + 1) * D_HYENA]
    gl = p[..., 3 * D_ATTN + (HYENA_ORDER + 1) * D_HYENA:]
    return q, k, v, hy, gl

def dwconv(u, w, b):
    pad = CONV_WIDTH // 2
    L = u.shape[1]
    up = jnp.pad(u, ((0, 0), (pad, pad), (0, 0)))
    return sum(up[:, j:j + L] * w[j] for j in range(CONV_WIDTH)) + b

def axial_rope(t):
    L, Dh = t.shape[1], t.shape[3]
    pos = jnp.arange(L)
    row = (pos // GRID_W).astype(jnp.float32)
    col = (pos % GRID_W).astype(jnp.float32)
    n_pairs = Dh // 4
    inv_freq = ROPE_BASE ** (-jnp.arange(n_pairs, dtype=jnp.float32) / n_pairs)

    def rot(u, p):
        ang = p[:, None] * inv_freq[None, :]
        cos = jnp.cos(ang)[None, :, None, :].astype(t.dtype)
        sin = jnp.sin(ang)[None, :, None, :].astype(t.dtype)
        u1, u2 = u[..., :n_pairs], u[..., n_pairs:]
        return jnp.concatenate([u1 * cos - u2 * sin, u2 * cos + u1 * sin], axis=-1)

    half = Dh // 2
    return jnp.concatenate([rot(t[..., :half], row), rot(t[..., half:], col)], axis=-1)

def neighbourhood_attention(q_rot, k_rot, v, q_plain, k_ctx, v_ctx, rpb):
    B, S, H, Dh = q_rot.shape
    rows = S // GRID_W
    win_r = min(WIN_ROWS, rows)
    n_nb = win_r * GRID_W
    scale = Dh ** -0.5

    def grid(t):
        return t.reshape(B, rows, GRID_W, H, Dh)

    k_grid, v_grid = grid(k_rot), grid(v)
    q_rows = jnp.moveaxis(grid(q_rot), 1, 0)
    qp_rows = jnp.moveaxis(grid(q_plain), 1, 0)
    qc = jnp.arange(GRID_W)[:, None]
    kc = jnp.arange(GRID_W)[None, :]
    c_start = jnp.clip(qc - WIN_COLS // 2, 0, GRID_W - WIN_COLS)
    col_in = (kc >= c_start) & (kc < c_start + WIN_COLS)
    dc_idx = jnp.clip(kc - qc, 1 - WIN_COLS, WIN_COLS - 1) + (WIN_COLS - 1)
    band_mask = jnp.broadcast_to(col_in[:, None, :], (GRID_W, win_r, GRID_W)).reshape(GRID_W, n_nb)

    def one_row(args):
        r, q_r, qp_r = args
        r_start = jnp.clip(r - win_r // 2, 0, rows - win_r)
        kb = lax.dynamic_slice_in_dim(k_grid, r_start, win_r, axis=1).reshape(B, n_nb, H, Dh)
        vb = lax.dynamic_slice_in_dim(v_grid, r_start, win_r, axis=1).reshape(B, n_nb, H, Dh)
        dr_idx = r_start + jnp.arange(win_r) - r + (WIN_ROWS - 1)
        bias = rpb[:, dr_idx[None, :, None], dc_idx[:, None, :]].reshape(H, GRID_W, n_nb)
        s_nb = jnp.einsum('bqhd,bkhd->bhqk', q_r, kb).astype(jnp.float32) * scale + bias.astype(jnp.float32)
        s_nb = jnp.where(band_mask, s_nb, -jnp.inf)
        s_cx = jnp.einsum('bqhd,bchd->bhqc', qp_r, k_ctx).astype(jnp.float32) * scale
        probs = jax.nn.softmax(jnp.concatenate([s_nb, s_cx], axis=-1), axis=-1).astype(v.dtype)
        return (jnp.einsum('bhqk,bkhd->bqhd', probs[..., :n_nb], vb)
                + jnp.einsum('bhqc,bchd->bqhd', probs[..., n_nb:], v_ctx))

    out = lax.map(one_row, (jnp.arange(rows), q_rows, qp_rows))
    return jnp.moveaxis(out, 0, 1).reshape(B, S, H * Dh)

def context_attention(q, k, v):
    B, C, H, Dh = q.shape
    s = jnp.einsum('bqhd,bkhd->bhqk', q, k).astype(jnp.float32) * (Dh ** -0.5)
    p = jax.nn.softmax(s, axis=-1).astype(v.dtype)
    return jnp.einsum('bhqk,bkhd->bqhd', p, v).reshape(B, C, H * Dh)

def hyena_filter(L, w1, b1, w2, b2, w3, b3, sin_freq, decay):
    pos = jnp.arange(L, dtype=jnp.float32)
    t = pos / max(L - 1, 1)
    bands = jnp.linspace(1e-4, POS_BANDS - 1, POS_BANDS, dtype=jnp.float32)
    ang = (2.0 * math.pi / L) * pos[:, None] * bands[None, :]
    z = jnp.concatenate([t[:, None], jnp.cos(ang), -jnp.sin(ang)], axis=-1)
    h = jnp.sin(sin_freq[0] * (z @ w1 + b1))
    h = jnp.sin(sin_freq[1] * (h @ w2 + b2))
    h = (h @ w3 + b3).reshape(L, 2, D_HYENA)
    h = (h * jnp.exp(-t[:, None, None] * jnp.abs(decay)[None])).astype(jnp.float32)
    k_circ = jnp.concatenate([h[:, 0], jnp.zeros((1, D_HYENA), jnp.float32), h[:0:-1, 1]], axis=0)
    return k_circ / jnp.sum(jnp.abs(k_circ), axis=0, keepdims=True)

def long_conv(u, k_circ, skip):
    L = u.shape[1]
    uf = u.astype(jnp.float32)
    spec = jnp.fft.rfft(uf, n=2 * L, axis=1) * jnp.fft.rfft(k_circ, axis=0)[None]
    y = jnp.fft.irfft(spec, n=2 * L, axis=1)[:, :L]
    return (y + uf * skip.astype(jnp.float32)).astype(u.dtype)

def hyena_branch(hy, conv_w, conv_b, k_circ, skip):
    x0, x1, v = jnp.split(dwconv(hy, conv_w, conv_b), HYENA_ORDER + 1, axis=-1)
    return x0 * long_conv(x1 * v, k_circ, skip)

def merge_branches(y_na, y_hy, gate_logits, w_o_na, w_o_hy, w_out):
    g_na, g_hy = jnp.split(jax.nn.sigmoid(gate_logits), N_BRANCHES, axis=-1)
    return (g_na * (y_na @ w_o_na) + g_hy * (y_hy @ w_o_hy)) @ w_out

def conv_ffn(h, w_up, conv_w, conv_b, w_down):
    u = dwconv(h @ w_up, conv_w, conv_b)
    a, val = jnp.split(u, 2, axis=-1)
    return (jax.nn.gelu(a) * val) @ w_down

def setup_inputs(seed: int = 0) -> dict:
    key = jax.random.key(seed)
    keys = jax.random.split(key, 32)
    counter = [0]

    def nk():
        k = keys[counter[0]]
        counter[0] += 1
        return k

    def nrm(shape, scale):
        return jax.random.normal(nk(), shape, jnp.float32) * scale

    L = DEPTH
    decay_lo = -math.log(DECAY_TARGET) / DECAY_SLOW_PCT
    decay_hi = -math.log(DECAY_TARGET) / DECAY_FAST_PCT
    return {
        'x': nrm((BATCH, SEQ, D_MODEL), 1.0),
        'c': nrm((BATCH, D_MODEL), 1.0),
        'ctx': nrm((BATCH, CTX_LEN, D_MODEL), 1.0),
        'c_ctx': nrm((D_MODEL,), 1.0),
        'w_mod': nrm((L, D_MODEL, N_MOD * D_MODEL), 0.5 * D_MODEL ** -0.5),
        'b_mod': nrm((L, N_MOD * D_MODEL), 0.02),
        'norm_mix_pre': 1.0 + nrm((L, D_MODEL), 0.1),
        'norm_mix_post': 1.0 + nrm((L, D_MODEL), 0.1),
        'norm_ffn_pre': 1.0 + nrm((L, D_MODEL), 0.1),
        'norm_ffn_post': 1.0 + nrm((L, D_MODEL), 0.1),
        'w_in': nrm((L, D_MODEL, D_IN), D_MODEL ** -0.5),
        'b_in': nrm((L, D_IN), 0.02),
        'na_rpb': nrm((L, N_HEADS, 2 * WIN_ROWS - 1, 2 * WIN_COLS - 1), 0.2),
        'hy_conv_w': nrm((L, CONV_WIDTH, (HYENA_ORDER + 1) * D_HYENA), CONV_WIDTH ** -0.5),
        'hy_conv_b': nrm((L, (HYENA_ORDER + 1) * D_HYENA), 0.02),
        'hy_filt_w1': nrm((L, POS_FEATS, FILTER_HIDDEN), POS_FEATS ** -0.5),
        'hy_filt_b1': nrm((L, FILTER_HIDDEN), 0.02),
        'hy_filt_w2': nrm((L, FILTER_HIDDEN, FILTER_HIDDEN), FILTER_HIDDEN ** -0.5),
        'hy_filt_b2': nrm((L, FILTER_HIDDEN), 0.02),
        'hy_filt_w3': nrm((L, FILTER_HIDDEN, 2 * D_HYENA), FILTER_HIDDEN ** -0.5),
        'hy_filt_b3': nrm((L, 2 * D_HYENA), 0.02),
        'hy_sin_freq': 1.0 + nrm((L, 2, FILTER_HIDDEN), 0.1),
        'hy_decay': jax.random.uniform(nk(), (L, 2, D_HYENA), jnp.float32, decay_lo, decay_hi),
        'hy_skip': nrm((L, D_HYENA), 1.0),
        'w_o_na': nrm((L, D_ATTN, D_MODEL), D_ATTN ** -0.5),
        'w_o_hy': nrm((L, D_HYENA, D_MODEL), D_HYENA ** -0.5),
        'w_out': nrm((L, D_MODEL, D_MODEL), D_MODEL ** -0.5),
        'ffn_w_up': nrm((L, D_MODEL, 2 * D_FF), D_MODEL ** -0.5),
        'ffn_conv_w': nrm((L, CONV_WIDTH, 2 * D_FF), CONV_WIDTH ** -0.5),
        'ffn_conv_b': nrm((L, 2 * D_FF), 0.02),
        'ffn_w_down': nrm((L, D_FF, D_MODEL), D_FF ** -0.5),
    }

def reference(x, c, ctx, c_ctx, w_mod, b_mod, norm_mix_pre, norm_mix_post, norm_ffn_pre, norm_ffn_post,
              w_in, b_in, na_rpb, hy_conv_w, hy_conv_b, hy_filt_w1, hy_filt_b1, hy_filt_w2, hy_filt_b2,
              hy_filt_w3, hy_filt_b3, hy_sin_freq, hy_decay, hy_skip, w_o_na, w_o_hy, w_out,
              ffn_w_up, ffn_conv_w, ffn_conv_b, ffn_w_down):
    seq_lat = x.shape[1]
    seq_ctx = ctx.shape[1]
    for layer in range(DEPTH):
        update_ctx = layer + 1 < DEPTH
        w_in_l, b_in_l = w_in[layer], b_in[layer]
        filt_params = (hy_filt_w1[layer], hy_filt_b1[layer], hy_filt_w2[layer], hy_filt_b2[layer],
                       hy_filt_w3[layer], hy_filt_b3[layer], hy_sin_freq[layer], hy_decay[layer])
        out_params = (w_o_na[layer], w_o_hy[layer], w_out[layer])
        ffn_params = (ffn_w_up[layer], ffn_conv_w[layer], ffn_conv_b[layer], ffn_w_down[layer])

        sh_mix, sc_mix, g_mix, sh_ffn, sc_ffn, g_ffn = adaln(c, w_mod[layer], b_mod[layer], N_MOD)
        n_ctx_mod = N_MOD if update_ctx else 2
        ctx_mod = adaln(c_ctx[None, :], w_mod[layer][:, :n_ctx_mod * D_MODEL],
                        b_mod[layer][:n_ctx_mod * D_MODEL], n_ctx_mod)

        hc = modulate(rmsnorm(ctx, norm_mix_pre[layer]), ctx_mod[0], ctx_mod[1])
        if update_ctx:
            q_c, k_c, v_c, hy_c, gl_c = split_proj(hc @ w_in_l + b_in_l)
        else:
            k_c, v_c = jnp.split(hc @ w_in_l[:, D_ATTN:3 * D_ATTN] + b_in_l[D_ATTN:3 * D_ATTN], 2, axis=-1)
        k_c, v_c = heads(k_c), heads(v_c)

        h = modulate(rmsnorm(x, norm_mix_pre[layer]), sh_mix, sc_mix)
        q, k, v, hy, gl = split_proj(h @ w_in_l + b_in_l)
        q, k, v = heads(q), heads(k), heads(v)
        y_na = neighbourhood_attention(axial_rope(q), axial_rope(k), v, q, k_c, v_c, na_rpb[layer])
        y_hy = hyena_branch(hy, hy_conv_w[layer], hy_conv_b[layer], hyena_filter(seq_lat, *filt_params), hy_skip[layer])
        x = x + g_mix * rmsnorm(merge_branches(y_na, y_hy, gl, *out_params), norm_mix_post[layer])

        h = modulate(rmsnorm(x, norm_ffn_pre[layer]), sh_ffn, sc_ffn)
        x = x + g_ffn * rmsnorm(conv_ffn(h, *ffn_params), norm_ffn_post[layer])

        if update_ctx:
            yc_na = context_attention(heads(q_c), k_c, v_c)
            yc_hy = hyena_branch(hy_c, hy_conv_w[layer], hy_conv_b[layer], hyena_filter(seq_ctx, *filt_params), hy_skip[layer])
            ctx = ctx + ctx_mod[2] * rmsnorm(merge_branches(yc_na, yc_hy, gl_c, *out_params), norm_mix_post[layer])
            hc = modulate(rmsnorm(ctx, norm_ffn_pre[layer]), ctx_mod[3], ctx_mod[4])
            ctx = ctx + ctx_mod[5] * rmsnorm(conv_ffn(hc, *ffn_params), norm_ffn_post[layer])
    return x


_drawn_inputs = setup_inputs


def setup_inputs(seed=0):
    import zlib

    import numpy as np

    out = dict(_drawn_inputs(seed))
    spreads = {}
    factors = {'ctx': 13.873,
     'b_in': 5.269,
     'na_rpb': 8.0,
     'hy_conv_b': 5.646,
     'hy_filt_w1': 4.97,
     'hy_filt_b1': 8.0,
     'hy_filt_w2': 4.628,
     'hy_filt_b2': 8.0,
     'hy_filt_w3': 4.31,
     'hy_filt_b3': 64.0,
     'hy_sin_freq': 8.0,
     'hy_decay': 46.223,
     'ffn_conv_b': 7.394}
    for name, (base, spread) in spreads.items():
        noise = np.random.default_rng([zlib.crc32(name.encode()), seed]).standard_normal(out[name].shape)
        drawn = base * np.exp(spread * noise) if base else spread * noise
        out[name] = jnp.asarray(drawn.astype(out[name].dtype))
    for name, factor in factors.items():
        out[name] = (out[name] * factor).astype(out[name].dtype)
    return out
```

```python
from contextlib import ExitStack

import concourse.bass as bass
import numpy as np
from concourse import mybir

F32 = mybir.dt.float32
F32R = mybir.dt.float32r
ALU = mybir.AluOpType
ACT = mybir.ActivationFunctionType
AX = mybir.AxisListType
ds = bass.ds

P = 128
D_MODEL, SEQ, CTX_LEN = 1024, 2048, 256
KD = D_MODEL // P
N_HEADS, HEAD_DIM, GRID_W = 8, 64, 64
ROWS = SEQ // GRID_W
D_ATTN, D_HYENA, D_FF = 512, 512, 2816
WIN_ROWS, WIN_COLS = 8, 16
KH = D_HYENA // P
FF_CHUNKS = D_FF // P
FILTER_HIDDEN, POS_BANDS = 64, 16
RMS_EPS = 1e-6
MASKED = -1e30
BANK = 512

Q0, K0, V0, HY0, GATE0, IN_CHUNKS = 0, 4, 8, 12, 24, 40
MOD_CHUNKS = 48
SH_MIX, SC_MIX, G_MIX, SH_FFN, SC_FFN, G_FFN = (KD * i for i in range(6))

NFFT = 2 * SEQ
R = 64

VEC = {}
_at = 0
for _name, _n in (("b_in", 40), ("b_mod", 48), ("mix_pre", 8), ("mix_post", 8), ("ffn_pre", 8), ("ffn_post", 8),
                  ("hy_w0", 12), ("hy_w1", 12), ("hy_w2", 12), ("hy_b", 12), ("skip", 4),
                  ("ff_w0", 44), ("ff_w1", 44), ("ff_w2", 44), ("ff_b", 44)):
    VEC[_name] = _at
    _at += _n
N_VEC = _at


class Core:

    def __init__(self, nc, dram):
        self.nc, self.d = nc, dram


def scope(nc, ctx, tag):
    sems = []

    def sb(name, shape, dt=F32):
        return ctx.enter_context(nc.sbuf_tensor(f"{tag}_{name}", shape, dt))

    def ps(name, shape):
        return ctx.enter_context(nc.psum_tensor(f"{tag}_{name}", shape, F32))

    def sem(name):
        s = ctx.enter_context(nc.semaphore(f"{tag}_{name}"))
        sems.append(s)
        return s

    return sb, ps, sem, sems


def clear(nc, sems):
    with nc.Block() as block:
        @block.gpsimd
        def _(pool):
            for s in sems:
                pool.sem_clear(s)


def setup_phase(nc, core):
    d = core.d
    with ExitStack() as ctx:
        sb, ps, sem, sems = scope(nc, ctx, "setup")
        const_in = sem("const_in")
        with nc.Block() as block:
            @block.sync
            def _(sp):
                sp.dma_start(core.vec[:, :], d["vec"]).then_inc(const_in, 16)
                sp.dma_start(core.ident[:, :], d["ident"]).then_inc(const_in, 16)
                sp.dma_start(core.mean[:, :], d["mean"]).then_inc(const_in, 16)
                sp.wait_ge(const_in, 48)
        clear(nc, sems)


def filter_phase(nc, core):
    d = core.d
    half = NFFT // 2
    two_pi_1, two_pi_2 = 6.28125, 0.0019350051879882812
    two_pi_3 = float(np.float64(2 * np.pi) - two_pi_1 - two_pi_2)
    magic = float(1.5 * 2 ** 23)
    pi_below = 3.1415925
    with ExitStack() as ctx:
        sb, ps, sem, sems = scope(nc, ctx, "filt")
        z = sb("z", [2 * POS_BANDS + 1, NFFT])
        w1 = sb("w1", [2 * POS_BANDS + 1, FILTER_HIDDEN])
        w2 = sb("w2", [P, FILTER_HIDDEN])
        w3 = sb("w3", [P, 2 * D_HYENA])
        hid = sb("hid", [P, 4])
        b3 = sb("b3", [P, D_HYENA])
        decay = sb("decay", [P, D_HYENA])
        neg_t = sb("neg_t", [P, NFFT // P])
        keep = sb("keep", [P, NFFT // P])
        dft = sb("dft", [P, P])
        ones = sb("ones", [P, 1])
        h1 = sb("h1", [P, half])
        h2 = sb("h2", [P, half])
        turns = sb("turns", [P, half])
        cond = sb("cond", [P, KD, 2])
        cond_s = sb("cond_s", [P, KD, 2])
        wm = sb("wm", [P, 3, KD, P])
        hs = sb("hs", [P, 2, P])
        dec = sb("dec", [P, 2, D_HYENA])
        kc = sb("kc", [P, 2, D_HYENA])
        kabs = sb("kabs", [P, 2, D_HYENA])
        ksum = sb("ksum", [P, D_HYENA])
        spec = sb("spec", [P, 2, D_HYENA])
        ps_h = ps("ps_h", [P, half])
        ps_s = ps("ps_s", [P, 2, BANK])
        ps_m = ps("ps_m", [P, 2])
        mod_sum = [ps_h[:, 2 * BANK:2 * BANK + 2], ps_h[:, 3 * BANK:3 * BANK + 2], ps_m[:, :]]
        ps_n = ps("ps_n", [P, KH])

        const_in, z_ready, mm_layer, layer, wrap = sem("const_in"), sem("z_ready"), sem("mm_layer"), sem("layer"), sem("wrap")
        wm_in = [sem(f"wm_in{m}") for m in range(3)]
        silu, mod_mm, mod_done = sem("silu"), sem("mod_mm"), sem("mod_done")
        hs_ready, tile_mm, dec_ready, kc_step, kc_ready = sem("hs_ready"), sem("tile_mm"), sem("dec_ready"), sem("kc_step"), sem("kc_ready")
        kabs_ready, ksum_done, spec_mm, spec_out = sem("kabs_ready"), sem("ksum_done"), sem("spec_mm"), sem("spec_out")
        stored = [sem(f"stored{s}") for s in range(2)]
        norm_mm, norm_done = sem("norm_mm"), sem("norm_done")
        tiles = NFFT // P // 2
        n_const = 16

        block_ctx = ExitStack()
        block = block_ctx.enter_context(nc.Block())

        @block.sync
        def _(sp):
            for dst, src in ((z, "z"), (w1, "filt_w1")):
                sp.dma_start(dst[:, :], d[src]).then_inc(const_in, 16)
            for h in range(2):
                sp.dma_start(w2[64 * h:64 * h + 64, :], d["filt_w2"]).then_inc(const_in, 16)
                sp.dma_start(w3[64 * h:64 * h + 64, :], d["filt_w3"]).then_inc(const_in, 16)
                sp.dma_start(hid[64 * h:64 * h + 64, :], d["filt_hid"]).then_inc(const_in, 16)
                sp.dma_start(b3[64 * h:64 * h + 64, :], d["filt_b3"][h:h + 1, :].partition_broadcast(64)).then_inc(const_in, 16)
                sp.dma_start(decay[64 * h:64 * h + 64, :], d["decay"][h:h + 1, :].partition_broadcast(64)).then_inc(const_in, 16)
            sp.dma_start(neg_t[:, :], d["neg_t"]).then_inc(const_in, 16)
            sp.dma_start(keep[:, :], d["keep"]).then_inc(const_in, 16)
            sp.dma_start(cond[:, :, :], d["cond"]).then_inc(const_in, 16)
            sp.dma_start(dft[:, :], d["dft_k"]).then_inc(const_in, 16)
            sp.sem_inc(stored[0], 16)
            sp.sem_inc(stored[1], 16)
            for m in range(3):
                sp.dma_start(wm[:, m, :, :], d["w_mod"][m]).then_inc(wm_in[m], 16)
            with sp.Fori(0, tiles) as i:
                for s in range(2):
                    sp.wait_ge(spec_out, 2 * i + s + 3)
                    sp.dma_start(d["spec_k"][ds((2 * i) + 2 * tiles * s, 2)].rearrange("g r c -> (g r) c"),
                                 spec[:, s, :]).then_inc(stored[s], 16)
                for m in range(3):
                    sp.wait_ge(mod_mm, 3 * i + m + 1)
                    sp.dma_start(wm[:, m, :, :], d["w_mod"][ds(3 * i + m + 3, 1)].rearrange("a p k n -> (a p) k n")
                                 ).then_inc(wm_in[m], 16)
            for s in range(2):
                sp.wait_ge(stored[s], 16 * (tiles + 1))
            for m in range(3):
                sp.wait_ge(wm_in[m], 16 * (tiles + 1))

        @block.gpsimd
        def _(pool):
            pool.sem_inc(ksum_done, 2)
            pool.memset(ksum[:, :], 0.0).then_inc(ksum_done, 1)
            pool.memset(ones[:, :], 1.0).then_inc(z_ready, 1)
            with pool.Fori(0, tiles) as i:
                for s in range(2):
                    pool.wait_ge(ksum_done, 2 * i + s + 3)
                    pool.wait_ge(kabs_ready, 2 * i + s + 1)
                    nc.gpsimd.tensor_tensor(ksum[:, :], ksum[:, :], kabs[:, s, :], ALU.add).then_inc(ksum_done, 1)

        @block.tensor
        def _(pe):
            pe.wait_ge(const_in, 16 * n_const)
            for h in range(2):
                for g in range(half // BANK):
                    last = nc.tensor.matmul(ps_h[64 * h:64 * h + 64, ds(BANK * g, BANK)], w1[:, :],
                                            z[:, ds(half * h + BANK * g, BANK)], start=True, stop=True)
            last.then_inc(mm_layer, 1)
            pe.wait_ge(layer, 1)
            for h in range(2):
                for g in range(half // BANK):
                    last = nc.tensor.matmul(ps_h[64 * h:64 * h + 64, ds(BANK * g, BANK)], w2[64 * h:64 * h + 64, :],
                                            h1[64 * h:64 * h + 64, ds(BANK * g, BANK)], start=True, stop=True)
            last.then_inc(mm_layer, 1)
            pe.wait_ge(layer, 2)
            pe.wait_ge(silu, 1)
            pe.wait_ge(z_ready, 2)

            def modulation(i, m):
                pe.wait_ge(wm_in[m], 16 * i + 16)
                pe.wait_ge(mod_done, 3 * i + m + 1)
                for k in range(KD):
                    last = nc.tensor.matmul(mod_sum[m], wm[:, m, k, :], cond_s[:, k, :], start=(k == 0), stop=(k == KD - 1))
                last.then_inc(mod_mm, 1)

            with pe.Fori(0, tiles) as i:
                for s in range(2):
                    pe.wait_ge(hs_ready, 2 * i + s + 1)
                    pe.wait_ge(kc_ready, 2 * i + s + 1)
                    modulation(i, s)
                    for h in range(2):
                        last = nc.tensor.matmul(ps_h[64 * h:64 * h + 64, ds(BANK * s, BANK)],
                                                hs[64 * s:64 * s + 64, s, 64 * h:64 * h + 64],
                                                w3[64 * s:64 * s + 64, ds(D_HYENA * h, D_HYENA)], start=True, stop=True)
                    last.then_inc(tile_mm, 1)
                modulation(i, 2)
                for s in range(2):
                    pe.wait_ge(kc_ready, 2 * i + s + 3)
                    nc.tensor.matmul(ps_s[:, s, :], dft[:, :], kc[:, s, :], start=True, stop=True).then_inc(spec_mm, 1)
            pe.wait_ge(ksum_done, 2 * tiles + 3)
            for q in range(KH):
                last = nc.tensor.matmul(ps_n[:, q:q + 1], ksum[:, ds(P * q, P)], ones[:, :], start=True, stop=True)
            last.then_inc(norm_mm, 1)

        @block.scalar
        def _(act):
            act.sem_inc(spec_out, 2)
            act.wait_ge(const_in, 16 * n_const)
            nc.scalar.activation(cond_s[:, :, :], cond[:, :, :], ACT.Silu).then_inc(silu, 1)
            nc.scalar.activation(decay[:, :], decay[:, :], ACT.Abs).then_inc(z_ready, 1)
            for n in range(2):
                act.wait_ge(wrap, 7 * n + 7)
                nc.scalar.activation((h1, h2)[n][:, :], turns[:, :], ACT.Sin).then_inc(layer, 1)
            act.wait_ge(z_ready, 2)
            with act.Fori(0, tiles) as i:
                for s in range(2):
                    act.wait_ge(kc_ready, 2 * i + s + 1)
                    nc.scalar.activation(dec[:, s, :], decay[:, :], ACT.Exp,
                                         scale=neg_t[:, ds(i + tiles * s, 1)]).then_inc(dec_ready, 1)
                for s in range(2):
                    act.wait_ge(kc_ready, 2 * i + s + 3)
                    act.wait_ge(ksum_done, 2 * i + s + 2)
                    nc.scalar.activation(kabs[:, s, :], kc[:, s, :], ACT.Abs).then_inc(kabs_ready, 1)
                    act.wait_ge(spec_mm, 2 * i + s + 1)
                    act.wait_ge(stored[s], 16 * i + 16)
                    nc.scalar.activation(spec[:, s, :], ps_s[:, s, :], ACT.Copy).then_inc(spec_out, 1)

        @block.vector
        def _(dve):
            done = [0]

            def chain(ins):
                ins.then_inc(wrap, 1)
                done[0] += 1
                dve.wait_ge(wrap, done[0])

            dve.sem_inc(kc_ready, 2)
            dve.sem_inc(mod_done, 3)
            dve.wait_ge(const_in, 16 * n_const)
            for n in range(2):
                dve.wait_ge(mm_layer, n + 1)
                chain(nc.vector.tensor_scalar(h2[:, :], ps_h[:, :], hid[:, 2 * n:2 * n + 1], hid[:, 2 * n + 1:2 * n + 2], ALU.add, ALU.mult))
                chain(nc.vector.tensor_scalar(turns[:, :], h2[:, :], float(1 / (2 * np.pi)), magic, ALU.mult, ALU.add))
                chain(nc.vector.tensor_scalar(turns[:, :], turns[:, :], -magic, None, ALU.add))
                chain(nc.vector.scalar_tensor_tensor(h2[:, :], turns[:, :], -two_pi_1, h2[:, :], ALU.mult, ALU.add))
                chain(nc.vector.scalar_tensor_tensor(h2[:, :], turns[:, :], -two_pi_2, h2[:, :], ALU.mult, ALU.add))
                chain(nc.vector.scalar_tensor_tensor(h2[:, :], turns[:, :], -two_pi_3, h2[:, :], ALU.mult, ALU.add))
                chain(nc.vector.tensor_scalar(turns[:, :], h2[:, :], pi_below, -pi_below, ALU.min, ALU.max))
            dve.wait_ge(layer, 2)

            with dve.Fori(0, tiles) as i:
                for s in range(2):
                    nc.vector.tensor_copy(hs[64 * s:64 * s + 64, s, :], h2[64 * s:64 * s + 64, ds(P * i, P)]).then_inc(hs_ready, 1)
                for s in range(2):
                    dve.wait_ge(tile_mm, 2 * i + s + 1)
                    dve.wait_ge(spec_out, 2 * i + s + 1)
                    nc.vector.tensor_tensor(kc[:, s, :], ps_h[:, ds(BANK * s, BANK)], b3[:, :], ALU.add).then_inc(kc_step, 1)
                    dve.wait_ge(kc_step, 2 * i + s + 1)
                    dve.wait_ge(dec_ready, 2 * i + s + 1)
                    nc.vector.scalar_tensor_tensor(kc[:, s, :], kc[:, s, :], keep[:, ds(i + tiles * s, 1)], dec[:, s, :],
                                                   ALU.mult, ALU.mult).then_inc(kc_ready, 1)
                for m in range(3):
                    dve.wait_ge(mod_mm, 3 * i + m + 1)
                    nc.vector.tensor_scalar(core.mod[:, ds(3 * i + m, 1), :].rearrange("p a c -> p (a c)"), mod_sum[m],
                                            core.vec[:, ds(3 * i + m + VEC["b_mod"], 1)], None, ALU.add).then_inc(mod_done, 1)
            dve.wait_ge(norm_mm, 1)
            nc.vector.reciprocal(core.rnorm[:, :], ps_n[:, :]).then_inc(norm_done, 1)
            dve.wait_ge(norm_done, 1)

        block_ctx.close()
        clear(nc, sems)


def mean_square(pe, core, out, sq):
    nc = core.nc
    for k in range(KD):
        last = nc.tensor.matmul(out, core.mean[:, :], sq[:, k, :], start=(k == 0), stop=(k == KD - 1))
    return last


def norm_phase(nc, core, tag, x_d, tokens, act_hi, act_lo, norm_w, cond_col, shift, scale, add=None):
    W = 256
    groups = tokens // W
    nb = min(2, groups)
    rounds = groups // nb
    with ExitStack() as ctx:
        sb, ps, sem, sems = scope(nc, ctx, tag)
        x = sb("x", [P, nb, KD, W])
        r = sb("r", [P, nb, KD, W]) if add else None
        sq = sb("sq", [P, KD, W])
        t = sb("t", [P, KD, W])
        rs = sb("rs", [P, 2, W])
        col = sb("col", [P, 3, KD])
        ms = ps("ms", [P, 2, BANK])
        x_in = [sem(f"x_in{b}") for b in range(nb)]
        r_in = [sem(f"r_in{b}") for b in range(nb)] if add else None
        stored = [sem(f"stored{b}") for b in range(nb)]
        cols, squared, ms_done, eps_added, rooted, rs_done = (sem(n) for n in ("cols", "squared", "ms_done", "eps_added", "rooted", "rs_done"))
        scaled, x1_step, x1_done, shifted, hi_done, lo_done = (sem(n) for n in ("scaled", "x1_step", "x1_done", "shifted", "hi_done", "lo_done"))
        want = act_hi is not None
        stats = int(want) + int(add is not None)
        freed = lo_done if want else x1_done

        def stat_base(i, b):
            return stats * (nb * i + b)

        block_ctx = ExitStack()
        block = block_ctx.enter_context(nc.Block())

        @block.sync
        def _(sp):
            for b in range(nb):
                sp.sem_inc(stored[b], 16)
            with sp.Fori(0, rounds) as i:
                for b in range(nb):
                    at = ds((nb * i + b) * W, W)
                    sp.wait_ge(freed, nb * i + b + 1)
                    sp.wait_ge(stored[b], 16 * i + 16)
                    sp.dma_start(x[:, b, :, :], x_d[:, :, at].rearrange("k p t -> p k t")).then_inc(x_in[b], 16)
                    if add:
                        sp.dma_start(r[:, b, :, :], add[0][:, :, at].rearrange("k p t -> p k t")).then_inc(r_in[b], 16)
                for b in range(nb):
                    at = ds((nb * i + b) * W, W)
                    if add:
                        sp.wait_ge(x1_done, nb * i + b + 1 + (0 if want else nb))
                        sp.dma_start(add[3][:, :, at].rearrange("k p t -> p k t"), x[:, b, :, :]).then_inc(stored[b], 16)
                    else:
                        sp.sem_inc(stored[b], 16)
            for b in range(nb):
                sp.wait_ge(stored[b], 16 * (rounds + 1))

        @block.gpsimd
        def _(pool):
            pass

        @block.tensor
        def _(pe):
            with pe.Fori(0, rounds) as i:
                for b in range(nb):
                    for n in range(stats):
                        pe.wait_ge(squared, stat_base(i, b) + n + 1)
                        mean_square(pe, core, ms[:, n, 0:W], sq).then_inc(ms_done, 1)

        @block.scalar
        def _(act):
            act.wait_ge(cols, 3 if want or add else 1)
            with act.Fori(0, rounds) as i:
                for b in range(nb):
                    for n in range(stats):
                        src = r if (add and n == 0) else x
                        if src is r:
                            act.wait_ge(r_in[b], 16 * i + 16)
                        elif add:
                            act.wait_ge(x1_done, nb * i + b + 1)
                        else:
                            act.wait_ge(x_in[b], 16 * i + 16)
                        nc.scalar.activation(sq[:, :, :], src[:, b, :, :], ACT.Square).then_inc(squared, 1)
                        act.wait_ge(eps_added, stat_base(i, b) + n + 1)
                        nc.scalar.activation(rs[:, n, :], rs[:, n, :], ACT.Sqrt).then_inc(rooted, 1)
                    if want:
                        act.wait_ge(scaled, nb * i + b + 1)
                        for k in range(KD):
                            last = nc.scalar.activation(t[:, k, :], t[:, k, :], ACT.Identity, bias=col[:, 1, k:k + 1], scale=col[:, 0, k:k + 1])
                        last.then_inc(shifted, 1)
                        act.wait_ge(shifted, nb * i + b + 1)
                        nc.scalar.activation(act_hi[:, :, ds((nb * i + b) * W, W)], t[:, :, :], ACT.Copy).then_inc(hi_done, 1)

        @block.vector
        def _(dve):
            dve.sem_inc(freed, nb)
            vec, mod = core.vec, core.mod
            if want:
                nc.vector.tensor_scalar(col[:, 2, :], mod[:, scale:scale + KD, cond_col], 1.0, None, ALU.add).then_inc(cols, 1)
                dve.wait_ge(cols, 1)
                nc.vector.tensor_tensor(col[:, 0, :], col[:, 2, :], vec[:, norm_w:norm_w + KD], ALU.mult).then_inc(cols, 1)
                nc.vector.tensor_copy(col[:, 1, :], mod[:, shift:shift + KD, cond_col]).then_inc(cols, 1)
                dve.wait_ge(cols, 3)
            else:
                dve.sem_inc(cols, 3)
            if add:
                nc.vector.tensor_tensor(col[:, 2, :], mod[:, add[1]:add[1] + KD, 0], vec[:, add[2]:add[2] + KD], ALU.mult).then_inc(x1_step, 1)
            with dve.Fori(0, rounds) as i:
                for b in range(nb):
                    for n in range(stats):
                        dve.wait_ge(ms_done, stat_base(i, b) + n + 1)
                        nc.vector.tensor_scalar(rs[:, n, :], ms[:, n, 0:W], RMS_EPS, None, ALU.add).then_inc(eps_added, 1)
                        dve.wait_ge(rooted, stat_base(i, b) + n + 1)
                        nc.vector.reciprocal(rs[:, n, :], rs[:, n, :]).then_inc(rs_done, 1)
                        dve.wait_ge(rs_done, stat_base(i, b) + n + 1)
                        rs_all = rs[:, n, :].unsqueeze(1).broadcast_to((P, KD, W))
                        if add and n == 0:
                            dve.wait_ge(x_in[b], 16 * i + 16)
                            nc.vector.tensor_tensor(r[:, b, :, :], r[:, b, :, :], rs_all, ALU.mult).then_inc(x1_step, 1)
                            dve.wait_ge(x1_step, nb * i + b + 2)
                            for k in range(KD):
                                last = nc.vector.scalar_tensor_tensor(x[:, b, k, :], r[:, b, k, :], col[:, 2, k:k + 1], x[:, b, k, :], ALU.mult, ALU.add)
                            last.then_inc(x1_done, 1)
                            if want:
                                dve.wait_ge(x1_done, nb * i + b + 1)
                        else:
                            nc.vector.tensor_tensor(t[:, :, :], x[:, b, :, :], rs_all, ALU.mult).then_inc(scaled, 1)
                    if want:
                        dve.wait_ge(hi_done, nb * i + b + 1)
                        at = ds((nb * i + b) * W, W)
                        nc.vector.tensor_tensor(act_lo[:, :, at], t[:, :, :], act_hi[:, :, at].bitcast(F32), ALU.subtract).then_inc(lo_done, 1)
                        dve.wait_ge(lo_done, nb * i + b + 1 + nb)

        block_ctx.close()
        clear(nc, sems)


def split_phase(nc, core, tag, src, act_hi, act_lo):
    with ExitStack() as ctx:
        sb, ps, sem, sems = scope(nc, ctx, tag)
        raw = sb("raw", [P, 2, SEQ])
        raw_in = [sem(f"raw_in{b}") for b in range(2)]
        hi_done, lo_done = sem("hi_done"), sem("lo_done")
        block_ctx = ExitStack()
        block = block_ctx.enter_context(nc.Block())

        @block.sync
        def _(sp):
            for k in range(KD):
                if k >= 2:
                    sp.wait_ge(lo_done, k - 1)
                sp.dma_start(raw[:, k % 2, :], src[k]).then_inc(raw_in[k % 2], 16)

        @block.scalar
        def _(act):
            for k in range(KD):
                act.wait_ge(raw_in[k % 2], 16 * (k // 2 + 1))
                nc.scalar.activation(act_hi[:, k, :], raw[:, k % 2, :], ACT.Copy).then_inc(hi_done, 1)

        @block.vector
        def _(dve):
            for k in range(KD):
                dve.wait_ge(hi_done, k + 1)
                nc.vector.tensor_tensor(act_lo[:, k, :], raw[:, k % 2, :], act_hi[:, k, :].bitcast(F32), ALU.subtract).then_inc(lo_done, 1)

        block_ctx.close()
        clear(nc, sems)


def product(nc, out, w_hi, w_lo, x_hi, x_lo, first, last):
    nc.tensor.matmul(out, w_hi, x_hi, start=first, stop=False)
    nc.tensor.matmul(out, w_hi, x_lo, start=False, stop=False)
    return nc.tensor.matmul(out, w_lo, x_hi, start=False, stop=last)


def weight_splitter(nc, pool, i, b, count0, zero, w_in, w_raw, w_hi, w_lo, hi_done, w_ready, mm_done):
    pool.wait_ge(w_in[b], 16 * i + 16)
    pool.wait_ge(mm_done, 2 * i + b + 1 + count0)
    nc.gpsimd.tensor_tensor(w_hi[:, b, :, :], w_raw[:, b, :, :], zero, ALU.add).then_inc(hi_done, 1)
    pool.wait_ge(hi_done, 2 * i + b + 1)
    nc.gpsimd.tensor_tensor(w_lo[:, b, :, :], w_raw[:, b, :, :], w_hi[:, b, :, :].bitcast(F32), ALU.subtract).then_inc(w_ready, 1)


def projection_phase(nc, core, tag, kind, w_d, first, count, act_hi, act_lo, tokens, out_d, bias=0):
    vec = core.vec
    rounds = count // 2
    bank = min(BANK, tokens)
    per_pair = kind == "ffn"
    with ExitStack() as ctx:
        sb, ps, sem, sems = scope(nc, ctx, tag)
        w_raw = sb("w_raw", [P, 2, KD, P])
        w_hi = sb("w_hi", [P, 2, KD, P], F32R)
        w_lo = sb("w_lo", [P, 2, KD, P], F32R)
        zero = sb("zero", [P, 1])
        zeros = zero[:, :].unsqueeze(1).broadcast_to((P, KD, P))
        n_out = 1 if per_pair else 2
        out = sb("out", [P, n_out, tokens])
        work = sb("work", [P, 2 if per_pair else 1, tokens]) if kind in ("conv", "ffn") else None
        acc = ps("acc", [P, 2, max(tokens, BANK)])
        w_in = [sem(f"w_in{b}") for b in range(2)]
        stored = [sem(f"stored{b}") for b in range(n_out)]
        zeroed, hi_done, w_ready, mm_done, evac = (sem(n) for n in ("zeroed", "hi_done", "w_ready", "mm_done", "evac"))
        act_out, conv_step, conv_done, gelu_done = (sem(n) for n in ("act_out", "conv_step", "conv_done", "gelu_done"))
        result = {"bias": evac, "sigmoid": evac, "plain": evac, "conv": conv_done, "ffn": conv_done}[kind]
        block_ctx = ExitStack()
        block = block_ctx.enter_context(nc.Block())

        def store(sp, i, b):
            if per_pair and b == 0:
                return
            if per_pair:
                sp.wait_ge(result, i + 2)
                sp.dma_start(out_d[ds(i, 1)].rearrange("a p t -> (a p) t"), out[:, 0, :]).then_inc(stored[0], 16)
            else:
                sp.wait_ge(result, 2 * i + b + (2 if kind == "conv" else 3))
                sp.dma_start(out_d[ds(2 * i + b, 1)].rearrange("a p t -> (a p) t"), out[:, b, :]).then_inc(stored[b], 16)

        @block.sync
        def _(sp):
            for s in stored:
                sp.sem_inc(s, 16)
            for b in range(2):
                sp.dma_start(w_raw[:, b, :, :], w_d[first + b]).then_inc(w_in[b], 16)
            if rounds > 1:
                with sp.Fori(0, rounds - 1) as i:
                    for b in range(2):
                        sp.wait_ge(w_ready, 2 * i + b + 1)
                        sp.dma_start(w_raw[:, b, :, :], w_d[ds(first + 2 * i + b + 2, 1)].rearrange("a p k n -> (a p) k n")
                                     ).then_inc(w_in[b], 16)
                        store(sp, i, b)
            for b in range(2):
                store(sp, rounds - 1, b)
            for s in stored:
                sp.wait_ge(s, 16 * (rounds + 1))

        @block.gpsimd
        def _(pool):
            pool.memset(zero[:, :], 0.0).then_inc(zeroed, 1)
            pool.wait_ge(zeroed, 1)
            with pool.Fori(0, rounds) as i:
                for b in range(2):
                    weight_splitter(nc, pool, i, b, 0, zeros, w_in, w_raw, w_hi, w_lo, hi_done, w_ready, mm_done)

        @block.tensor
        def _(pe):
            pe.sem_inc(mm_done, 2)
            with pe.Fori(0, rounds) as i:
                for b in range(2):
                    pe.wait_ge(w_ready, 2 * i + b + 1)
                    pe.wait_ge(evac, 2 * i + b + 1)
                    for g in range(tokens // bank):
                        at = slice(bank * g, bank * (g + 1))
                        for k in range(KD):
                            last = product(nc, acc[:, b, at], w_hi[:, b, k, :], w_lo[:, b, k, :],
                                           act_hi[:, k, at], act_lo[:, k, at], k == 0, k == KD - 1)
                    last.then_inc(mm_done, 1)

        @block.scalar
        def _(act):
            if kind in ("bias", "sigmoid", "plain"):
                act.sem_inc(evac, 2)
            with act.Fori(0, rounds) as i:
                for b in range(2):
                    c = 2 * i + b
                    act.wait_ge(mm_done, c + 3)
                    if kind in ("bias", "sigmoid"):
                        act.wait_ge(stored[b], 16 * i + 16)
                        nc.scalar.activation(out[:, b, :], acc[:, b, 0:tokens], ACT.Sigmoid if kind == "sigmoid" else ACT.Identity,
                                             bias=vec[:, ds(c + bias, 1)]).then_inc(evac, 1)
                    elif kind == "plain":
                        act.wait_ge(stored[b], 16 * i + 16)
                        nc.scalar.activation(out[:, b, :], acc[:, b, 0:tokens], ACT.Copy).then_inc(evac, 1)
                    elif kind == "conv":
                        act.wait_ge(conv_done, c + 1)
                        nc.scalar.activation(work[:, 0, :], acc[:, b, :], ACT.Identity, bias=vec[:, ds(c + bias, 1)]).then_inc(evac, 1)
                    else:
                        act.wait_ge(conv_done, i + 1)
                        nc.scalar.activation(work[:, b, :], acc[:, b, :], ACT.Identity, bias=vec[:, ds(c + VEC["ff_b"], 1)],
                                             scale=vec[:, ds(c + VEC["ff_w1"], 1)]).then_inc(act_out, 1)
                        if b == 0:
                            act.wait_ge(evac, c + 3)
                            nc.scalar.activation(work[:, 0, :], work[:, 0, :], ACT.Gelu_apprx_tanh).then_inc(gelu_done, 1)

        @block.vector
        def _(dve):
            if kind == "conv":
                dve.sem_inc(evac, 2)
                dve.sem_inc(conv_done, 1)
                with dve.Fori(0, rounds) as i:
                    for b in range(2):
                        c = 2 * i + b
                        o, u = out[:, b, :], work[:, 0, :]
                        dve.wait_ge(evac, c + 3)
                        dve.wait_ge(stored[b], 16 * i + 16)
                        nc.vector.tensor_scalar(o, u, vec[:, ds(c + VEC["hy_w1"], 1)], vec[:, ds(c + VEC["hy_b"], 1)], ALU.mult, ALU.add
                                                ).then_inc(conv_step, 1)
                        dve.wait_ge(conv_step, 2 * c + 1)
                        nc.vector.scalar_tensor_tensor(o[:, 1:], u[:, :-1], vec[:, ds(c + VEC["hy_w0"], 1)], o[:, 1:], ALU.mult, ALU.add
                                                       ).then_inc(conv_step, 1)
                        dve.wait_ge(conv_step, 2 * c + 2)
                        nc.vector.scalar_tensor_tensor(o[:, :-1], u[:, 1:], vec[:, ds(c + VEC["hy_w2"], 1)], o[:, :-1], ALU.mult, ALU.add
                                                       ).then_inc(conv_done, 1)
            elif kind == "ffn":
                dve.sem_inc(evac, 2)
                dve.sem_inc(conv_done, 1)
                with dve.Fori(0, rounds) as i:
                    for b in range(2):
                        c = 2 * i + b
                        o, u = work[:, b, :], acc[:, b, :]
                        dve.wait_ge(act_out, c + 1)
                        nc.vector.scalar_tensor_tensor(o[:, 1:], u[:, :-1], vec[:, ds(c + VEC["ff_w0"], 1)], o[:, 1:], ALU.mult, ALU.add
                                                       ).then_inc(conv_step, 1)
                        dve.wait_ge(conv_step, c + 1)
                        nc.vector.scalar_tensor_tensor(o[:, :-1], u[:, 1:], vec[:, ds(c + VEC["ff_w2"], 1)], o[:, :-1], ALU.mult, ALU.add
                                                       ).then_inc(evac, 1)
                    dve.wait_ge(gelu_done, i + 1)
                    dve.wait_ge(evac, 2 * i + 4)
                    dve.wait_ge(stored[0], 16 * i + 16)
                    nc.vector.tensor_tensor(out[:, 0, :], work[:, 0, :], work[:, 1, :], ALU.mult).then_inc(conv_done, 1)

        block_ctx.close()
        clear(nc, sems)


def attention_phase(nc, core):
    d = core.d
    PAIRS = ROWS // 2
    UNITS = 2 * PAIRS
    HALO = WIN_ROWS // 2
    NB = (WIN_ROWS + 1) * GRID_W
    CX = NB
    TAB = 14 * GRID_W

    def window(p):
        if p == 0 or p == 1:
            return WIN_ROWS * GRID_W, 0, (6 - 2 * p) * GRID_W
        if p >= PAIRS - 2:
            return WIN_ROWS * GRID_W, ROWS - WIN_ROWS, (2 - 2 * (p - PAIRS + 2)) * GRID_W
        return NB, 2 * p - HALO, None

    with ExitStack() as ctx:
        sb, ps, sem, sems = scope(nc, ctx, "att")
        cos, sin = sb("cos", [P, SEQ]), sb("sin", [P, SEQ])
        colmask = sb("colmask", [P, GRID_W])
        q, k, v = sb("q", [P, SEQ]), sb("k", [P, SEQ]), sb("v", [P, SEQ])
        qp, kp = sb("qp", [P, SEQ]), sb("kp", [P, SEQ])
        qr, kr = sb("qr", [P, SEQ]), sb("kr", [P, SEQ])
        kx, vx = sb("kx", [P, CTX_LEN]), sb("vx", [P, CTX_LEN])
        table = sb("table", [P, 2, TAB])
        inner = sb("inner", [P, 2, NB])
        VT = SEQ // P + CTX_LEN // P
        vt = sb("vt", [P, VT, P])
        e = sb("e", [P, 2, NB + CTX_LEN])
        pt = sb("pt", [P, 2, 7, P])
        stat = sb("stat", [P, 2, 8])
        o_sb = sb("o_sb", [P, 2, P])
        y = sb("y", [P, SEQ])
        s_ps = ps("s_ps", [P, 2, 2 * BANK])
        t_ps = ps("t_ps", [P, 2, BANK])
        o_ps = ps("o_ps", [P, BANK])[:, 0:P]
        ot_ps = ps("ot_ps", [P, BANK])[:, 0:P]

        const_in, loaded, stored = sem("const_in"), sem("loaded"), sem("stored")
        q_step, k_step, prepared, k_ready, tab_step, tab_ready = (sem(n) for n in ("q_step", "k_step", "prepared", "k_ready", "tab_step", "tab_ready"))
        v_mm, v_out = sem("v_mm"), sem("v_out")
        scores, row_max, logits, neg_max, exp_done, inverse = (sem(n) for n in ("scores", "row_max", "logits", "neg_max", "exp_done", "inverse"))
        flipped, pt_a, pt_b, pv, o_norm, o_flip, y_out, idle = (sem(n) for n in ("flipped", "pt_a", "pt_b", "pv", "o_norm", "o_flip", "y_out", "idle"))
        sums = sem("sums")
        LOADS = 3 + 16 + 2 + 1
        V_GROUPS = (VT + 3) // 4
        block_ctx = ExitStack()
        block = block_ctx.enter_context(nc.Block())

        def rows_of(dram, c):
            return dram[ds(c, 1)].rearrange("a p t -> (a p) t")

        @block.sync
        def _(sp):
            sp.dma_start(cos[:, :], d["cos"]).then_inc(const_in, 16)
            sp.dma_start(sin[:, :], d["sin"]).then_inc(const_in, 16)
            sp.dma_start(colmask[:, :], d["colmask"]).then_inc(const_in, 16)
            with sp.Fori(0, N_HEADS // 2) as j:
                sp.wait_ge(idle, j + 1)
                for dst, dram, c in ((q, d["proj"], Q0), (k, d["proj"], K0), (v, d["proj"], V0)):
                    sp.dma_start(dst[:, :], rows_of(dram, j + c)).then_inc(loaded, 16)
                for dst, c in ((qp, Q0), (kp, K0)):
                    for blk in range(8):
                        sp.dma_start(dst[16 * blk:16 * blk + 16, :],
                                     d["proj"][ds(j + c, 1), 16 * (blk ^ 1):16 * (blk ^ 1) + 16, :].rearrange("a p t -> (a p) t")
                                     ).then_inc(loaded, 16)
                sp.dma_start(kx[:, :], rows_of(d["ctx_kv"], j)).then_inc(loaded, 16)
                sp.dma_start(vx[:, :], rows_of(d["ctx_kv"], j + KH)).then_inc(loaded, 16)
                sp.dma_start(table[:, :, :], d["rpb"][ds(2 * j, 2)].rearrange("h p t -> p h t")).then_inc(loaded, 16)
                sp.wait_ge(y_out, PAIRS * j + PAIRS)
                sp.dma_start(rows_of(d["branches"], j), y[:, :]).then_inc(stored, 16)
                sp.wait_ge(stored, 16 * j + 16)
                sp.sem_inc(idle, 1)
            sp.wait_ge(stored, 16 * (N_HEADS // 2))

        @block.gpsimd
        def _(pool):
            pool.sem_inc(idle, 1)
            pool.wait_ge(const_in, 48)
            mask = colmask[:, :].unsqueeze(1).broadcast_to((P, TAB // GRID_W, GRID_W))
            with pool.Fori(0, N_HEADS // 2) as j:
                pool.wait_ge(loaded, (16 * LOADS) * j + 16 * LOADS)
                nc.gpsimd.tensor_tensor(kr[:, :], k[:, :], cos[:, :], ALU.mult).then_inc(k_step, 1)
                nc.gpsimd.tensor_tensor(kp[:, :], kp[:, :], sin[:, :], ALU.mult).then_inc(k_step, 1)
                pool.wait_ge(k_step, 2 * j + 2)
                nc.gpsimd.tensor_tensor(kr[:, :], kr[:, :], kp[:, :], ALU.add).then_inc(k_ready, 1)
                for h in range(2):
                    tab = table[:, h, :].rearrange("p (r c) -> p r c", c=GRID_W)
                    nc.gpsimd.tensor_tensor(tab, tab, mask, ALU.add).then_inc(tab_step, 1)

        @block.tensor
        def _(pe):
            def flip_values(j):
                pe.wait_ge(loaded, (16 * LOADS) * j + 16 * LOADS)
                for g in range(V_GROUPS):
                    if g >= 4:
                        pe.wait_ge(v_out, V_GROUPS * j + g - 3)
                    for t in range(4 * g, min(4 * g + 4, VT)):
                        src = v[:, ds(P * t, P)] if t < SEQ // P else vx[:, ds(P * (t - SEQ // P), P)]
                        last = nc.tensor.transpose(s_ps[:, g % 4 // 2, ds(BANK * (g % 2) + P * (t % 4), P)], src, core.ident[:, :])
                    last.then_inc(v_mm, 1)

            def score(j, s):
                p, h = divmod(s, 2)
                nk, row, _ = window(p)
                lo, hi = 64 * h, 64 * h + 64
                if s >= 2:
                    pe.wait_ge(exp_done, UNITS * j + s - 1)
                qs = qr[lo:hi, ds(P * p, P)]
                out = s_ps[:, s % 2, :]
                nc.tensor.matmul(out[:, 0:BANK], qs, kr[lo:hi, ds(GRID_W * row, BANK)], start=True, stop=True)
                if nk > BANK:
                    nc.tensor.matmul(out[:, BANK:nk], qs, kr[lo:hi, ds(GRID_W * row + BANK, nk - BANK)], start=True, stop=True)
                nc.tensor.matmul(out[:, CX:CX + CTX_LEN], q[lo:hi, ds(P * p, P)], kx[lo:hi, :], start=True, stop=True).then_inc(scores, 1)

            def flip_probs(j, s):
                nk = window(s // 2)[0]
                pe.wait_ge(exp_done, UNITS * j + s + 1)
                if s >= 1:
                    pe.wait_ge(pt_a, UNITS * j + s)
                    pe.wait_ge(pt_b, UNITS * j + s)
                for t in (0, 1, 2, 3, 4, 5, 6):
                    if t == 4 and nk == BANK:
                        continue
                    at = P * t if t < 5 else CX + P * (t - 5)
                    last = nc.tensor.transpose(t_ps[:, t // 4, ds(P * (t % 4), P)], e[:, s % 2, ds(at, P)], core.ident[:, :])
                last.then_inc(flipped, 1)

            def values(j, s):
                p, h = divmod(s, 2)
                nk, row, _ = window(p)
                pe.wait_ge(pt_a, UNITS * j + s + 1)
                pe.wait_ge(pt_b, UNITS * j + s + 1)
                if s >= 1:
                    pe.wait_ge(o_norm, UNITS * j + s)
                out = o_ps[:, ds(64 * h, 64)]
                for t in (0, 1, 2, 3, 4, 5, 6):
                    if t == 4 and nk == BANK:
                        continue
                    keys = 64 if t == 4 else P
                    tile = row // 2 + t if t < 5 else SEQ // P + t - 5
                    last = nc.tensor.matmul(out, pt[0:keys, s % 2, t, :], vt[0:keys, tile, ds(64 * h, 64)], start=(t == 0), stop=(t == 6))
                last.then_inc(pv, 1)

            def flip_out(j, p):
                pe.wait_ge(o_norm, UNITS * j + 2 * p + 2)
                if p >= 1:
                    pe.wait_ge(y_out, PAIRS * j + p)
                nc.tensor.transpose(ot_ps, o_sb[:, p % 2, :], core.ident[:, :]).then_inc(o_flip, 1)

            with pe.Fori(0, N_HEADS // 2) as j:
                flip_values(j)
                pe.wait_ge(v_out, V_GROUPS * j + V_GROUPS)
                pe.wait_ge(prepared, j + 1)
                pe.wait_ge(k_ready, j + 1)
                for s in range(UNITS + 4):
                    if s < UNITS:
                        score(j, s)
                    if 1 <= s <= UNITS:
                        flip_probs(j, s - 1)
                    if 2 <= s <= UNITS + 1:
                        values(j, s - 2)
                    if s >= 4 and s % 2 == 0:
                        flip_out(j, (s - 4) // 2)

        @block.scalar
        def _(act):
            def exps(j, s):
                nk = window(s // 2)[0]
                b = s % 2
                st = stat[:, b, :]
                act.wait_ge(neg_max, UNITS * j + s + 1)
                nc.scalar.activation(e[:, b, 0:nk], e[:, b, 0:nk], ACT.Exp, bias=st[:, 2:3], accum_out=st[:, 3:4])
                nc.scalar.activation(e[:, b, CX:CX + CTX_LEN], s_ps[:, b, CX:CX + CTX_LEN], ACT.Exp, bias=st[:, 2:3],
                                     accum_out=st[:, 4:5]).then_inc(exp_done, 1)

            def out_a(j, s):
                act.wait_ge(flipped, UNITS * j + s + 1)
                if s >= 2:
                    act.wait_ge(pv, UNITS * j + s - 1)
                nc.scalar.activation(pt[:, s % 2, 0:4, :], t_ps[:, 0, :].rearrange("p (t n) -> p t n", n=P), ACT.Copy).then_inc(pt_a, 1)

            def out_y(j, p):
                act.wait_ge(o_flip, PAIRS * j + p + 1)
                nc.scalar.activation(y[:, ds(P * p, P)], ot_ps, ACT.Copy).then_inc(y_out, 1)

            with act.Fori(0, N_HEADS // 2) as j:
                for g in range(V_GROUPS):
                    act.wait_ge(v_mm, V_GROUPS * j + g + 1)
                    n = min(4, VT - 4 * g)
                    nc.scalar.activation(vt[:, 4 * g:4 * g + n, :],
                                         s_ps[:, g % 4 // 2, ds(BANK * (g % 2), P * n)].rearrange("p (t n) -> p t n", n=P), ACT.Copy).then_inc(v_out, 1)
                for s in range(UNITS + 4):
                    if s < UNITS:
                        exps(j, s)
                    if 1 <= s <= UNITS:
                        out_a(j, s - 1)
                    if s >= 4 and s % 2 == 0:
                        out_y(j, (s - 4) // 2)

        @block.vector
        def _(dve):
            scale = HEAD_DIM ** -0.5

            def logit(j, s):
                p, h = divmod(s, 2)
                nk, _, col = window(p)
                b = s % 2
                st = stat[:, b, :]
                bias = inner[:, h, :] if col is None else table[:, h, ds(col, nk)]
                dve.wait_ge(scores, UNITS * j + s + 1)
                if s >= 2:
                    dve.wait_ge(flipped, UNITS * j + s - 1)
                nc.vector.reduce_max(st[:, 0:1], s_ps[:, b, CX:CX + CTX_LEN], AX.X).then_inc(row_max, 1)
                nc.vector.tensor_tensor_reduce(out=e[:, b, 0:nk], in0=s_ps[:, b, 0:nk], in1=bias, scale=1.0, scalar=MASKED,
                                               op0=ALU.add, op1=ALU.max, accum_out=st[:, 1:2]).then_inc(logits, 1)
                dve.wait_ge(row_max, UNITS * j + s + 1)
                dve.wait_ge(logits, UNITS * j + s + 1)
                nc.vector.tensor_scalar(st[:, 2:3], st[:, 1:2], st[:, 0:1], -1.0, ALU.max, ALU.mult).then_inc(neg_max, 1)

            def out_b(j, s):
                nk = window(s // 2)[0]
                first = 0 if nk > BANK else 1
                dve.wait_ge(flipped, UNITS * j + s + 1)
                if s >= 2:
                    dve.wait_ge(pv, UNITS * j + s - 1)
                nc.vector.tensor_copy(pt[:, s % 2, 4 + first:7, :],
                                      t_ps[:, 1, P * first:3 * P].rearrange("p (t n) -> p t n", n=P)).then_inc(pt_b, 1)

            def invert(j, s):
                st = stat[:, s % 2, :]
                dve.wait_ge(exp_done, UNITS * j + s + 1)
                nc.vector.tensor_tensor(st[:, 5:6], st[:, 3:4], st[:, 4:5], ALU.add).then_inc(sums, 1)
                dve.wait_ge(sums, UNITS * j + s + 1)
                nc.vector.reciprocal(st[:, 6:7], st[:, 5:6]).then_inc(inverse, 1)

            def normalise(j, s):
                p, h = divmod(s, 2)
                dve.wait_ge(pv, UNITS * j + s + 1)
                dve.wait_ge(inverse, UNITS * j + s + 1)
                if p >= 2:
                    dve.wait_ge(o_flip, PAIRS * j + p - 1)
                nc.vector.tensor_scalar(o_sb[:, p % 2, ds(64 * h, 64)], o_ps[:, ds(64 * h, 64)], stat[:, s % 2, 6:7], None,
                                        ALU.mult).then_inc(o_norm, 1)

            with dve.Fori(0, N_HEADS // 2) as j:
                dve.wait_ge(const_in, 48)
                dve.wait_ge(loaded, (16 * LOADS) * j + 16 * LOADS)
                nc.vector.tensor_scalar(q[:, :], q[:, :], scale, None, ALU.mult).then_inc(q_step, 1)
                nc.vector.scalar_tensor_tensor(qp[:, :], qp[:, :], scale, sin[:, :], ALU.mult, ALU.mult).then_inc(q_step, 1)
                dve.wait_ge(q_step, 3 * j + 1)
                nc.vector.tensor_tensor(qr[:, :], q[:, :], cos[:, :], ALU.mult).then_inc(q_step, 1)
                dve.wait_ge(q_step, 3 * j + 3)
                nc.vector.tensor_tensor(qr[:, :], qr[:, :], qp[:, :], ALU.add).then_inc(prepared, 1)
                dve.wait_ge(tab_step, 2 * j + 2)
                nc.vector.tensor_copy(inner[:, :, :], table[:, :, 2 * GRID_W:2 * GRID_W + NB]).then_inc(tab_ready, 1)
                dve.wait_ge(tab_ready, 3 * j + 1)
                nc.vector.memset(inner[0:64, :, NB - GRID_W:NB], MASKED).then_inc(tab_ready, 1)
                nc.vector.memset(inner[64:128, :, 0:GRID_W], MASKED).then_inc(tab_ready, 1)
                dve.wait_ge(tab_ready, 3 * j + 3)
                for s in range(UNITS + 3):
                    if 2 <= s <= UNITS + 1:
                        normalise(j, s - 2)
                    if s < UNITS:
                        logit(j, s)
                    if 1 <= s <= UNITS:
                        invert(j, s - 1)
                        out_b(j, s - 1)

        block_ctx.close()
        clear(nc, sems)


def hyena_phase(nc, core):
    d = core.d
    with ExitStack() as ctx:
        sb, ps, sem, sems = scope(nc, ctx, "hy")
        x1 = sb("x1", [P, KH, SEQ])
        vv = sb("vv", [P, KH, SEQ])
        dft = sb("dft", [P, 2, P])
        idft = sb("idft", [P, R])
        ua = sb("ua", [P, 2, KH, P])
        ut = sb("ut", [P, 2, D_HYENA])
        spec = sb("spec", [P, 2, 2, D_HYENA])
        const_in, u_in, u_ready, skip_done = sem("const_in"), sem("u_in"), sem("u_ready"), sem("skip_done")
        ua_ready, flip, ut_ready, s1_mm, s1_out = (sem(n) for n in ("ua_ready", "flip", "ut_ready", "s1_mm", "s1_out"))
        s1_stored = [sem(f"s1_stored{b}") for b in range(2)]
        with ExitStack() as inner_ctx:
            ps1 = inner_ctx.enter_context(nc.psum_tensor("hy_flip_ps", [P, 2, BANK], F32))
            ps2 = inner_ctx.enter_context(nc.psum_tensor("hy_s1_ps", [P, 2, 2, BANK], F32))
            block_ctx = ExitStack()
            block = block_ctx.enter_context(nc.Block())
            TILES = R // 4

            @block.sync
            def _(sp):
                sp.dma_start(dft[:, :, :], d["dft_u"]).then_inc(const_in, 16)
                sp.dma_start(idft[:, :], d["idft"]).then_inc(const_in, 16)
                for q in range(KH):
                    sp.dma_start(x1[:, q, :], d["proj"][HY0 + KH + q]).then_inc(u_in, 16)
                    sp.dma_start(vv[:, q, :], d["proj"][HY0 + 2 * KH + q]).then_inc(u_in, 16)
                for b in range(2):
                    sp.sem_inc(s1_stored[b], 16)
                with sp.Fori(0, TILES // 2) as i:
                    for b in range(2):
                        sp.wait_ge(s1_out, 2 * i + b + 1)
                        for h in range(2):
                            sp.dma_start(d["spec_u"][ds(8 * i + 4 * b + 2 * h, 2)].rearrange("g r c -> (g r) c"),
                                         spec[:, b, h, :]).then_inc(s1_stored[b], 16)
                for b in range(2):
                    sp.wait_ge(s1_stored[b], 16 + 32 * (TILES // 2))

            @block.vector
            def _(dve):
                dve.wait_ge(u_in, 32 * KH)
                nc.vector.tensor_tensor(vv[:, :, :], x1[:, :, :], vv[:, :, :], ALU.mult).then_inc(u_ready, 1)
                dve.wait_ge(u_ready, 1)
                tokens = vv[:, :, :].rearrange("p q (a b) -> p q b a", b=R)
                dve.sem_inc(flip, 2)
                with dve.Fori(0, TILES // 2) as i:
                    for b in range(2):
                        dve.wait_ge(flip, 2 * i + b + 1)
                        for q in range(KH):
                            last = nc.vector.tensor_copy(ua[:, b, q, :].rearrange("p (g a) -> p g a", g=4),
                                                         tokens[:, q, ds(8 * i + 4 * b, 4), :])
                        last.then_inc(ua_ready, 1)
                for q in range(KH):
                    last = nc.vector.tensor_scalar(x1[:, q, :], vv[:, q, :], core.vec[:, VEC["skip"] + q:VEC["skip"] + q + 1], None, ALU.mult)
                last.then_inc(skip_done, 1)
                dve.wait_ge(skip_done, 1)

            @block.tensor
            def _(pe):
                pe.wait_ge(const_in, 32)
                with pe.Fori(0, TILES // 2) as i:
                    for b in range(2):
                        pe.wait_ge(ua_ready, 2 * i + b + 1)
                        for q in range(KH):
                            last = nc.tensor.transpose(ps1[:, b, ds(P * q, P)], ua[:, b, q, :], core.ident[:, :])
                        last.then_inc(flip, 1)
                    for b in range(2):
                        pe.wait_ge(ut_ready, 2 * i + b + 1)
                        for h in range(2):
                            last = nc.tensor.matmul(ps2[:, b, h, :], dft[:, h, :], ut[:, b, :], start=True, stop=True)
                        last.then_inc(s1_mm, 1)

            @block.scalar
            def _(act):
                with act.Fori(0, TILES // 2) as i:
                    for b in range(2):
                        act.wait_ge(flip, 2 * i + b + 3)
                        nc.scalar.activation(ut[:, b, :], ps1[:, b, :], ACT.Copy).then_inc(ut_ready, 1)
                    for b in range(2):
                        act.wait_ge(s1_mm, 2 * i + b + 1)
                        act.wait_ge(s1_stored[b], 32 * i + 16)
                        nc.scalar.activation(spec[:, b, :, :], ps2[:, b, :, :], ACT.Copy).then_inc(s1_out, 1)

            block_ctx.close()

        G = R // 2
        with ExitStack() as inner_ctx:
            isb = lambda n, s: inner_ctx.enter_context(nc.sbuf_tensor(f"hy_{n}", s, F32))
            tw = isb("tw", [P, 2, 5, P])
            au, ak = isb("au", [P, 2, D_HYENA]), isb("ak", [P, 2, D_HYENA])
            ka, kb = isb("ka", [P, 2, D_HYENA]), isb("kb", [P, 2, D_HYENA])
            prod = isb("prod", [P, 2, 2, D_HYENA])
            yy = isb("yy", [P, 2, D_HYENA])
            bo = isb("bo", [P, 2, D_HYENA])
            psg = inner_ctx.enter_context(nc.psum_tensor("hy_g_ps", [P, 2, 4, BANK], F32))
            g_in = [sem(f"g_in{b}") for b in range(2)]
            b_stored = [sem(f"b_stored{b}") for b in range(2)]
            fwd, k_out, prods, y_ready, inv, b_out = (sem(n) for n in ("fwd", "k_out", "prods", "y_ready", "inv", "b_out"))
            block_ctx = ExitStack()
            block = block_ctx.enter_context(nc.Block())
            FWD_LOADS = 5

            @block.sync
            def _(sp):
                for b in range(2):
                    sp.sem_inc(b_stored[b], 16)

                def load(g, b):
                    sp.dma_start(tw[:, b, :, :], d["twiddle"][ds(g, 1)].rearrange("a p m n -> (a p) m n")).then_inc(g_in[b], 16)
                    for c in range(2):
                        for dst, src in ((au, "spec_u"), (ak, "spec_k")):
                            sp.dma_start(dst[64 * c:64 * c + 64, b, :], d[src][:, ds(2 * g + c, 1), :].rearrange("n a c -> n (a c)")
                                         ).then_inc(g_in[b], 16)

                with sp.Fori(0, G // 2) as i:
                    for b in range(2):
                        sp.wait_ge(inv, 2 * i + b + 1)
                        load(2 * i + b, b)
                    for b in range(2):
                        sp.wait_ge(b_out, 2 * i + b + 1)
                        for c in range(2):
                            sp.dma_start(d["spec_y"][:, ds(4 * i + 2 * b + c, 1), :].rearrange("n a c -> n (a c)"),
                                         bo[64 * c:64 * c + 64, b, :]).then_inc(b_stored[b], 16)
                for b in range(2):
                    sp.wait_ge(b_stored[b], 16 + 32 * (G // 2))

            @block.tensor
            def _(pe):
                pe.sem_inc(inv, 2)
                with pe.Fori(0, G // 2) as i:
                    for b in range(2):
                        pe.wait_ge(g_in[b], (16 * FWD_LOADS) * i + 16 * FWD_LOADS)
                        pe.wait_ge(k_out, 2 * i + b + 1)
                        for n, src in ((2, ak), (3, ak), (0, au), (1, au)):
                            last = nc.tensor.matmul(psg[:, b, n, :], tw[:, b, n, :], src[:, b, :], start=True, stop=True)
                        last.then_inc(fwd, 1)
                    for b in range(2):
                        pe.wait_ge(y_ready, 2 * i + b + 1)
                        nc.tensor.matmul(psg[:, b, 2, :], tw[:, b, 4, :], yy[:, b, :], start=True, stop=True).then_inc(inv, 1)

            @block.scalar
            def _(act):
                act.sem_inc(k_out, 2)
                with act.Fori(0, G // 2) as i:
                    for b in range(2):
                        act.wait_ge(fwd, 2 * i + b + 1)
                        nc.scalar.activation(ka[:, b, :], psg[:, b, 2, :], ACT.Copy)
                        nc.scalar.activation(kb[:, b, :], psg[:, b, 3, :], ACT.Copy).then_inc(prods, 1)
                    for b in range(2):
                        act.wait_ge(inv, 2 * i + b + 3)
                        act.wait_ge(b_stored[b], 32 * i + 16)
                        nc.scalar.activation(bo[:, b, :], psg[:, b, 2, :], ACT.Copy).then_inc(b_out, 1)
                        act.wait_ge(b_out, 2 * i + b + 1)
                        act.sem_inc(k_out, 1)

            @block.vector
            def _(dve):
                with dve.Fori(0, G // 2) as i:
                    for b in range(2):
                        dve.wait_ge(prods, 2 * i + b + 1)
                        nc.vector.tensor_tensor(prod[:, b, 0, :], psg[:, b, 0, :], ka[:, b, :], ALU.mult)
                        nc.vector.tensor_tensor(prod[:, b, 1, :], psg[:, b, 1, :], kb[:, b, :], ALU.mult).then_inc(u_ready, 1)

            @block.gpsimd
            def _(pool):
                with pool.Fori(0, G // 2) as i:
                    for b in range(2):
                        pool.wait_ge(u_ready, 2 * i + b + 2)
                        nc.gpsimd.tensor_tensor(yy[:, b, :], prod[:, b, 0, :], prod[:, b, 1, :], ALU.add).then_inc(y_ready, 1)

            block_ctx.close()

        with ExitStack() as inner_ctx:
            bt = inner_ctx.enter_context(nc.sbuf_tensor("hy_bt", [P, 2, 8, D_HYENA], F32))
            x0 = inner_ctx.enter_context(nc.sbuf_tensor("hy_x0", [P, KH, SEQ], F32))
            psy = inner_ctx.enter_context(nc.psum_tensor("hy_y_ps", [P, 2, KH, BANK], F32))
            bt_in = [sem(f"bt_in{b}") for b in range(2)]
            x0_in, y_mm, y_sum, y_done, y_stored = (sem(n) for n in ("x0_in", "y_mm", "y_sum", "y_done", "y_stored"))
            block_ctx = ExitStack()
            block = block_ctx.enter_context(nc.Block())
            TG = R // 16

            @block.sync
            def _(sp):
                sp.sem_inc(y_mm, 2)
                with sp.Fori(0, TG // 2) as i:
                    for b in range(2):
                        sp.wait_ge(y_mm, 2 * i + b + 1)
                        sp.dma_start(bt[:, b, :, :], d["spec_y"][ds(32 * i + 16 * b, 16)].rearrange("(t g) r c -> (g r) t c", g=2)
                                     ).then_inc(bt_in[b], 16)
                for q in range(KH):
                    sp.dma_start(x0[:, q, :], d["proj"][HY0 + q]).then_inc(x0_in, 16)
                for q in range(KH):
                    sp.wait_ge(y_done, q + 1)
                    sp.dma_start(d["branches"][KH + q], x1[:, q, :]).then_inc(y_stored, 16)
                sp.wait_ge(y_stored, 16 * KH)

            @block.tensor
            def _(pe):
                pe.wait_ge(const_in, 32)
                with pe.Fori(0, TG // 2) as i:
                    for b in range(2):
                        pe.wait_ge(bt_in[b], 16 * i + 16)
                        pe.wait_ge(y_sum, 2 * i + b + 1)
                        for t in range(8):
                            for q in range(KH):
                                last = nc.tensor.matmul(psy[:, b, q, ds(R * t, R)], bt[:, b, t, ds(P * q, P)], idft[:, :], start=True, stop=True)
                        last.then_inc(y_mm, 1)

            @block.vector
            def _(dve):
                dve.sem_inc(y_sum, 2)
                tokens = x1[:, :, :].rearrange("p q (a b) -> p q b a", b=R)
                with dve.Fori(0, TG // 2) as i:
                    for b in range(2):
                        dve.wait_ge(y_mm, 2 * i + b + 3)
                        for q in range(KH):
                            at = tokens[:, q, ds(32 * i + 16 * b, 16), :]
                            last = nc.vector.scalar_tensor_tensor(at, psy[:, b, q, :].rearrange("p (n a) -> p n a", a=SEQ // R),
                                                                  core.rnorm[:, q:q + 1], at, ALU.mult, ALU.add)
                        last.then_inc(y_sum, 1)
                dve.wait_ge(y_sum, TG + 2)
                dve.wait_ge(x0_in, 16 * KH)
                for q in range(KH):
                    nc.vector.tensor_tensor(x1[:, q, :], x1[:, q, :], x0[:, q, :], ALU.mult).then_inc(y_done, 1)

            block_ctx.close()
        clear(nc, sems)


def merge_phase(nc, core, act_hi, act_lo):
    d = core.d
    HALF = SEQ // 2
    with ExitStack() as ctx:
        sb, ps, sem, sems = scope(nc, ctx, "merge")
        w_raw = sb("w_raw", [P, 2, KD, P])
        w_hi = sb("w_hi", [P, 2, KD, P], F32R)
        w_lo = sb("w_lo", [P, 2, KD, P], F32R)
        zero = sb("zero", [P, 1])
        zeros = zero[:, :].unsqueeze(1).broadcast_to((P, KD, P))
        gate = sb("gate", [P, 2, 2, HALF])
        out = sb("out", [P, 2, HALF])
        acc = ps("acc", [P, 2, 2, HALF])
        w_in = [sem(f"w_in{b}") for b in range(2)]
        gate_in = [sem(f"gate_in{b}") for b in range(2)]
        stored = [sem(f"stored{b}") for b in range(2)]
        zeroed, hi_done, w_ready, mm_done, evac, gated = (sem(n) for n in ("zeroed", "hi_done", "w_ready", "mm_done", "evac", "gated"))
        unit_mm, products = sem("unit_mm"), sem("products")
        block_ctx = ExitStack()
        block = block_ctx.enter_context(nc.Block())

        @block.sync
        def _(sp):
            for h in range(2):
                sp.sem_inc(stored[h], 16)
            for b in range(2):
                sp.dma_start(w_raw[:, b, :, :], d["w_o"][b]).then_inc(w_in[b], 16)

            def chunk(i, b, prefetch):
                c = 2 * i + b
                if prefetch:
                    sp.wait_ge(w_ready, c + 1)
                    sp.dma_start(w_raw[:, b, :, :], d["w_o"][ds(c + 2, 1)].rearrange("a p k n -> (a p) k n")).then_inc(w_in[b], 16)
                for h in range(2):
                    sp.wait_ge(evac, 2 * c + h + 1)
                    for n in range(2):
                        sp.dma_start(gate[:, h, n, :], d["proj"][ds(c + GATE0 + KD * n, 1), :, HALF * h:HALF * (h + 1)].rearrange("a p t -> (a p) t")
                                     ).then_inc(gate_in[h], 16)
                for h in range(2):
                    sp.wait_ge(gated, 2 * c + h + 1)
                    sp.dma_start(d["mixed"][ds(c, 1), :, HALF * h:HALF * (h + 1)].rearrange("a p t -> (a p) t"), out[:, h, :]).then_inc(stored[h], 16)

            with sp.Fori(0, KD // 2 - 1) as i:
                for b in range(2):
                    chunk(i, b, True)
            for b in range(2):
                chunk(KD // 2 - 1, b, False)
            for h in range(2):
                sp.wait_ge(stored[h], 16 * (KD + 1))

        @block.gpsimd
        def _(pool):
            pool.memset(zero[:, :], 0.0).then_inc(zeroed, 1)
            pool.wait_ge(zeroed, 1)
            with pool.Fori(0, KD // 2) as i:
                for b in range(2):
                    weight_splitter(nc, pool, i, b, 0, zeros, w_in, w_raw, w_hi, w_lo, hi_done, w_ready, mm_done)

        @block.tensor
        def _(pe):
            pe.sem_inc(mm_done, 2)
            with pe.Fori(0, KD // 2) as i:
                for b in range(2):
                    c = 2 * i + b
                    pe.wait_ge(w_ready, c + 1)
                    for h in range(2):
                        pe.wait_ge(evac, 2 * c + h + 1)
                        for n in range(2):
                            for g in range(HALF // BANK):
                                at = slice(HALF * h + BANK * g, HALF * h + BANK * (g + 1))
                                for k in range(KH):
                                    last = product(nc, acc[:, h, n, ds(BANK * g, BANK)], w_hi[:, b, KH * n + k, :], w_lo[:, b, KH * n + k, :],
                                                   act_hi[:, KH * n + k, at], act_lo[:, KH * n + k, at], k == 0, k == KH - 1)
                        last.then_inc(unit_mm, 1)
                    pe.wait_ge(unit_mm, 2 * c + 2)
                    pe.sem_inc(mm_done, 1)

        @block.vector
        def _(dve):
            dve.sem_inc(evac, 2)
            with dve.Fori(0, KD) as c:
                for h in range(2):
                    dve.wait_ge(unit_mm, 2 * c + h + 1)
                    dve.wait_ge(gate_in[h], 32 * c + 32)
                    nc.vector.tensor_tensor(gate[:, h, :, :], acc[:, h, :, :], gate[:, h, :, :], ALU.mult).then_inc(products, 1)
                    dve.wait_ge(products, 2 * c + h + 1)
                    dve.wait_ge(stored[h], 16 * c + 16)
                    nc.vector.tensor_tensor(out[:, h, :], gate[:, h, 0, :], gate[:, h, 1, :], ALU.add).then_inc(gated, 1)
                    dve.wait_ge(gated, 2 * c + h + 1)
                    dve.sem_inc(evac, 1)

        block_ctx.close()
        clear(nc, sems)


def down_phase(nc, core):
    d = core.d
    with ExitStack() as ctx:
        sb, ps, sem, sems = scope(nc, ctx, "down")
        w_hi = sb("w_hi", [P, FF_CHUNKS, D_MODEL], F32R)
        w_lo = sb("w_lo", [P, FF_CHUNKS, D_MODEL], F32R)
        raw = sb("raw", [P, 2, D_MODEL])
        g_raw = sb("g_raw", [P, 2, BANK])
        g_hi, g_lo = sb("g_hi", [P, 2, BANK], F32R), sb("g_lo", [P, 2, BANK], F32R)
        out = sb("out", [P, 2, BANK])
        acc = ps("acc", [P, KD, BANK])
        w_in = [sem(f"w_in{b}") for b in range(2)]
        g_in = [sem(f"g_in{b}") for b in range(2)]
        stored = [sem(f"stored{b}") for b in range(2)]
        w_hi_done, w_lo_done, g_hi_done, g_ready, mm_done, out_mm, evac = (
            sem(n) for n in ("w_hi_done", "w_lo_done", "g_hi_done", "g_ready", "mm_done", "out_mm", "evac"))
        GROUPS = SEQ // BANK
        block_ctx = ExitStack()
        block = block_ctx.enter_context(nc.Block())

        @block.sync
        def _(sp):
            for b in range(2):
                sp.sem_inc(stored[b], 16)
            for k in range(FF_CHUNKS):
                if k >= 2:
                    sp.wait_ge(w_lo_done, k - 1)
                sp.dma_start(raw[:, k % 2, :], d["w_down"][k]).then_inc(w_in[k % 2], 16)
            with sp.Fori(0, GROUPS) as t:
                for k in range(FF_CHUNKS):
                    sp.wait_ge(g_ready, FF_CHUNKS * t + k + 1)
                    sp.dma_start(g_raw[:, k % 2, :], d["hidden"][k, :, ds(BANK * t, BANK)]).then_inc(g_in[k % 2], 16)
                for n in range(KD):
                    sp.wait_ge(evac, KD * t + n + 1 + KD)
                    sp.dma_start(d["branch"][n, :, ds(BANK * t, BANK)], out[:, n % 2, :]).then_inc(stored[n % 2], 16)
            for b in range(2):
                sp.wait_ge(stored[b], 16 * (GROUPS * KD // 2 + 1))

        @block.tensor
        def _(pe):
            with pe.Fori(0, GROUPS) as t:
                for k in range(FF_CHUNKS):
                    pe.wait_ge(w_lo_done, k + 1)
                    pe.wait_ge(g_ready, FF_CHUNKS * t + k + 3)
                    for n in range(KD):
                        if k == 0:
                            pe.wait_ge(evac, KD * t + n + 1)
                        w = slice(P * n, P * n + P)
                        last = product(nc, acc[:, n, :], w_hi[:, k, w], w_lo[:, k, w], g_hi[:, k % 2, :], g_lo[:, k % 2, :],
                                       k == 0, k == FF_CHUNKS - 1)
                        if k == FF_CHUNKS - 1 :
                            last.then_inc(out_mm, 1)
                    if k < FF_CHUNKS - 1:
                        last.then_inc(mm_done, 1)
                    else:
                        pe.wait_ge(out_mm, KD * t + KD)
                        pe.sem_inc(mm_done, 1)

        @block.scalar
        def _(act):
            act.sem_inc(evac, KD)
            act.sem_inc(mm_done, 2)
            for k in range(FF_CHUNKS):
                act.wait_ge(w_in[k % 2], 16 * (k // 2 + 1))
                nc.scalar.activation(w_hi[:, k, :], raw[:, k % 2, :], ACT.Copy).then_inc(w_hi_done, 1)
            with act.Fori(0, GROUPS) as t:
                for k in range(FF_CHUNKS):
                    act.wait_ge(g_in[k % 2], (16 * (FF_CHUNKS // 2)) * t + 16 * (k // 2 + 1))
                    act.wait_ge(mm_done, FF_CHUNKS * t + k + 1)
                    nc.scalar.activation(g_hi[:, k % 2, :], g_raw[:, k % 2, :], ACT.Copy).then_inc(g_hi_done, 1)
                for n in range(KD):
                    act.wait_ge(out_mm, KD * t + n + 1)
                    act.wait_ge(stored[n % 2], (16 * (KD // 2)) * t + 16 * (n // 2 + 1))
                    nc.scalar.activation(out[:, n % 2, :], acc[:, n, :], ACT.Copy).then_inc(evac, 1)

        @block.vector
        def _(dve):
            dve.sem_inc(g_ready, 2)
            for k in range(FF_CHUNKS):
                dve.wait_ge(w_hi_done, k + 1)
                nc.vector.tensor_tensor(w_lo[:, k, :], raw[:, k % 2, :], w_hi[:, k, :].bitcast(F32), ALU.subtract).then_inc(w_lo_done, 1)
            with dve.Fori(0, GROUPS) as t:
                for k in range(FF_CHUNKS):
                    dve.wait_ge(g_hi_done, FF_CHUNKS * t + k + 1)
                    nc.vector.tensor_tensor(g_lo[:, k % 2, :], g_raw[:, k % 2, :], g_hi[:, k % 2, :].bitcast(F32), ALU.subtract).then_inc(g_ready, 1)

        block_ctx.close()
        clear(nc, sems)


def layer_program(nc, d):
    core = Core(nc, d)
    for name, shape in (("proj", (IN_CHUNKS, P, SEQ)), ("ctx_kv", (2 * KH, P, CTX_LEN)), ("branches", (KD, P, SEQ)),
                        ("mixed", (KD, P, SEQ)), ("branch", (KD, P, SEQ)), ("x1", (KD, P, SEQ)), ("hidden", (FF_CHUNKS, P, SEQ)),
                        ("spec_k", (R, R, D_HYENA)), ("spec_u", (R, R, D_HYENA)), ("spec_y", (R, R, D_HYENA))):
        d[name] = nc.dram_tensor(f"scratch_{name}", shape, F32).ap()
    with ExitStack() as ctx:
        core.vec = ctx.enter_context(nc.sbuf_tensor("vec", [P, N_VEC], F32))
        core.mod = ctx.enter_context(nc.sbuf_tensor("mod", [P, MOD_CHUNKS, 2], F32))
        core.mean = ctx.enter_context(nc.sbuf_tensor("mean", [P, P], F32))
        core.ident = ctx.enter_context(nc.sbuf_tensor("ident", [P, P], F32))
        core.rnorm = ctx.enter_context(nc.sbuf_tensor("rnorm", [P, KH], F32))
        setup_phase(nc, core)
        filter_phase(nc, core)

        def operand(stack, tag, tokens):
            return (stack.enter_context(nc.sbuf_tensor(f"{tag}_hi", [P, KD, tokens], F32R)),
                    stack.enter_context(nc.sbuf_tensor(f"{tag}_lo", [P, KD, tokens], F32R)))

        with ExitStack() as s:
            hi, lo = operand(s, "ctx_act", CTX_LEN)
            norm_phase(nc, core, "norm_ctx", d["ctx"], CTX_LEN, hi, lo, VEC["mix_pre"], 1, SH_MIX, SC_MIX)
            projection_phase(nc, core, "proj_ctx", "bias", d["w_in"], K0, 2 * KH, hi, lo, CTX_LEN, d["ctx_kv"], VEC["b_in"] + K0)
        with ExitStack() as s:
            hi, lo = operand(s, "mix_act", SEQ)
            norm_phase(nc, core, "norm_mix", d["x"], SEQ, hi, lo, VEC["mix_pre"], 0, SH_MIX, SC_MIX)
            for tag, kind, first, last in (("proj_qkv", "bias", Q0, HY0), ("proj_hy", "conv", HY0, GATE0), ("proj_gate", "sigmoid", GATE0, IN_CHUNKS)):
                projection_phase(nc, core, tag, kind, d["w_in"], first, last - first, hi, lo, SEQ, d["proj"][first:last], VEC["b_in"] + first)
        attention_phase(nc, core)
        hyena_phase(nc, core)
        with ExitStack() as s:
            hi, lo = operand(s, "branch_act", SEQ)
            split_phase(nc, core, "split_branches", d["branches"], hi, lo)
            merge_phase(nc, core, hi, lo)
            split_phase(nc, core, "split_mixed", d["mixed"], hi, lo)
            projection_phase(nc, core, "proj_out", "plain", d["w_out"], 0, KD, hi, lo, SEQ, d["branch"])
        with ExitStack() as s:
            hi, lo = operand(s, "ffn_act", SEQ)
            norm_phase(nc, core, "norm_ffn", d["x"], SEQ, hi, lo, VEC["ffn_pre"], 0, SH_FFN, SC_FFN,
                       add=(d["branch"], G_MIX, VEC["mix_post"], d["x1"]))
            projection_phase(nc, core, "proj_up", "ffn", d["w_up"], 0, 2 * FF_CHUNKS, hi, lo, SEQ, d["hidden"])
        down_phase(nc, core)
        norm_phase(nc, core, "norm_out", d["x1"], SEQ, None, None, None, 0, None, None,
                   add=(d["branch"], G_FFN, VEC["ffn_post"], d["out"]))


def frequencies(g):
    if g:
        return [(g + R * k2, part) for part in ("re", "im") for k2 in range(R)]
    return ([(R * k2, "re") for k2 in range(33)] + [(32 + R * k2, "re") for k2 in range(32)]
            + [(R * k2, "im") for k2 in range(1, 32)] + [(32 + R * k2, "im") for k2 in range(32)])


def root(e):
    return np.exp(-2j * np.pi * np.asarray(e) / NFFT)


def stage1(n1):
    m = np.zeros((len(n1), R))
    for g in range(R // 2):
        for c in range(2):
            if g == 0:
                m[:, c] = root(R * n1 * (32 * c)).real
            else:
                z = root(R * n1 * g)
                m[:, 2 * g + c] = z.imag if c else z.real
    return m


def inverse_stage1(n1):
    m = np.zeros((R, len(n1)))
    for g in range(R // 2):
        for c in range(2):
            if g == 0:
                m[c] = root(R * n1 * (32 * c)).real
            else:
                z = np.conj(root(R * n1 * g))
                m[2 * g + c] = -z.imag if c else z.real
    return m


def twiddles():
    n2 = np.arange(R)
    groups = []
    for g in range(R // 2):
        rows = frequencies(g)

        def forward(rows):
            m = np.zeros((P, P))
            for i, (k, part, sign) in enumerate(rows):
                z = root(n2 * k) * sign
                if g:
                    m[:R, i], m[R:, i] = (z.real, -z.imag) if part == "re" else (z.imag, z.real)
                else:
                    c = int(k % R != 0)
                    m[R * c:R * c + R, i] = z.real if part == "re" else z.imag
            return m

        other = {"re": "im", "im": "re"}
        real = lambda k: k % (NFFT // 2) == 0
        x = forward([(k, part, 1) for k, part in rows])
        xs = forward([(k, other[part], 0 if real(k) else (-1 if part == "re" else 1)) for k, part in rows])
        ka = forward([(k, "re", 1) for k, part in rows])
        kb = forward([(k, "im", 0 if real(k) else 1) for k, part in rows])
        inv = np.zeros((P, P))
        for i, (k, part) in enumerate(rows):
            z = np.conj(root(n2 * k)) * ((1 if real(k) else 2) / NFFT)
            v = z if part == "re" else 1j * z
            if g:
                inv[i, :R], inv[i, R:] = v.real, v.imag
            else:
                c = int(k % R != 0)
                inv[i, R * c:R * c + R] = v.real
        groups.append(np.stack([x, xs, ka, kb, inv], 1))
    return np.array(groups)


def shape_constants():
    f = np.float32
    c = {}
    c["ident"] = np.eye(P, dtype=f)
    c["mean"] = np.full((P, P), 1.0 / D_MODEL, f)
    j, side, g, n1 = np.meshgrid(np.arange(R // 2), np.arange(2), np.arange(2), np.arange(32), indexing="ij")
    n = (R * (32 * side + n1) + 2 * j + g).reshape(-1)
    pos = np.where(n <= SEQ, n, NFFT - n).astype(f)
    t = pos / f(SEQ - 1)
    bands = np.linspace(1e-4, POS_BANDS - 1, POS_BANDS, dtype=f)
    ang = (f(2.0 * np.pi / SEQ) * pos)[:, None] * bands[None, :]
    c["z"] = np.ascontiguousarray(np.concatenate([t[:, None], np.cos(ang), -np.sin(ang)], 1).astype(f).T)
    c["neg_t"] = np.ascontiguousarray(-t.reshape(-1, P).T)
    c["keep"] = np.ascontiguousarray((n != SEQ).astype(f).reshape(-1, P).T)
    s1 = stage1(np.arange(R))
    dft_k = np.zeros((2, 2, 32, 2, R))
    for gg in range(2):
        for side in range(2):
            dft_k[side, gg, :, gg, :] = s1[32 * side:32 * side + 32]
    c["dft_k"] = dft_k.reshape(P, P).astype(f)
    dft_u = np.zeros((4, 32, 2, 2, R))
    for gg in range(4):
        dft_u[gg, :, gg // 2, gg % 2, :] = s1[:32]
    c["dft_u"] = dft_u.reshape(P, 2, P).astype(f)
    idft = np.zeros((2, R, 2, 32))
    for gg in range(2):
        idft[gg, :, gg, :] = inverse_stage1(np.arange(32))
    c["idft"] = idft.reshape(P, R).astype(f)
    c["twiddle"] = twiddles().astype(f)
    tok = np.arange(SEQ)
    inv_freq = (f(10000.0) ** (-np.arange(16, dtype=f) / f(16))).astype(f)
    cos, sin = np.zeros((P, SEQ), f), np.zeros((P, SEQ), f)
    for ch in range(P):
        axis = (tok // GRID_W, tok % GRID_W)[ch % HEAD_DIM // 32].astype(f)
        a = axis * inv_freq[ch % 16]
        cos[ch], sin[ch] = np.cos(a), np.sin(a) * (-1 if ch % 32 < 16 else 1)
    c["cos"], c["sin"] = cos, sin
    qc, kc = np.arange(GRID_W)[:, None], np.arange(GRID_W)[None, :]
    start = np.clip(qc - WIN_COLS // 2, 0, GRID_W - WIN_COLS)
    mask = np.where((kc >= start) & (kc < start + WIN_COLS), 0.0, MASKED).astype(f)
    c["colmask"] = np.tile(mask, (2, 1))
    return c


def laid_out(x, c, ctx, c_ctx, w_mod, b_mod, norm_mix_pre, norm_mix_post, norm_ffn_pre, norm_ffn_post,
             w_in, b_in, na_rpb, hy_conv_w, hy_conv_b, hy_filt_w1, hy_filt_b1, hy_filt_w2, hy_filt_b2,
             hy_filt_w3, hy_filt_b3, hy_sin_freq, hy_decay, hy_skip, w_o_na, w_o_hy, w_out,
             ffn_w_up, ffn_conv_w, ffn_conv_b, ffn_w_down):
    def tiles(w):
        k, n = w.shape[0] // P, w.shape[1] // P
        return np.ascontiguousarray(w.reshape(k, P, n, P).transpose(2, 1, 0, 3))

    def cols(v):
        return np.asarray(v).reshape(-1, P).T

    def pairs(v):
        s = v.shape[:-1]
        return np.swapaxes(v.reshape(*s, 2, FF_CHUNKS, P), -3, -2).reshape(*s, 2 * D_FF)

    a = {}
    a["x"] = np.ascontiguousarray(x[0].T).reshape(KD, P, SEQ)
    a["ctx"] = np.ascontiguousarray(ctx[0].T).reshape(KD, P, CTX_LEN)
    a["cond"] = np.ascontiguousarray(np.stack([cols(c[0]), cols(c_ctx)], -1))
    a["w_mod"] = np.concatenate([tiles(w_mod[0]), np.zeros((3, P, KD, P), w_mod.dtype)])
    a["w_in"] = tiles(w_in[0])
    a["w_o"] = tiles(np.concatenate([w_o_na[0], w_o_hy[0]]))
    a["w_out"] = tiles(w_out[0])
    a["w_up"] = tiles(pairs(ffn_w_up[0]))
    a["w_down"] = np.ascontiguousarray(ffn_w_down[0].reshape(FF_CHUNKS, P, D_MODEL))
    cw, fw = hy_conv_w[0], pairs(ffn_conv_w[0])
    a["vec"] = np.ascontiguousarray(np.concatenate([cols(v) for v in (
        b_in[0], b_mod[0], norm_mix_pre[0], norm_mix_post[0], norm_ffn_pre[0], norm_ffn_post[0],
        cw[0], cw[1], cw[2], hy_conv_b[0], hy_skip[0], fw[0], fw[1], fw[2], pairs(ffn_conv_b[0]))], 1))
    a["filt_w1"], a["filt_w2"], a["filt_w3"] = hy_filt_w1[0], hy_filt_w2[0], hy_filt_w3[0]
    a["filt_hid"] = np.ascontiguousarray(np.stack([hy_filt_b1[0], hy_sin_freq[0, 0], hy_filt_b2[0], hy_sin_freq[0, 1]], 1))
    a["filt_b3"] = hy_filt_b3[0].reshape(2, D_HYENA)
    a["decay"] = hy_decay[0]
    qc, kc = np.arange(GRID_W)[:, None], np.arange(GRID_W)[None, :]
    dc = np.clip(kc - qc, 1 - WIN_COLS, WIN_COLS - 1) + WIN_COLS - 1
    rel = na_rpb[0][:, :, dc].transpose(0, 2, 1, 3)
    a["rpb"] = np.ascontiguousarray(np.stack([rel[:, :, 1 - qr:15 - qr] for qr in range(2)], 1)).reshape(N_HEADS, P, 14 * GRID_W)
    return a


def kernel(**inputs):
    import concourse.bacc as bacc
    from concourse.bass_utils import run_bass_kernel_spmd

    arrays = {**laid_out(**{k: np.asarray(v) for k, v in inputs.items()}), **shape_constants()}
    nc = bacc.Bacc("TRN2", target_bir_lowering=False, num_devices=1)
    d = {n: nc.dram_tensor(f"in_{n}", a.shape, mybir.dt.from_np(a.dtype), kind="ExternalInput").ap() for n, a in arrays.items()}
    d["out"] = nc.dram_tensor("out", (KD, P, SEQ), F32, kind="ExternalOutput").ap()
    layer_program(nc, d)
    result = run_bass_kernel_spmd(nc, [{f"in_{n}": np.ascontiguousarray(a) for n, a in arrays.items()}], core_ids=[0])
    return np.ascontiguousarray(result.results[0]["out"].reshape(D_MODEL, SEQ).T)[None]
```

```python
from contextlib import ExitStack

import concourse.bass as bass
import numpy as np
from concourse import mybir

F32 = mybir.dt.float32
F32R = mybir.dt.float32r
ALU = mybir.AluOpType
ACT = mybir.ActivationFunctionType
AX = mybir.AxisListType
ds = bass.ds

P = 128
D_MODEL, SEQ, CTX_LEN = 1024, 2048, 256
KD = D_MODEL // P
N_HEADS, HEAD_DIM, GRID_W = 8, 64, 64
ROWS = SEQ // GRID_W
D_ATTN, D_HYENA, D_FF = 512, 512, 2816
WIN_ROWS, WIN_COLS = 8, 16
KH = D_HYENA // P
FF_CHUNKS = D_FF // P
FILTER_HIDDEN, POS_BANDS = 64, 16
RMS_EPS = 1e-6
MASKED = -1e30
BANK = 512

Q0, K0, V0, HY0, GATE0, IN_CHUNKS = 0, 4, 8, 12, 24, 40
MOD_CHUNKS = 48
SH_MIX, SC_MIX, G_MIX, SH_FFN, SC_FFN, G_FFN = (KD * i for i in range(6))

NFFT = 2 * SEQ
R = 64

HEAD_ORDER = np.arange(HEAD_DIM).reshape(2, 2, 16).transpose(1, 0, 2).reshape(-1)

VEC = {}
_at = 0
for _name, _n in (("b_in", 40), ("b_mod", 48), ("mix_pre", 8), ("mix_post", 8), ("ffn_pre", 8), ("ffn_post", 8),
                  ("hy_w0", 12), ("hy_w1", 12), ("hy_w2", 12), ("hy_b", 12), ("skip", 4),
                  ("ff_w0", 44), ("ff_w1", 44), ("ff_w2", 44), ("ff_b", 44)):
    VEC[_name] = _at
    _at += _n
N_VEC = _at


class Core:

    def __init__(self, nc, dram):
        self.nc, self.d = nc, dram


def scope(nc, ctx, tag):
    sems = []

    def sb(name, shape, dt=F32):
        return ctx.enter_context(nc.sbuf_tensor(f"{tag}_{name}", shape, dt))

    def ps(name, shape):
        return ctx.enter_context(nc.psum_tensor(f"{tag}_{name}", shape, F32))

    def sem(name):
        s = ctx.enter_context(nc.semaphore(f"{tag}_{name}"))
        sems.append(s)
        return s

    return sb, ps, sem, sems


def clear(nc, sems):
    with nc.Block() as block:
        @block.gpsimd
        def _(pool):
            nums = sorted(s.num for s in sems)
            starts = [n for n in nums if n - 1 not in nums]
            ends = [n + 1 for n in nums if n + 1 not in nums]
            for a, b in zip(starts, ends):
                pool.sem_clear(range(a, b))


def setup_phase(nc, core):
    d = core.d
    with ExitStack() as ctx:
        sb, ps, sem, sems = scope(nc, ctx, "setup")
        const_in = sem("const_in")
        with nc.Block() as block:
            @block.sync
            def _(sp):
                sp.dma_start(core.vec[:, :], d["vec"]).then_inc(const_in, 16)
                sp.dma_start(core.ident[:, :], d["ident"]).then_inc(const_in, 16)
                sp.dma_start(core.mean[:, :], d["mean"]).then_inc(const_in, 16)
                sp.wait_ge(const_in, 48)
        clear(nc, sems)


def filter_phase(nc, core):
    d = core.d
    half = NFFT // 2
    two_pi_1, two_pi_2 = 6.28125, 0.0019350051879882812
    two_pi_3 = float(np.float64(2 * np.pi) - two_pi_1 - two_pi_2)
    magic = float(1.5 * 2 ** 23)
    pi_below = 3.1415925
    with ExitStack() as ctx:
        sb, ps, sem, sems = scope(nc, ctx, "filt")
        z = sb("z", [2 * POS_BANDS + 1, NFFT])
        w1 = sb("w1", [2 * POS_BANDS + 1, FILTER_HIDDEN])
        w2 = sb("w2", [P, FILTER_HIDDEN])
        w3 = sb("w3", [P, 2 * D_HYENA])
        hid = sb("hid", [P, 4])
        b3 = sb("b3", [P, D_HYENA])
        decay = sb("decay", [P, D_HYENA])
        neg_t = sb("neg_t", [P, NFFT // P])
        keep = sb("keep", [P, NFFT // P])
        dft = sb("dft", [P, P])
        ones = sb("ones", [P, 1])
        h1 = sb("h1", [P, half])
        h2 = sb("h2", [P, half])
        turns = sb("turns", [P, half])
        cond = sb("cond", [P, KD, 2])
        cond_s = sb("cond_s", [P, KD, 2])
        wm = sb("wm", [P, 4, KD // 2, BANK])
        mod_row = sb("mod_row", [2, MOD_CHUNKS * P])
        hs = sb("hs", [P, 2, P])
        dec = sb("dec", [P, 2, D_HYENA])
        kc = sb("kc", [P, 2, D_HYENA])
        kabs = sb("kabs", [P, 2, D_HYENA])
        ksum = sb("ksum", [P, D_HYENA])
        spec = sb("spec", [P, 2, D_HYENA])
        ps_h = ps("ps_h", [P, half])
        ps_s = ps("ps_s", [P, 2, BANK])
        ps_m = ps("ps_m", [P, MOD_CHUNKS, 2])
        ps_n = ps("ps_n", [P, KH])

        const_in, z_ready, mm_layer, layer, wrap = sem("const_in"), sem("z_ready"), sem("mm_layer"), sem("layer"), sem("wrap")
        wm_in = [sem(f"wm_in{m}") for m in range(4)]
        silu, wm_used, mod_mm, mod_out, mod_flip, mod_done = (sem(n) for n in ("silu", "wm_used", "mod_mm", "mod_out", "mod_flip", "mod_done"))
        hs_ready, tile_mm, dec_ready, kc_step, kc_ready = sem("hs_ready"), sem("tile_mm"), sem("dec_ready"), sem("kc_step"), sem("kc_ready")
        kabs_ready, ksum_done, spec_mm, spec_out = sem("kabs_ready"), sem("ksum_done"), sem("spec_mm"), sem("spec_out")
        stored = [sem(f"stored{s}") for s in range(2)]
        norm_mm, norm_done, tile_begun = sem("norm_mm"), sem("norm_done"), sem("tile_begun")
        tiles = NFFT // P // 2
        n_const = 16
        MOD_ROUNDS = MOD_CHUNKS * P // (2 * BANK)

        block_ctx = ExitStack()
        block = block_ctx.enter_context(nc.Block())

        @block.sync
        def _(sp):
            for dst, src in ((z, "z"), (w1, "filt_w1")):
                sp.dma_start(dst[:, :], d[src]).then_inc(const_in, 16)
            for h in range(2):
                sp.dma_start(w2[64 * h:64 * h + 64, :], d["filt_w2"]).then_inc(const_in, 16)
                sp.dma_start(w3[64 * h:64 * h + 64, :], d["filt_w3"]).then_inc(const_in, 16)
                sp.dma_start(hid[64 * h:64 * h + 64, :], d["filt_hid"]).then_inc(const_in, 16)
                sp.dma_start(b3[64 * h:64 * h + 64, :], d["filt_b3"][h:h + 1, :].partition_broadcast(64)).then_inc(const_in, 16)
                sp.dma_start(decay[64 * h:64 * h + 64, :], d["decay"][h:h + 1, :].partition_broadcast(64)).then_inc(const_in, 16)
            sp.dma_start(neg_t[:, :], d["neg_t"]).then_inc(const_in, 16)
            sp.dma_start(keep[:, :], d["keep"]).then_inc(const_in, 16)
            sp.dma_start(cond[:, :, :], d["cond"]).then_inc(const_in, 16)
            sp.dma_start(dft[:, :], d["dft_k"]).then_inc(const_in, 16)
            sp.sem_inc(stored[0], 16)
            sp.sem_inc(stored[1], 16)
            with sp.Fori(0, MOD_ROUNDS) as i:
                for m in range(4):
                    sp.wait_ge(wm_used, 4 * i + m + 1)
                    sp.dma_start(wm[:, m, :, :], d["w_mod"][:, m % 2, :, ds((2 * BANK) * i + BANK * (m // 2), BANK)]).then_inc(wm_in[m], 16)
            with sp.Fori(0, tiles) as i:
                for s in range(2):
                    sp.wait_ge(spec_out, 2 * i + s + 3)
                    sp.dma_start(d["spec_k"][ds((2 * i) + 2 * tiles * s, 2)].rearrange("g r c -> (g r) c"),
                                 spec[:, s, :]).then_inc(stored[s], 16)
            for s in range(2):
                sp.wait_ge(stored[s], 16 * (tiles + 1))

        @block.gpsimd
        def _(pool):
            pool.sem_inc(ksum_done, 2)
            pool.memset(ksum[:, :], 0.0).then_inc(ksum_done, 1)
            pool.memset(ones[:, :], 1.0).then_inc(z_ready, 1)
            with pool.Fori(0, tiles) as i:
                for s in range(2):
                    pool.wait_ge(ksum_done, 2 * i + s + 3)
                    pool.wait_ge(kabs_ready, 2 * i + s + 1)
                    nc.gpsimd.tensor_tensor(ksum[:, :], ksum[:, :], kabs[:, s, :], ALU.add).then_inc(ksum_done, 1)

        @block.tensor
        def _(pe):
            def modulation(start, end):
                with pe.Fori(start, end) as i:
                    for g in range(2):
                        pe.wait_ge(mod_out, 2 * i + g + 1)
                        for h in range(2):
                            pe.wait_ge(wm_in[2 * g + h], 16 * i + 16)
                            for k in range(KD // 2):
                                last = nc.tensor.matmul(ps_s[0:2, g, :], cond_s[:, KD // 2 * h + k, :], wm[:, 2 * g + h, k, :],
                                                        start=(h == 0 and k == 0), stop=(h == 1 and k == KD // 2 - 1))
                            if h == 0:
                                last.then_inc(wm_used, 1)
                        last.then_inc(mod_mm, 1)
                        pe.wait_ge(mod_mm, 2 * i + g + 1)
                        pe.sem_inc(wm_used, 1)

            pe.sem_inc(wm_used, 4)
            pe.wait_ge(const_in, 16 * n_const)
            for h in range(2):
                for g in range(half // BANK):
                    last = nc.tensor.matmul(ps_h[64 * h:64 * h + 64, ds(BANK * g, BANK)], w1[:, :],
                                            z[:, ds(half * h + BANK * g, BANK)], start=True, stop=True)
            last.then_inc(mm_layer, 1)
            pe.wait_ge(silu, 1)
            modulation(0, 1)
            pe.wait_ge(layer, 1)
            for h in range(2):
                for g in range(half // BANK):
                    last = nc.tensor.matmul(ps_h[64 * h:64 * h + 64, ds(BANK * g, BANK)], w2[64 * h:64 * h + 64, :],
                                            h1[64 * h:64 * h + 64, ds(BANK * g, BANK)], start=True, stop=True)
            last.then_inc(mm_layer, 1)
            modulation(1, 2)
            pe.wait_ge(layer, 2)
            pe.wait_ge(z_ready, 2)
            modulation(2, MOD_ROUNDS)
            pe.wait_ge(mod_out, 2 * MOD_ROUNDS + 2)
            for c in range(MOD_CHUNKS):
                last = nc.tensor.transpose(ps_m[:, c, :], mod_row[:, P * c:P * c + P], core.ident[0:2, 0:2])
            last.then_inc(mod_flip, 1)

            with pe.Fori(0, tiles) as i:
                for s in range(2):
                    pe.wait_ge(hs_ready, 2 * i + s + 1)
                    pe.wait_ge(kc_ready, 2 * i + s + 1)
                    pe.sem_inc(tile_begun, 1)
                    for h in range(2):
                        last = nc.tensor.matmul(ps_h[64 * h:64 * h + 64, ds(BANK * s, BANK)],
                                                hs[64 * s:64 * s + 64, s, 64 * h:64 * h + 64],
                                                w3[64 * s:64 * s + 64, ds(D_HYENA * h, D_HYENA)], start=True, stop=True)
                    last.then_inc(tile_mm, 1)
                for s in range(2):
                    pe.wait_ge(kc_ready, 2 * i + s + 3)
                    nc.tensor.matmul(ps_s[:, s, :], dft[:, :], kc[:, s, :], start=True, stop=True).then_inc(spec_mm, 1)
            pe.wait_ge(tile_begun, 2 * tiles)
            pe.wait_ge(ksum_done, 2 * tiles + 3)
            for q in range(KH):
                last = nc.tensor.matmul(ps_n[:, q:q + 1], ksum[:, ds(P * q, P)], ones[:, :], start=True, stop=True)
            last.then_inc(norm_mm, 1)

        @block.scalar
        def _(act):
            def modulation(start, end):
                with act.Fori(start, end) as i:
                    for g in range(2):
                        act.wait_ge(mod_mm, 2 * i + g + 1)
                        nc.scalar.activation(mod_row[:, ds((2 * BANK) * i + BANK * g, BANK)], ps_s[0:2, g, :], ACT.Copy).then_inc(mod_out, 1)

            act.sem_inc(spec_out, 2)
            act.sem_inc(mod_out, 2)
            act.wait_ge(const_in, 16 * n_const)
            nc.scalar.activation(cond_s[:, :, :], cond[:, :, :], ACT.Silu).then_inc(silu, 1)
            nc.scalar.activation(decay[:, :], decay[:, :], ACT.Abs).then_inc(z_ready, 1)
            for n in range(2):
                modulation(n, n + 1)
                act.wait_ge(wrap, 7 * n + 7)
                nc.scalar.activation((h1, h2)[n][:, :], turns[:, :], ACT.Sin).then_inc(layer, 1)
            modulation(2, MOD_ROUNDS)
            act.wait_ge(z_ready, 2)
            with act.Fori(0, tiles) as i:
                for s in range(2):
                    act.wait_ge(kc_ready, 2 * i + s + 1)
                    nc.scalar.activation(dec[:, s, :], decay[:, :], ACT.Exp,
                                         scale=neg_t[:, ds(i + tiles * s, 1)]).then_inc(dec_ready, 1)
                for s in range(2):
                    act.wait_ge(kc_ready, 2 * i + s + 3)
                    act.wait_ge(ksum_done, 2 * i + s + 2)
                    nc.scalar.activation(kabs[:, s, :], kc[:, s, :], ACT.Abs).then_inc(kabs_ready, 1)
                    act.wait_ge(spec_mm, 2 * i + s + 1)
                    act.wait_ge(stored[s], 16 * i + 16)
                    nc.scalar.activation(spec[:, s, :], ps_s[:, s, :], ACT.Copy).then_inc(spec_out, 1)

        @block.vector
        def _(dve):
            done = [0]

            def chain(ins):
                ins.then_inc(wrap, 1)
                done[0] += 1
                dve.wait_ge(wrap, done[0])

            dve.sem_inc(kc_ready, 2)
            dve.wait_ge(const_in, 16 * n_const)
            for n in range(2):
                dve.wait_ge(mm_layer, n + 1)
                chain(nc.vector.tensor_scalar(h2[:, :], ps_h[:, :], hid[:, 2 * n:2 * n + 1], hid[:, 2 * n + 1:2 * n + 2], ALU.add, ALU.mult))
                chain(nc.vector.tensor_scalar(turns[:, :], h2[:, :], float(1 / (2 * np.pi)), magic, ALU.mult, ALU.add))
                chain(nc.vector.tensor_scalar(turns[:, :], turns[:, :], -magic, None, ALU.add))
                chain(nc.vector.scalar_tensor_tensor(h2[:, :], turns[:, :], -two_pi_1, h2[:, :], ALU.mult, ALU.add))
                chain(nc.vector.scalar_tensor_tensor(h2[:, :], turns[:, :], -two_pi_2, h2[:, :], ALU.mult, ALU.add))
                chain(nc.vector.scalar_tensor_tensor(h2[:, :], turns[:, :], -two_pi_3, h2[:, :], ALU.mult, ALU.add))
                chain(nc.vector.tensor_scalar(turns[:, :], h2[:, :], pi_below, -pi_below, ALU.min, ALU.max))
            dve.wait_ge(layer, 2)

            with dve.Fori(0, tiles) as i:
                for s in range(2):
                    nc.vector.tensor_copy(hs[64 * s:64 * s + 64, s, :], h2[64 * s:64 * s + 64, ds(P * i, P)]).then_inc(hs_ready, 1)
                for s in range(2):
                    dve.wait_ge(tile_mm, 2 * i + s + 1)
                    dve.wait_ge(spec_out, 2 * i + s + 1)
                    nc.vector.tensor_tensor(kc[:, s, :], ps_h[:, ds(BANK * s, BANK)], b3[:, :], ALU.add).then_inc(kc_step, 1)
                    dve.wait_ge(kc_step, 2 * i + s + 1)
                    dve.wait_ge(dec_ready, 2 * i + s + 1)
                    nc.vector.scalar_tensor_tensor(kc[:, s, :], kc[:, s, :], keep[:, ds(i + tiles * s, 1)], dec[:, s, :],
                                                   ALU.mult, ALU.mult).then_inc(kc_ready, 1)
            dve.wait_ge(mod_flip, 1)
            nc.vector.tensor_tensor(core.mod[:, :, :], ps_m[:, :, :],
                                    core.vec[:, VEC["b_mod"]:VEC["b_mod"] + MOD_CHUNKS].unsqueeze(2).broadcast_to((P, MOD_CHUNKS, 2)), ALU.add
                                    ).then_inc(mod_done, 1)
            dve.wait_ge(mod_done, 1)
            dve.wait_ge(norm_mm, 1)
            nc.vector.reciprocal(core.rnorm[:, :], ps_n[:, :]).then_inc(norm_done, 1)
            dve.wait_ge(norm_done, 1)

        block_ctx.close()
        clear(nc, sems)


def mean_square(pe, core, out, sq):
    nc = core.nc
    for k in range(KD):
        last = nc.tensor.matmul(out, core.mean[:, :], sq[:, k, :], start=(k == 0), stop=(k == KD - 1))
    return last


def norm_phase(nc, core, tag, x_d, tokens, act_hi, act_lo, norm_w, cond_col, shift, scale, add=None):
    W = 256
    groups = tokens // W
    nb = min(2, groups)
    rounds = groups // nb
    with ExitStack() as ctx:
        sb, ps, sem, sems = scope(nc, ctx, tag)
        x = sb("x", [P, nb, KD, W])
        r = sb("r", [P, nb, KD, W]) if add else None
        sq = sb("sq", [P, KD, W])
        t = sb("t", [P, KD, W])
        rs = sb("rs", [P, 2, W])
        col = sb("col", [P, 3, KD])
        ms = ps("ms", [P, 2, BANK])
        x_in = [sem(f"x_in{b}") for b in range(nb)]
        r_in = [sem(f"r_in{b}") for b in range(nb)] if add else None
        stored = [sem(f"stored{b}") for b in range(nb)]
        cols, squared, ms_done, eps_added, rooted, rs_done = (sem(n) for n in ("cols", "squared", "ms_done", "eps_added", "rooted", "rs_done"))
        scaled, x1_step, x1_done, shifted, hi_done, lo_done = (sem(n) for n in ("scaled", "x1_step", "x1_done", "shifted", "hi_done", "lo_done"))
        want = act_hi is not None
        stats = int(want) + int(add is not None)
        freed = lo_done if want else x1_done

        def stat_base(i, b):
            return stats * (nb * i + b)

        block_ctx = ExitStack()
        block = block_ctx.enter_context(nc.Block())

        @block.sync
        def _(sp):
            for b in range(nb):
                sp.sem_inc(stored[b], 16)
            with sp.Fori(0, rounds) as i:
                for b in range(nb):
                    at = ds((nb * i + b) * W, W)
                    sp.wait_ge(freed, nb * i + b + 1)
                    sp.wait_ge(stored[b], 16 * i + 16)
                    sp.dma_start(x[:, b, :, :], x_d[:, :, at].rearrange("k p t -> p k t")).then_inc(x_in[b], 16)
                    if add:
                        sp.dma_start(r[:, b, :, :], add[0][:, :, at].rearrange("k p t -> p k t")).then_inc(r_in[b], 16)
                for b in range(nb):
                    at = ds((nb * i + b) * W, W)
                    if add:
                        sp.wait_ge(x1_done, nb * i + b + 1 + (0 if want else nb))
                        sp.dma_start(add[3][:, :, at].rearrange("k p t -> p k t"), x[:, b, :, :]).then_inc(stored[b], 16)
                    else:
                        sp.sem_inc(stored[b], 16)
            for b in range(nb):
                sp.wait_ge(stored[b], 16 * (rounds + 1))

        @block.gpsimd
        def _(pool):
            pass

        @block.tensor
        def _(pe):
            with pe.Fori(0, rounds) as i:
                for b in range(nb):
                    for n in range(stats):
                        pe.wait_ge(squared, stat_base(i, b) + n + 1)
                        mean_square(pe, core, ms[:, n, 0:W], sq).then_inc(ms_done, 1)

        @block.scalar
        def _(act):
            act.wait_ge(cols, 3 if want or add else 1)
            with act.Fori(0, rounds) as i:
                for b in range(nb):
                    for n in range(stats):
                        src = r if (add and n == 0) else x
                        if src is r:
                            act.wait_ge(r_in[b], 16 * i + 16)
                        elif add:
                            act.wait_ge(x1_done, nb * i + b + 1)
                        else:
                            act.wait_ge(x_in[b], 16 * i + 16)
                        nc.scalar.activation(sq[:, :, :], src[:, b, :, :], ACT.Square).then_inc(squared, 1)
                        act.wait_ge(eps_added, stat_base(i, b) + n + 1)
                        nc.scalar.activation(rs[:, n, :], rs[:, n, :], ACT.Sqrt).then_inc(rooted, 1)
                    if want:
                        act.wait_ge(scaled, nb * i + b + 1)
                        for k in range(KD):
                            last = nc.scalar.activation(t[:, k, :], t[:, k, :], ACT.Identity, bias=col[:, 1, k:k + 1], scale=col[:, 0, k:k + 1])
                        last.then_inc(shifted, 1)
                        act.wait_ge(shifted, nb * i + b + 1)
                        nc.scalar.activation(act_hi[:, :, ds((nb * i + b) * W, W)], t[:, :, :], ACT.Copy).then_inc(hi_done, 1)

        @block.vector
        def _(dve):
            dve.sem_inc(freed, nb)
            vec, mod = core.vec, core.mod
            if want:
                nc.vector.tensor_scalar(col[:, 2, :], mod[:, scale:scale + KD, cond_col], 1.0, None, ALU.add).then_inc(cols, 1)
                dve.wait_ge(cols, 1)
                nc.vector.tensor_tensor(col[:, 0, :], col[:, 2, :], vec[:, norm_w:norm_w + KD], ALU.mult).then_inc(cols, 1)
                nc.vector.tensor_copy(col[:, 1, :], mod[:, shift:shift + KD, cond_col]).then_inc(cols, 1)
                dve.wait_ge(cols, 3)
            else:
                dve.sem_inc(cols, 3)
            if add:
                nc.vector.tensor_tensor(col[:, 2, :], mod[:, add[1]:add[1] + KD, 0], vec[:, add[2]:add[2] + KD], ALU.mult).then_inc(x1_step, 1)
            with dve.Fori(0, rounds) as i:
                for b in range(nb):
                    for n in range(stats):
                        dve.wait_ge(ms_done, stat_base(i, b) + n + 1)
                        nc.vector.tensor_scalar(rs[:, n, :], ms[:, n, 0:W], RMS_EPS, None, ALU.add).then_inc(eps_added, 1)
                        dve.wait_ge(rooted, stat_base(i, b) + n + 1)
                        nc.vector.reciprocal(rs[:, n, :], rs[:, n, :]).then_inc(rs_done, 1)
                        dve.wait_ge(rs_done, stat_base(i, b) + n + 1)
                        rs_all = rs[:, n, :].unsqueeze(1).broadcast_to((P, KD, W))
                        if add and n == 0:
                            dve.wait_ge(x_in[b], 16 * i + 16)
                            nc.vector.tensor_tensor(r[:, b, :, :], r[:, b, :, :], rs_all, ALU.mult).then_inc(x1_step, 1)
                            dve.wait_ge(x1_step, nb * i + b + 2)
                            for k in range(KD):
                                last = nc.vector.scalar_tensor_tensor(x[:, b, k, :], r[:, b, k, :], col[:, 2, k:k + 1], x[:, b, k, :], ALU.mult, ALU.add)
                            last.then_inc(x1_done, 1)
                            if want:
                                dve.wait_ge(x1_done, nb * i + b + 1)
                        else:
                            nc.vector.tensor_tensor(t[:, :, :], x[:, b, :, :], rs_all, ALU.mult).then_inc(scaled, 1)
                    if want:
                        dve.wait_ge(hi_done, nb * i + b + 1)
                        at = ds((nb * i + b) * W, W)
                        nc.vector.tensor_tensor(act_lo[:, :, at], t[:, :, :], act_hi[:, :, at].bitcast(F32), ALU.subtract).then_inc(lo_done, 1)
                        dve.wait_ge(lo_done, nb * i + b + 1 + nb)

        block_ctx.close()
        clear(nc, sems)


def split_phase(nc, core, tag, src, act_hi, act_lo):
    with ExitStack() as ctx:
        sb, ps, sem, sems = scope(nc, ctx, tag)
        raw = sb("raw", [P, 2, SEQ])
        raw_in = [sem(f"raw_in{b}") for b in range(2)]
        hi_done, lo_done = sem("hi_done"), sem("lo_done")
        block_ctx = ExitStack()
        block = block_ctx.enter_context(nc.Block())

        @block.sync
        def _(sp):
            for k in range(KD):
                if k >= 2:
                    sp.wait_ge(lo_done, k - 1)
                sp.dma_start(raw[:, k % 2, :], src[k]).then_inc(raw_in[k % 2], 16)

        @block.scalar
        def _(act):
            for k in range(KD):
                act.wait_ge(raw_in[k % 2], 16 * (k // 2 + 1))
                nc.scalar.activation(act_hi[:, k, :], raw[:, k % 2, :], ACT.Copy).then_inc(hi_done, 1)

        @block.vector
        def _(dve):
            for k in range(KD):
                dve.wait_ge(hi_done, k + 1)
                nc.vector.tensor_tensor(act_lo[:, k, :], raw[:, k % 2, :], act_hi[:, k, :].bitcast(F32), ALU.subtract).then_inc(lo_done, 1)

        block_ctx.close()
        clear(nc, sems)


def product(nc, out, w_hi, w_lo, x_hi, x_lo, first, last):
    nc.tensor.matmul(out, w_hi, x_hi, start=first, stop=False)
    nc.tensor.matmul(out, w_hi, x_lo, start=False, stop=False)
    return nc.tensor.matmul(out, w_lo, x_hi, start=False, stop=last)


def weight_splitter(nc, pool, i, b, count0, zero, w_in, w_raw, w_hi, w_lo, hi_done, w_ready, mm_done):
    pool.wait_ge(w_in[b], 16 * i + 16)
    pool.wait_ge(mm_done, 2 * i + b + 1 + count0)
    nc.gpsimd.tensor_tensor(w_hi[:, b, :, :], w_raw[:, b, :, :], zero, ALU.add).then_inc(hi_done, 1)
    pool.wait_ge(hi_done, 2 * i + b + 1)
    nc.gpsimd.tensor_tensor(w_lo[:, b, :, :], w_raw[:, b, :, :], w_hi[:, b, :, :].bitcast(F32), ALU.subtract).then_inc(w_ready, 1)


def projection_phase(nc, core, tag, w_d, segments, act_hi, act_lo, tokens, rotary=None):
    vec = core.vec
    bank = min(BANK, tokens)
    kinds = [seg[0] for seg in segments]
    per_pair = "ffn" in kinds
    starts = [sum(seg[2] for seg in segments[:n]) for n in range(len(segments))]
    total = sum(seg[2] for seg in segments)
    rounds = total // 2
    with ExitStack() as ctx:
        sb, ps, sem, sems = scope(nc, ctx, tag)
        w_raw = sb("w_raw", [P, 2, KD, P])
        w_hi = sb("w_hi", [P, 2, KD, P], F32R)
        w_lo = sb("w_lo", [P, 2, KD, P], F32R)
        zero = sb("zero", [P, 1])
        zeros = zero[:, :].unsqueeze(1).broadcast_to((P, KD, P))
        q_bias = sb("q_bias", [P, KH]) if "query" in kinds else None
        n_out = 1 if per_pair else 2
        out = sb("out", [P, n_out, tokens])
        work = sb("work", [P, 2 if per_pair else 1, tokens]) if per_pair or "conv" in kinds else None
        acc = ps("acc", [P, 2, max(tokens, BANK)])
        if rotary:
            HALF = tokens // 2
            cos, sin = sb("cos", [P, 2, HALF]), sb("sin", [P, 2, HALF])
            qk, partner = sb("qk", [P, HALF]), sb("partner", [P, HALF])
            ROT_LOADS = 1 + 4
        rot_const, rot_in, rot_step, rot_done, rot_stored = (
            sem(n) for n in ("rot_const", "rot_in", "rot_step", "rot_done", "rot_stored")) if rotary else [None] * 5
        w_in = [sem(f"w_in{b}") for b in range(2)]
        stored = [sem(f"stored{b}") for b in range(n_out)]
        zeroed, q_scaled, hi_done, w_ready, mm_done, evac = (sem(n) for n in ("zeroed", "q_scaled", "hi_done", "w_ready", "mm_done", "evac"))
        act_out, conv_step, conv_done, gelu_done = (sem(n) for n in ("act_out", "conv_step", "conv_done", "gelu_done"))
        block_ctx = ExitStack()
        block = block_ctx.enter_context(nc.Block())

        @block.sync
        def _(sp):
            for s in stored:
                sp.sem_inc(s, 16)
            for b in range(2):
                sp.dma_start(w_raw[:, b, :, :], w_d[segments[0][1] + b]).then_inc(w_in[b], 16)

            def rot_load(i, b):
                sp.wait_ge(rot_stored, 32 * i + (16 * b + 16))
                at = slice(HALF * b, HALF * (b + 1))
                sp.dma_start(qk[:, :], rotary[1][ds(i, 1), :, at].rearrange("a p t -> (a p) t")).then_inc(rot_in, 16)
                for blk in range(4):
                    row = 32 * (blk ^ 1)
                    sp.dma_start(partner[32 * blk:32 * blk + 32, :], rotary[1][ds(i, 1), row:row + 32, at].rearrange("a p t -> (a p) t")
                                 ).then_inc(rot_in, 16)

            def rot_store(i, b):
                sp.wait_ge(rot_done, 2 * i + b + 1)
                sp.dma_start(rotary[0][ds(i, 1), :, HALF * b:HALF * (b + 1)].rearrange("a p t -> (a p) t"), qk[:, :]).then_inc(rot_stored, 16)

            if rotary:
                sp.dma_start(cos[:, :, :], core.d["cos"]).then_inc(rot_const, 16)
                sp.dma_start(sin[:, :, :], core.d["sin"]).then_inc(rot_const, 16)
                sp.sem_inc(rot_stored, 16)

            def chunk(start, kind, out_d, i, b, source):
                c = 2 * i + b + start
                if source is not None:
                    sp.wait_ge(w_ready, c + 1)
                    sp.dma_start(w_raw[:, b, :, :], w_d[ds(source, 1)].rearrange("a p k n -> (a p) k n")).then_inc(w_in[b], 16)
                if kind == "ffn":
                    if b == 0:
                        return
                    sp.wait_ge(conv_done, i + 2)
                    sp.dma_start(out_d[ds(i, 1)].rearrange("a p t -> (a p) t"), out[:, 0, :]).then_inc(stored[0], 16)
                    return
                rotate = rotary and kind == "sigmoid"
                if rotate:
                    rot_load(i, b)
                if kind == "conv":
                    sp.wait_ge(conv_done, 2 * i + b + 2)
                else:
                    sp.wait_ge(evac, c + 3)
                sp.dma_start(out_d[ds(2 * i + b, 1)].rearrange("a p t -> (a p) t"), out[:, b, :]).then_inc(stored[b], 16)
                if rotate:
                    rot_store(i, b)

            for n, (kind, first, count, out_d, _bias) in enumerate(segments):
                if rotary and kind == "sigmoid":
                    for b in range(2):
                        sp.wait_ge(stored[b], 8 * starts[n] + 16)
                if count > 2:
                    with sp.Fori(0, count // 2 - 1) as i:
                        for b in range(2):
                            chunk(starts[n], kind, out_d, i, b, 2 * i + (first + b + 2))
                for b in range(2):
                    nxt = segments[n + 1][1] + b if n + 1 < len(segments) else None
                    chunk(starts[n], kind, out_d, count // 2 - 1, b, nxt)
            for s in stored:
                sp.wait_ge(s, 16 * (rounds + 1))
            if rotary:
                sp.wait_ge(rot_stored, 16 * 17)

        @block.gpsimd
        def _(pool):
            pool.memset(zero[:, :], 0.0).then_inc(zeroed, 1)
            pool.wait_ge(zeroed, 1)
            plain_rounds = starts[kinds.index("sigmoid")] // 2 if rotary else rounds
            with pool.Fori(0, plain_rounds) as i:
                for b in range(2):
                    weight_splitter(nc, pool, i, b, 0, zeros, w_in, w_raw, w_hi, w_lo, hi_done, w_ready, mm_done)
            if rotary:
                pool.wait_ge(rot_const, 32)
                tt = nc.gpsimd.tensor_tensor

                def split(i, b):
                    weight_splitter(nc, pool, i + plain_rounds, b, 0, zeros, w_in, w_raw, w_hi, w_lo, hi_done, w_ready, mm_done)

                def rotate(u, b):
                    pool.wait_ge(rot_in, (16 * ROT_LOADS) * u + 16 * ROT_LOADS)
                    tt(qk[:, :], qk[:, :], cos[:, b, :], ALU.mult).then_inc(rot_step, 1)
                    tt(partner[:, :], partner[:, :], sin[:, b, :], ALU.mult).then_inc(rot_step, 1)
                    pool.wait_ge(rot_step, 2 * u + 2)
                    tt(qk[:, :], qk[:, :], partner[:, :], ALU.add).then_inc(rot_done, 1)

                split(0, 0)
                with pool.Fori(0, rounds - plain_rounds - 1) as i:
                    split(i, 1)
                    rotate(2 * i, 0)
                    split(i + 1, 0)
                    rotate(2 * i + 1, 1)
                last = rounds - plain_rounds - 1
                split(last, 1)
                rotate(2 * last, 0)
                rotate(2 * last + 1, 1)

        @block.tensor
        def _(pe):
            pe.sem_inc(mm_done, 2)
            with pe.Fori(0, rounds) as i:
                for b in range(2):
                    pe.wait_ge(w_ready, 2 * i + b + 1)
                    pe.wait_ge(evac, 2 * i + b + 1)
                    for g in range(tokens // bank):
                        at = slice(bank * g, bank * (g + 1))
                        for k in range(KD):
                            last = product(nc, acc[:, b, at], w_hi[:, b, k, :], w_lo[:, b, k, :],
                                           act_hi[:, k, at], act_lo[:, k, at], k == 0, k == KD - 1)
                    last.then_inc(mm_done, 1)

        @block.scalar
        def _(act):
            if not per_pair:
                act.sem_inc(evac, 2)
            if "query" in kinds:
                act.wait_ge(q_scaled, 1)
            for n, (kind, first, count, out_d, bias) in enumerate(segments):
                with act.Fori(0, count // 2) as i:
                    for b in range(2):
                        m = 2 * i + b
                        act.wait_ge(mm_done, m + starts[n] + 3)
                        if kind in ("bias", "sigmoid", "query", "plain"):
                            act.wait_ge(stored[b], 16 * i + (8 * starts[n] + 16))
                        if kind in ("bias", "sigmoid"):
                            nc.scalar.activation(out[:, b, :], acc[:, b, 0:tokens], ACT.Sigmoid if kind == "sigmoid" else ACT.Identity,
                                                 bias=vec[:, ds(m + bias, 1)]).then_inc(evac, 1)
                        elif kind == "query":
                            nc.scalar.activation(out[:, b, :], acc[:, b, 0:tokens], ACT.Identity, bias=q_bias[:, ds(m, 1)],
                                                 scale=HEAD_DIM ** -0.5).then_inc(evac, 1)
                        elif kind == "plain":
                            nc.scalar.activation(out[:, b, :], acc[:, b, 0:tokens], ACT.Copy).then_inc(evac, 1)
                        elif kind == "conv":
                            act.wait_ge(conv_done, m + 1)
                            nc.scalar.activation(work[:, 0, :], acc[:, b, :], ACT.Identity, bias=vec[:, ds(m + bias, 1)]).then_inc(evac, 1)
                        else:
                            act.wait_ge(conv_done, i + 1)
                            nc.scalar.activation(work[:, b, :], acc[:, b, :], ACT.Identity, bias=vec[:, ds(m + VEC["ff_b"], 1)],
                                                 scale=vec[:, ds(m + VEC["ff_w1"], 1)]).then_inc(act_out, 1)
                            if b == 0:
                                act.wait_ge(evac, m + 3)
                                nc.scalar.activation(work[:, 0, :], work[:, 0, :], ACT.Gelu_apprx_tanh).then_inc(gelu_done, 1)

        @block.vector
        def _(dve):
            if "query" in kinds:
                bias = segments[kinds.index("query")][4]
                nc.vector.tensor_scalar(q_bias[:, :], vec[:, bias:bias + KH], HEAD_DIM ** -0.5, None, ALU.mult).then_inc(q_scaled, 1)
            if "conv" in kinds:
                start, count = starts[kinds.index("conv")], segments[kinds.index("conv")][2]
                dve.sem_inc(conv_done, 1)
                with dve.Fori(0, count // 2) as i:
                    for b in range(2):
                        m = 2 * i + b
                        o, u = out[:, b, :], work[:, 0, :]
                        dve.wait_ge(evac, m + start + 3)
                        dve.wait_ge(stored[b], 16 * i + (8 * start + 16))
                        nc.vector.tensor_scalar(o, u, vec[:, ds(m + VEC["hy_w1"], 1)], vec[:, ds(m + VEC["hy_b"], 1)], ALU.mult, ALU.add
                                                ).then_inc(conv_step, 1)
                        dve.wait_ge(conv_step, 2 * m + 1)
                        nc.vector.scalar_tensor_tensor(o[:, 1:], u[:, :-1], vec[:, ds(m + VEC["hy_w0"], 1)], o[:, 1:], ALU.mult, ALU.add
                                                       ).then_inc(conv_step, 1)
                        dve.wait_ge(conv_step, 2 * m + 2)
                        nc.vector.scalar_tensor_tensor(o[:, :-1], u[:, 1:], vec[:, ds(m + VEC["hy_w2"], 1)], o[:, :-1], ALU.mult, ALU.add
                                                       ).then_inc(conv_done, 1)
            if per_pair:
                dve.sem_inc(evac, 2)
                dve.sem_inc(conv_done, 1)
                with dve.Fori(0, rounds) as i:
                    for b in range(2):
                        c = 2 * i + b
                        o, u = work[:, b, :], acc[:, b, :]
                        dve.wait_ge(act_out, c + 1)
                        nc.vector.scalar_tensor_tensor(o[:, 1:], u[:, :-1], vec[:, ds(c + VEC["ff_w0"], 1)], o[:, 1:], ALU.mult, ALU.add
                                                       ).then_inc(conv_step, 1)
                        dve.wait_ge(conv_step, c + 1)
                        nc.vector.scalar_tensor_tensor(o[:, :-1], u[:, 1:], vec[:, ds(c + VEC["ff_w2"], 1)], o[:, :-1], ALU.mult, ALU.add
                                                       ).then_inc(evac, 1)
                    dve.wait_ge(gelu_done, i + 1)
                    dve.wait_ge(evac, 2 * i + 4)
                    dve.wait_ge(stored[0], 16 * i + 16)
                    nc.vector.tensor_tensor(out[:, 0, :], work[:, 0, :], work[:, 1, :], ALU.mult).then_inc(conv_done, 1)

        block_ctx.close()
        clear(nc, sems)


def attention_phase(nc, core):
    d = core.d
    PAIRS = ROWS // 2
    BLOCKS = PAIRS // 2
    NB = (WIN_ROWS + 1) * GRID_W
    EDGE = WIN_ROWS * GRID_W
    CX = CTX_LEN
    CXT = CX // P
    TAB = 14 * GRID_W
    TILES = SEQ // P
    E_BUFS = 4
    UNITS = 2 * PAIRS

    def window(p):
        if p < 2:
            return EDGE, 0, (6 - 2 * p) * GRID_W
        if p >= PAIRS - 2:
            return EDGE, ROWS - WIN_ROWS, (2 - 2 * (p - PAIRS + 2)) * GRID_W
        return NB, 2 * p - WIN_ROWS // 2, None

    def slots(m):
        if m in (0, BLOCKS - 1):
            row = window(2 * m)[1]
            nb = [(3 + i, row // 2 + i) for i in range(4)]
        else:
            nb = [(2 + i, 2 * m - 2 + i) for i in range(6)]
        return [(0, TILES), (1, TILES + 1)] + nb

    with ExitStack() as ctx:
        sb, ps, sem, sems = scope(nc, ctx, "att")
        colmask = sb("colmask", [P, GRID_W])
        fold = sb("fold", [P, HEAD_DIM])
        zero = sb("zero", [P, 1])
        q, qr, k = (sb(n, [P, SEQ]) for n in ("q", "qr", "k"))
        kx = sb("kx", [P, CX])
        v, vx = sb("v", [P, SEQ]), sb("vx", [P, CX])
        q_rot, q_plain = sb("q_rot", [P, 2, SEQ], F32R), sb("q_plain", [P, 2, SEQ], F32R)
        k_hh, k_ll = sb("k_hh", [P, 2, SEQ], F32R), sb("k_ll", [P, 2, SEQ], F32R)
        kx_hh, kx_ll = sb("kx_hh", [P, 2, CX], F32R), sb("kx_ll", [P, 2, CX], F32R)
        table = sb("table", [P, 2, TAB])
        inner = sb("inner", [P, 2, CX + NB])
        vt = sb("vt", [P, TILES + CXT, 2, 2, HEAD_DIM], F32R)
        e = sb("e", [P, E_BUFS, 7 * P])
        pt_hi, pt_lo = sb("pt_hi", [P, 2, 8, 2 * P], F32R), sb("pt_lo", [P, 2, 8, 2 * P], F32R)
        stat = sb("stat", [P, E_BUFS, 8])
        o_sb = sb("o_sb", [P, 2 * P])
        y = sb("y", [HEAD_DIM, 2, 2 * P])
        s_ps = ps("s_ps", [P, 2, 2 * BANK])
        t_ps = ps("t_ps", [P, 2, BANK])
        o_ps = ps("o_ps", [P, BANK])
        y_ps = ps("y_ps", [P, BANK])

        const_in, loaded, v_in, zeroed = sem("const_in"), sem("loaded"), sem("v_in"), sem("zeroed")
        step, prepared, raw_used, head_done = sem("step"), sem("prepared"), sem("raw_used"), sem("head_done")
        v_flip, v_hi, v_lo, inner_ready = sem("v_flip"), sem("v_hi"), sem("v_lo"), sem("inner_ready")
        scores, row_max, logits, neg_max, exp_done, sums, inverse, normed = (
            sem(n) for n in ("scores", "row_max", "logits", "neg_max", "exp_done", "sums", "inverse", "normed"))
        flip_a, flip_b, hi_a, hi_b, lo_a, lo_b = (sem(n) for n in ("flip_a", "flip_b", "hi_a", "hi_b", "lo_a", "lo_b"))
        pv, o_out, y_mm, y_out = sem("pv"), sem("o_out"), sem("y_mm"), sem("y_out")
        stored = [sem(f"stored{b}") for b in range(2)]
        LOADS = 4 * 2 + 1
        V_GROUPS = -(-(TILES + CXT) // 4)
        STEPS_P = 7
        block_ctx = ExitStack()
        block = block_ctx.enter_context(nc.Block())

        def head(j, hb):
            return 2 * j + hb

        def tile_groups():
            return [(g, 4 * g, min(4, TILES + CXT - 4 * g)) for g in range(V_GROUPS)]

        def v_bank(g):
            return s_ps[:, g % 4 // 2, ds(BANK * (g % 2), BANK)]

        @block.sync
        def _(sp):
            sp.dma_start(colmask[:, :], d["colmask"]).then_inc(const_in, 16)
            sp.dma_start(fold[:, :], d["fold"]).then_inc(const_in, 16)
            with sp.Fori(0, N_HEADS // 2) as j:
                for hb in range(2):
                    if hb == 0:
                        sp.wait_ge(v_flip, V_GROUPS * j + 1)
                        sp.dma_start(v[:, :], d["proj"][ds(j + V0, 1)].rearrange("a p t -> (a p) t")).then_inc(v_in, 16)
                        sp.dma_start(vx[:, :], d["ctx_kv"][ds(j + KH, 1)].rearrange("a p t -> (a p) t")).then_inc(v_in, 16)
                    sp.wait_ge(raw_used, head(j, hb) + 1)
                    for half in range(2):
                        at = 64 * half
                        for dst, src, c in ((q, "proj", Q0), (qr, "rotated", Q0), (k, "rotated", K0)):
                            sp.dma_start(dst[at:at + 64, :], d[src][ds(j + c, 1), 64 * hb:64 * hb + 64, :].rearrange("a p t -> (a p) t")
                                         ).then_inc(loaded, 16)
                        sp.dma_start(kx[at:at + 64, :], d["ctx_kv"][ds(j, 1), 64 * hb:64 * hb + 64, :].rearrange("a p t -> (a p) t")
                                     ).then_inc(loaded, 16)
                    sp.wait_ge(head_done, head(j, hb) + 1)
                    sp.dma_start(table[:, hb, :], d["rpb"][ds(2 * j + hb, 1)].rearrange("h p t -> (h p) t")).then_inc(loaded, 16)
            for b in range(2):
                sp.wait_ge(stored[b], 16 * (N_HEADS * BLOCKS // 2 + 1))

        @block.gpsimd
        def _(pool):
            nc.gpsimd.memset(zero[:, :], 0.0).then_inc(zeroed, 1)
            nc.gpsimd.memset(inner[:, :, 0:CX], 0.0).then_inc(zeroed, 1)
            nc.gpsimd.memset(e[:, :, CX + NB:7 * P], 0.0).then_inc(zeroed, 1)
            for pt in (pt_hi, pt_lo):
                nc.gpsimd.memset(pt[:, :, 7, 0:P].bitcast(F32), 0.0).then_inc(zeroed, 1)
                nc.gpsimd.memset(pt[:, :, 2, P:2 * P].bitcast(F32), 0.0).then_inc(zeroed, 1)
            pool.sem_inc(raw_used, 1)
            pool.wait_ge(const_in, 32)
            pool.wait_ge(zeroed, 7)
            tt = nc.gpsimd.tensor_tensor
            wide = zero[:, :].broadcast_to((P, SEQ))
            mask = colmask[:, :].unsqueeze(1).broadcast_to((P, TAB // GRID_W, GRID_W))
            low = slice(64, 128)
            with pool.Fori(0, N_HEADS // 2) as j:
                for hb in range(2):
                    base = STEPS_P * head(j, hb)
                    pool.wait_ge(head_done, head(j, hb) + 1)
                    pool.wait_ge(loaded, (16 * LOADS) * head(j, hb) + 16 * LOADS)
                    tab = table[:, hb, :].rearrange("p (r c) -> p r c", c=GRID_W)
                    tt(tab, tab, mask, ALU.add).then_inc(step, 1)
                    for hi, raw in ((kx_hh, kx), (q_plain, q), (q_rot, qr), (k_hh, k)):
                        tt(hi[:, hb, :], raw[:, :], wide[:, 0:raw.shape[1]], ALU.add).then_inc(step, 1)
                    pool.wait_ge(step, base + 5)
                    tt(kx_ll[:, hb, :], kx[:, :], kx_hh[:, hb, :].bitcast(F32), ALU.subtract).then_inc(step, 1)
                    tt(k_ll[:, hb, :], k[:, :], k_hh[:, hb, :].bitcast(F32), ALU.subtract).then_inc(step, 1)
                    pool.wait_ge(step, base + 7)
                    tt(q_plain[low, hb, :], q[low, :], q_plain[low, hb, :].bitcast(F32), ALU.subtract)
                    tt(q_rot[low, hb, :], qr[low, :], q_rot[low, hb, :].bitcast(F32), ALU.subtract).then_inc(prepared, 1)
                    pool.wait_ge(prepared, head(j, hb) + 1)
                    pool.sem_inc(raw_used, 1)

        @block.tensor
        def _(pe):
            def score(j, u):
                hb, s = divmod(u, PAIRS)
                nk, row, _ = window(s)
                if u >= 2:
                    pe.wait_ge(exp_done, UNITS * j + u - 1)
                out, at = s_ps[:, u % 2, :], ds(P * s, P)
                nc.tensor.matmul(out[:, 0:CX], q_plain[:, hb, at], kx_hh[:, hb, :], start=True, stop=False)
                nc.tensor.matmul(out[:, 0:CX], q_plain[:, hb, at], kx_ll[:, hb, :], start=False, stop=True)
                for lo, n in ((0, CX), (CX, nk - CX)):
                    keys, to = ds(GRID_W * row + lo, n), out[:, CX + lo:CX + lo + n]
                    nc.tensor.matmul(to, q_rot[:, hb, at], k_hh[:, hb, keys], start=True, stop=False)
                    last = nc.tensor.matmul(to, q_rot[:, hb, at], k_ll[:, hb, keys], start=False, stop=True)
                last.then_inc(scores, 1)

            def flip(j, u):
                nk = window(u % PAIRS)[0]
                pe.wait_ge(normed, UNITS * j + u + 1)
                if u >= 1:
                    pe.wait_ge(lo_a, UNITS * j + u)
                for t in range(4):
                    last = nc.tensor.transpose(t_ps[:, 0, ds(P * t, P)], e[:, u % E_BUFS, ds(P * t, P)], core.ident[:, :])
                last.then_inc(flip_a, 1)
                if u >= 1:
                    pe.wait_ge(lo_b, UNITS * j + u)
                for t in range(4, 7 if nk == NB else 6):
                    last = nc.tensor.transpose(t_ps[:, 1, ds(P * (t - 4), P)], e[:, u % E_BUFS, ds(P * t, P)], core.ident[:, :])
                last.then_inc(flip_b, 1)

            def values(j, m):
                pe.wait_ge(lo_a, UNITS * j + 2 * m + 2)
                pe.wait_ge(lo_b, UNITS * j + 2 * m + 2)
                if m >= 1:
                    pe.wait_ge(o_out, (2 * BLOCKS) * j + m)
                hb, todo = m // BLOCKS, slots(m % BLOCKS)
                for n, (slot, tile) in enumerate(todo):
                    w = vt[:, tile, hb, :, :].rearrange("p a c -> p (a c)")
                    nc.tensor.matmul(o_ps[:, 0:2 * P], w, pt_hi[:, m % 2, slot, :], start=(n == 0), stop=False)
                    last = nc.tensor.matmul(o_ps[:, 0:2 * P], w, pt_lo[:, m % 2, slot, :], start=False, stop=(n == len(todo) - 1))
                last.then_inc(pv, 1)

            def fold_halves(j, m):
                pe.wait_ge(o_out, (2 * BLOCKS) * j + m + 1)
                if m >= 1:
                    pe.wait_ge(y_out, (2 * BLOCKS) * j + m)
                nc.tensor.matmul(y_ps[0:HEAD_DIM, 0:2 * P], fold[:, :], o_sb[:, :], start=True, stop=True).then_inc(y_mm, 1)

            pe.sem_inc(v_flip, 1)
            pe.wait_ge(const_in, 32)
            pe.wait_ge(zeroed, 7)
            with pe.Fori(0, N_HEADS // 2) as j:
                pe.wait_ge(v_in, 32 * j + 32)
                for g, first, n in tile_groups():
                    if g >= 4:
                        pe.wait_ge(v_lo, V_GROUPS * j + g - 3)
                    for t in range(first, first + n):
                        src = v[:, ds(P * t, P)] if t < TILES else vx[:, ds(P * (t - TILES), P)]
                        last = nc.tensor.transpose(v_bank(g)[:, ds(P * (t - first), P)], src, core.ident[:, :])
                    last.then_inc(v_flip, 1)
                pe.wait_ge(v_lo, V_GROUPS * j + V_GROUPS)
                for t in range(UNITS + 4):
                    if t in (0, PAIRS):
                        pe.wait_ge(prepared, head(j, t // PAIRS) + 1)
                    if t < UNITS:
                        score(j, t)
                    if 2 <= t < UNITS + 2:
                        flip(j, t - 2)
                    if t >= 4 and t % 2 == 0:
                        values(j, (t - 4) // 2)
                    if t >= 5 and t % 2:
                        fold_halves(j, (t - 5) // 2)

        def dest(pt, m, a, nk, bank):
            cols = slice(P * a, P * a + P)
            buf = pt[:, m % 2, :, :]
            if nk == NB and a == 0:
                return buf[:, 0:4, cols] if bank == 0 else buf[:, 4:7, cols]
            if bank == 0:
                return buf[:, 0:6, cols].rearrange("p (x c) q -> p x c q", c=3)[:, :, 0:2, :]
            return buf[:, 5:8, cols] if nk == NB else buf[:, 5:7, cols]

        def source(nk, a, bank):
            if bank == 0:
                t = t_ps[:, 0, :].rearrange("p (c q) -> p c q", q=P)
                return t if nk == NB and a == 0 else t_ps[:, 0, :].rearrange("p (x c q) -> p x c q", c=2, q=P)
            n = 3 if nk == NB else 2
            return t_ps[:, 1, 0:n * P].rearrange("p (c q) -> p c q", q=P)

        @block.scalar
        def _(act):
            def hi(j, u, bank):
                m, a = divmod(u, 2)
                nk = window(u % PAIRS)[0]
                if bank == 0 and a == 0 and m >= 2:
                    act.wait_ge(pv, (2 * BLOCKS) * j + m - 1)
                act.wait_ge((flip_a, flip_b)[bank], UNITS * j + u + 1)
                nc.scalar.activation(dest(pt_hi, m, a, nk, bank), source(nk, a, bank), ACT.Copy).then_inc((hi_a, hi_b)[bank], 1)

            def exps(j, u):
                nk, _, col = window(u % PAIRS)
                st, ee, b = stat[:, u % E_BUFS, :], e[:, u % E_BUFS, :], u % 2
                act.wait_ge(neg_max, UNITS * j + u + 1)
                if col is None:
                    nc.scalar.activation(ee[:, 0:CX + nk], ee[:, 0:CX + nk], ACT.Exp, bias=st[:, 2:3], accum_out=st[:, 5:6]).then_inc(exp_done, 1)
                else:
                    nc.scalar.activation(ee[:, 0:CX], s_ps[:, b, 0:CX], ACT.Exp, bias=st[:, 2:3], accum_out=st[:, 3:4])
                    nc.scalar.activation(ee[:, CX:CX + nk], ee[:, CX:CX + nk], ACT.Exp, bias=st[:, 2:3], accum_out=st[:, 4:5]).then_inc(exp_done, 1)

            act.sem_inc(head_done, 2)
            for b in range(2):
                act.sem_inc(stored[b], 16)
            with act.Fori(0, N_HEADS // 2) as j:
                for g, first, n in tile_groups():
                    act.wait_ge(v_flip, V_GROUPS * j + g + 2)
                    act_in = v_bank(g)[:, 0:P * n].rearrange("p (t h c) -> p t h c", h=2, c=HEAD_DIM)
                    nc.scalar.activation(vt[:, first:first + n, :, 0, :], act_in, ACT.Copy).then_inc(v_hi, 1)
                for t in range(UNITS + 4):
                    if 2 <= t < UNITS + 2:
                        hi(j, t - 2, 0)
                        hi(j, t - 2, 1)
                    if t < UNITS:
                        exps(j, t)
                    if t % PAIRS == PAIRS - 1 and t < UNITS:
                        act.sem_inc(head_done, 1)
                    if t >= 4 and t % 2 == 0:
                        act.wait_ge(pv, (2 * BLOCKS) * j + (t - 4) // 2 + 1)
                        nc.scalar.activation(o_sb[:, :], o_ps[:, 0:2 * P], ACT.Copy).then_inc(o_out, 1)
                    if t >= 5 and t % 2:
                        m = (t - 5) // 2
                        act.wait_ge(y_mm, (2 * BLOCKS) * j + m + 1)
                        act.wait_ge(stored[m % 2], (16 * BLOCKS) * j + 16 * (m // 2) + 16)
                        nc.scalar.activation(y[:, m % 2, :], y_ps[0:HEAD_DIM, 0:2 * P], ACT.Copy).then_inc(y_out, 1)
                        act.wait_ge(y_out, (2 * BLOCKS) * j + m + 1)
                        hb, at = 64 * (m // BLOCKS), 2 * P * (m % BLOCKS)
                        act.dma_start(d["branches"][ds(j, 1), hb:hb + 64, at:at + 2 * P].rearrange("a p t -> (a p) t"), y[:, m % 2, :]
                                      ).then_inc(stored[m % 2], 16)

        @block.vector
        def _(dve):
            def edge(j, u):
                hb, s = divmod(u, PAIRS)
                return 8 * j + 4 * hb + (s if s < 2 else s - PAIRS + 4) + 1

            def logit(j, u):
                hb, s = divmod(u, PAIRS)
                nk, _, col = window(s)
                st, ee, b = stat[:, u % E_BUFS, :], e[:, u % E_BUFS, :], u % 2
                dve.wait_ge(scores, UNITS * j + u + 1)
                if u >= E_BUFS:
                    dve.wait_ge(flip_b, UNITS * j + u - E_BUFS + 1)
                if col is None:
                    nc.vector.memset(st[:, 7:8], 0.0)
                    nc.vector.tensor_tensor_reduce(out=ee[:, 0:CX + nk], in0=s_ps[:, b, 0:CX + nk], in1=inner[:, hb, :], scale=1.0,
                                                   scalar=MASKED, op0=ALU.add, op1=ALU.max, accum_out=st[:, 1:2]).then_inc(logits, 1)
                    dve.wait_ge(logits, UNITS * j + u + 1)
                    nc.vector.tensor_scalar(st[:, 2:3], st[:, 1:2], -1.0, None, ALU.mult).then_inc(neg_max, 1)
                else:
                    nc.vector.reduce_max(st[:, 0:1], s_ps[:, b, 0:CX], AX.X).then_inc(row_max, 1)
                    nc.vector.tensor_tensor_reduce(out=ee[:, CX:CX + nk], in0=s_ps[:, b, CX:CX + nk], in1=table[:, hb, ds(col, nk)], scale=1.0,
                                                   scalar=MASKED, op0=ALU.add, op1=ALU.max, accum_out=st[:, 1:2]).then_inc(logits, 1)
                    dve.wait_ge(row_max, edge(j, u))
                    dve.wait_ge(logits, UNITS * j + u + 1)
                    nc.vector.tensor_scalar(st[:, 2:3], st[:, 1:2], st[:, 0:1], -1.0, ALU.max, ALU.mult).then_inc(neg_max, 1)

            def normalise(j, u):
                nk, _, col = window(u % PAIRS)
                st, ee = stat[:, u % E_BUFS, :], e[:, u % E_BUFS, :]
                dve.wait_ge(exp_done, UNITS * j + u + 1)
                if col is not None:
                    nc.vector.tensor_tensor(st[:, 5:6], st[:, 3:4], st[:, 4:5], ALU.add).then_inc(sums, 1)
                    dve.wait_ge(sums, edge(j, u))
                nc.vector.reciprocal(st[:, 6:7], st[:, 5:6]).then_inc(inverse, 1)
                dve.wait_ge(inverse, UNITS * j + u + 1)
                nc.vector.tensor_scalar(ee[:, 0:CX + nk], ee[:, 0:CX + nk], st[:, 6:7], None, ALU.mult).then_inc(normed, 1)

            def lo(j, u, bank):
                m, a = divmod(u, 2)
                nk = window(u % PAIRS)[0]
                dve.wait_ge((hi_a, hi_b)[bank], UNITS * j + u + 1)
                nc.vector.tensor_tensor(dest(pt_lo, m, a, nk, bank), source(nk, a, bank), dest(pt_hi, m, a, nk, bank).bitcast(F32), ALU.subtract
                                        ).then_inc((lo_a, lo_b)[bank], 1)

            dve.wait_ge(zeroed, 7)
            with dve.Fori(0, N_HEADS // 2) as j:
                for g, first, n in tile_groups():
                    dve.wait_ge(v_hi, V_GROUPS * j + g + 1)
                    nc.vector.tensor_tensor(vt[:, first:first + n, :, 1, :], v_bank(g)[:, 0:P * n].rearrange("p (t h c) -> p t h c", h=2, c=HEAD_DIM),
                                            vt[:, first:first + n, :, 0, :].bitcast(F32), ALU.subtract).then_inc(v_lo, 1)
                for t in range(UNITS + 2):
                    if t % PAIRS == 0 and t < UNITS:
                        hb = t // PAIRS
                        dve.wait_ge(prepared, head(j, hb) + 1)
                        nc.vector.tensor_copy(inner[:, hb, CX:CX + NB], table[:, hb, 2 * GRID_W:2 * GRID_W + NB]).then_inc(inner_ready, 1)
                        dve.wait_ge(inner_ready, 3 * head(j, hb) + 1)
                        nc.vector.memset(inner[0:64, hb, CX + NB - GRID_W:CX + NB], MASKED).then_inc(inner_ready, 1)
                        nc.vector.memset(inner[64:128, hb, CX:CX + GRID_W], MASKED).then_inc(inner_ready, 1)
                        dve.wait_ge(inner_ready, 3 * head(j, hb) + 3)
                    if t < UNITS:
                        logit(j, t)
                    if t >= 2:
                        lo(j, t - 2, 0)
                    if 1 <= t < UNITS + 1:
                        normalise(j, t - 1)
                    if t >= 2:
                        lo(j, t - 2, 1)

        block_ctx.close()
        clear(nc, sems)


def hyena_phase(nc, core):
    d = core.d
    with ExitStack() as ctx:
        sb, ps, sem, sems = scope(nc, ctx, "hy")
        x1 = sb("x1", [P, KH, SEQ])
        vv = sb("vv", [P, KH, SEQ])
        dft = sb("dft", [P, 2, P])
        idft = sb("idft", [P, R])
        ua = sb("ua", [P, 2, KH, P])
        ut = sb("ut", [P, 2, D_HYENA])
        spec = sb("spec", [P, 2, 2, D_HYENA])
        const_in, u_in, u_ready, skip_done = sem("const_in"), sem("u_in"), sem("u_ready"), sem("skip_done")
        ua_ready, flip, ut_ready, s1_mm, s1_out = (sem(n) for n in ("ua_ready", "flip", "ut_ready", "s1_mm", "s1_out"))
        s1_stored = [sem(f"s1_stored{b}") for b in range(2)]
        with ExitStack() as inner_ctx:
            ps1 = inner_ctx.enter_context(nc.psum_tensor("hy_flip_ps", [P, 2, BANK], F32))
            ps2 = inner_ctx.enter_context(nc.psum_tensor("hy_s1_ps", [P, 2, 2, BANK], F32))
            block_ctx = ExitStack()
            block = block_ctx.enter_context(nc.Block())
            TILES = R // 4

            @block.sync
            def _(sp):
                sp.dma_start(dft[:, :, :], d["dft_u"]).then_inc(const_in, 16)
                sp.dma_start(idft[:, :], d["idft"]).then_inc(const_in, 16)
                for q in range(KH):
                    sp.dma_start(x1[:, q, :], d["proj"][HY0 + KH + q]).then_inc(u_in, 16)
                    sp.dma_start(vv[:, q, :], d["proj"][HY0 + 2 * KH + q]).then_inc(u_in, 16)
                for b in range(2):
                    sp.sem_inc(s1_stored[b], 16)
                with sp.Fori(0, TILES // 2) as i:
                    for b in range(2):
                        sp.wait_ge(s1_out, 2 * i + b + 1)
                        for h in range(2):
                            sp.dma_start(d["spec_u"][ds(8 * i + 4 * b + 2 * h, 2)].rearrange("g r c -> (g r) c"),
                                         spec[:, b, h, :]).then_inc(s1_stored[b], 16)
                for b in range(2):
                    sp.wait_ge(s1_stored[b], 16 + 32 * (TILES // 2))

            @block.vector
            def _(dve):
                dve.wait_ge(u_in, 32 * KH)
                nc.vector.tensor_tensor(vv[:, :, :], x1[:, :, :], vv[:, :, :], ALU.mult).then_inc(u_ready, 1)
                dve.wait_ge(u_ready, 1)
                tokens = vv[:, :, :].rearrange("p q (a b) -> p q b a", b=R)
                dve.sem_inc(flip, 2)
                with dve.Fori(0, TILES // 2) as i:
                    for b in range(2):
                        dve.wait_ge(flip, 2 * i + b + 1)
                        for q in range(KH):
                            last = nc.vector.tensor_copy(ua[:, b, q, :].rearrange("p (g a) -> p g a", g=4),
                                                         tokens[:, q, ds(8 * i + 4 * b, 4), :])
                        last.then_inc(ua_ready, 1)
                for q in range(KH):
                    last = nc.vector.tensor_scalar(x1[:, q, :], vv[:, q, :], core.vec[:, VEC["skip"] + q:VEC["skip"] + q + 1], None, ALU.mult)
                last.then_inc(skip_done, 1)
                dve.wait_ge(skip_done, 1)

            @block.tensor
            def _(pe):
                pe.wait_ge(const_in, 32)
                with pe.Fori(0, TILES // 2) as i:
                    for b in range(2):
                        pe.wait_ge(ua_ready, 2 * i + b + 1)
                        for q in range(KH):
                            last = nc.tensor.transpose(ps1[:, b, ds(P * q, P)], ua[:, b, q, :], core.ident[:, :])
                        last.then_inc(flip, 1)
                    for b in range(2):
                        pe.wait_ge(ut_ready, 2 * i + b + 1)
                        for h in range(2):
                            last = nc.tensor.matmul(ps2[:, b, h, :], dft[:, h, :], ut[:, b, :], start=True, stop=True)
                        last.then_inc(s1_mm, 1)

            @block.scalar
            def _(act):
                with act.Fori(0, TILES // 2) as i:
                    for b in range(2):
                        act.wait_ge(flip, 2 * i + b + 3)
                        nc.scalar.activation(ut[:, b, :], ps1[:, b, :], ACT.Copy).then_inc(ut_ready, 1)
                    for b in range(2):
                        act.wait_ge(s1_mm, 2 * i + b + 1)
                        act.wait_ge(s1_stored[b], 32 * i + 16)
                        nc.scalar.activation(spec[:, b, :, :], ps2[:, b, :, :], ACT.Copy).then_inc(s1_out, 1)

            block_ctx.close()

        G = R // 2
        NB = 4
        ROUNDS = G // NB
        with ExitStack() as inner_ctx:
            isb = lambda n, s: inner_ctx.enter_context(nc.sbuf_tensor(f"hy_{n}", s, F32))
            tw = isb("tw", [P, NB, 5, P])
            au, ak = isb("au", [P, NB, D_HYENA]), isb("ak", [P, NB, D_HYENA])
            ka, kb = isb("ka", [P, 2, D_HYENA]), isb("kb", [P, 2, D_HYENA])
            prod = isb("prod", [P, 2, 2, D_HYENA])
            yy = isb("yy", [P, 2, D_HYENA])
            bo = isb("bo", [P, 2, D_HYENA])
            psg = inner_ctx.enter_context(nc.psum_tensor("hy_g_ps", [P, 2, 4, BANK], F32))
            g_in = [sem(f"g_in{b}") for b in range(NB)]
            b_stored = [sem(f"b_stored{b}") for b in range(2)]
            fwd_k, fwd_u, k_out, prods, y_ready, inv, b_out = (sem(n) for n in ("fwd_k", "fwd_u", "k_out", "prods", "y_ready", "inv", "b_out"))
            block_ctx = ExitStack()
            block = block_ctx.enter_context(nc.Block())
            FWD_LOADS = 5

            def staggered(engine, first, second):
                first(0, 0)
                with engine.Fori(0, ROUNDS - 1) as i:
                    for b in range(NB):
                        first(i + (b + 1) // NB, (b + 1) % NB)
                        second(i, b)
                for b in range(NB):
                    if b + 1 < NB:
                        first(ROUNDS - 1, b + 1)
                    second(ROUNDS - 1, b)

            @block.sync
            def _(sp):
                with sp.Fori(0, ROUNDS) as i:
                    for b in range(NB):
                        g = NB * i + b
                        sp.wait_ge(inv, g + 1)
                        sp.dma_start(tw[:, b, :, :], d["twiddle"][ds(g, 1)].rearrange("a p m n -> (a p) m n")).then_inc(g_in[b], 16)
                        for dst, src in ((ak, "spec_k"), (au, "spec_u")):
                            for c in range(2):
                                sp.dma_start(dst[64 * c:64 * c + 64, b, :], d[src][:, ds(2 * g + c, 1), :].rearrange("n a c -> n (a c)")
                                             ).then_inc(g_in[b], 16)

            @block.tensor
            def _(pe):
                def forward(i, b):
                    g = NB * i + b
                    pe.wait_ge(g_in[b], (16 * FWD_LOADS) * i + 16 * FWD_LOADS)
                    pe.wait_ge(k_out, g + 1)
                    nc.tensor.matmul(psg[:, b % 2, 2, :], tw[:, b, 2, :], ak[:, b, :], start=True, stop=True)
                    nc.tensor.matmul(psg[:, b % 2, 3, :], tw[:, b, 3, :], ak[:, b, :], start=True, stop=True).then_inc(fwd_k, 1)
                    pe.wait_ge(prods, g + 1)
                    nc.tensor.matmul(psg[:, b % 2, 1, :], tw[:, b, 1, :], au[:, b, :], start=True, stop=True)
                    pe.wait_ge(b_out, g + 1)
                    nc.tensor.matmul(psg[:, b % 2, 0, :], tw[:, b, 0, :], au[:, b, :], start=True, stop=True).then_inc(fwd_u, 1)

                def inverse(i, b):
                    pe.wait_ge(y_ready, NB * i + b + 1)
                    nc.tensor.matmul(psg[:, b % 2, 0, :], tw[:, b, 4, :], yy[:, b % 2, :], start=True, stop=True).then_inc(inv, 1)

                pe.sem_inc(inv, NB)
                staggered(pe, forward, inverse)

            @block.scalar
            def _(act):
                def copy_k(i, b):
                    act.wait_ge(fwd_k, NB * i + b + 1)
                    nc.scalar.activation(ka[:, b % 2, :], psg[:, b % 2, 2, :], ACT.Copy)
                    nc.scalar.activation(kb[:, b % 2, :], psg[:, b % 2, 3, :], ACT.Copy).then_inc(k_out, 1)

                def store(i, b):
                    g = NB * i + b
                    act.wait_ge(inv, g + NB + 1)
                    act.wait_ge(b_stored[b % 2], (16 * NB) * i + 32 * (b // 2) + 16)
                    nc.scalar.activation(bo[:, b % 2, :], psg[:, b % 2, 0, :], ACT.Copy).then_inc(b_out, 1)
                    act.wait_ge(b_out, g + 3)
                    for c in range(2):
                        act.dma_start(d["spec_y"][:, ds(2 * g + c, 1), :].rearrange("n a c -> n (a c)"),
                                      bo[64 * c:64 * c + 64, b % 2, :]).then_inc(b_stored[b % 2], 16)

                act.sem_inc(k_out, 2)
                act.sem_inc(b_out, 2)
                for b in range(2):
                    act.sem_inc(b_stored[b], 16)
                staggered(act, copy_k, store)
                for b in range(2):
                    act.wait_ge(b_stored[b], 16 + 16 * G)

            @block.vector
            def _(dve):
                dve.sem_inc(prods, 2)
                with dve.Fori(0, G // 2) as i:
                    for b in range(2):
                        dve.wait_ge(k_out, 2 * i + b + 3)
                        dve.wait_ge(fwd_u, 2 * i + b + 1)
                        nc.vector.tensor_tensor(prod[:, b, 1, :], psg[:, b, 1, :], kb[:, b, :], ALU.mult)
                        nc.vector.tensor_tensor(prod[:, b, 0, :], psg[:, b, 0, :], ka[:, b, :], ALU.mult).then_inc(prods, 1)

            @block.gpsimd
            def _(pool):
                with pool.Fori(0, G // 2) as i:
                    for b in range(2):
                        pool.wait_ge(prods, 2 * i + b + 3)
                        nc.gpsimd.tensor_tensor(yy[:, b, :], prod[:, b, 0, :], prod[:, b, 1, :], ALU.add).then_inc(y_ready, 1)

            block_ctx.close()

        with ExitStack() as inner_ctx:
            bt = inner_ctx.enter_context(nc.sbuf_tensor("hy_bt", [P, 2, 8, D_HYENA], F32))
            x0 = inner_ctx.enter_context(nc.sbuf_tensor("hy_x0", [P, KH, SEQ], F32))
            psy = inner_ctx.enter_context(nc.psum_tensor("hy_y_ps", [P, 2, KH, BANK], F32))
            bt_in = [sem(f"bt_in{b}") for b in range(2)]
            x0_in, y_mm, y_sum, y_done, y_stored = (sem(n) for n in ("x0_in", "y_mm", "y_sum", "y_done", "y_stored"))
            block_ctx = ExitStack()
            block = block_ctx.enter_context(nc.Block())
            TG = R // 16

            @block.sync
            def _(sp):
                sp.sem_inc(y_mm, 2)
                with sp.Fori(0, TG // 2) as i:
                    for b in range(2):
                        sp.wait_ge(y_mm, 2 * i + b + 1)
                        sp.dma_start(bt[:, b, :, :], d["spec_y"][ds(32 * i + 16 * b, 16)].rearrange("(t g) r c -> (g r) t c", g=2)
                                     ).then_inc(bt_in[b], 16)
                for q in range(KH):
                    sp.wait_ge(y_done, q + 1)
                    sp.dma_start(d["branches"][KH + q], x1[:, q, :]).then_inc(y_stored, 16)
                sp.wait_ge(y_stored, 16 * KH)

            @block.scalar
            def _(act):
                for q in range(KH):
                    act.dma_start(x0[:, q, :], d["proj"][HY0 + q]).then_inc(x0_in, 16)

            @block.tensor
            def _(pe):
                pe.wait_ge(const_in, 32)
                with pe.Fori(0, TG // 2) as i:
                    for b in range(2):
                        pe.wait_ge(bt_in[b], 16 * i + 16)
                        pe.wait_ge(y_sum, 2 * i + b + 1)
                        for t in range(8):
                            for q in range(KH):
                                last = nc.tensor.matmul(psy[:, b, q, ds(R * t, R)], bt[:, b, t, ds(P * q, P)], idft[:, :], start=True, stop=True)
                        last.then_inc(y_mm, 1)

            @block.vector
            def _(dve):
                dve.sem_inc(y_sum, 2)
                tokens = x1[:, :, :].rearrange("p q (a b) -> p q b a", b=R)
                with dve.Fori(0, TG // 2) as i:
                    for b in range(2):
                        dve.wait_ge(y_mm, 2 * i + b + 3)
                        for q in range(KH):
                            at = tokens[:, q, ds(32 * i + 16 * b, 16), :]
                            last = nc.vector.scalar_tensor_tensor(at, psy[:, b, q, :].rearrange("p (n a) -> p n a", a=SEQ // R),
                                                                  core.rnorm[:, q:q + 1], at, ALU.mult, ALU.add)
                        last.then_inc(y_sum, 1)
                dve.wait_ge(y_sum, TG + 2)
                dve.wait_ge(x0_in, 16 * KH)
                for q in range(KH):
                    nc.vector.tensor_tensor(x1[:, q, :], x1[:, q, :], x0[:, q, :], ALU.mult).then_inc(y_done, 1)

            block_ctx.close()
        clear(nc, sems)


def merge_phase(nc, core, act_hi, act_lo):
    d = core.d
    HALF = SEQ // 2
    with ExitStack() as ctx:
        sb, ps, sem, sems = scope(nc, ctx, "merge")
        w_raw = sb("w_raw", [P, 2, KD, P])
        w_hi = sb("w_hi", [P, 2, KD, P], F32R)
        w_lo = sb("w_lo", [P, 2, KD, P], F32R)
        zero = sb("zero", [P, 1])
        zeros = zero[:, :].unsqueeze(1).broadcast_to((P, KD, P))
        gate = sb("gate", [P, 2, 2, HALF])
        out = sb("out", [P, 2, HALF])
        acc = ps("acc", [P, 2, 2, HALF])
        w_in = [sem(f"w_in{b}") for b in range(2)]
        gate_in = [sem(f"gate_in{b}") for b in range(2)]
        stored = [sem(f"stored{b}") for b in range(2)]
        zeroed, hi_done, w_ready, mm_done, evac, gated = (sem(n) for n in ("zeroed", "hi_done", "w_ready", "mm_done", "evac", "gated"))
        unit_mm, products = sem("unit_mm"), sem("products")
        block_ctx = ExitStack()
        block = block_ctx.enter_context(nc.Block())

        @block.sync
        def _(sp):
            for h in range(2):
                sp.sem_inc(stored[h], 16)
            for b in range(2):
                sp.dma_start(w_raw[:, b, :, :], d["w_o"][b]).then_inc(w_in[b], 16)

            def chunk(i, b, prefetch):
                c = 2 * i + b
                if prefetch:
                    sp.wait_ge(w_ready, c + 1)
                    sp.dma_start(w_raw[:, b, :, :], d["w_o"][ds(c + 2, 1)].rearrange("a p k n -> (a p) k n")).then_inc(w_in[b], 16)
                for h in range(2):
                    sp.wait_ge(evac, 2 * c + h + 1)
                    for n in range(2):
                        sp.dma_start(gate[:, h, n, :], d["proj"][ds(c + GATE0 + KD * n, 1), :, HALF * h:HALF * (h + 1)].rearrange("a p t -> (a p) t")
                                     ).then_inc(gate_in[h], 16)
                for h in range(2):
                    sp.wait_ge(gated, 2 * c + h + 1)
                    sp.dma_start(d["mixed"][ds(c, 1), :, HALF * h:HALF * (h + 1)].rearrange("a p t -> (a p) t"), out[:, h, :]).then_inc(stored[h], 16)

            with sp.Fori(0, KD // 2 - 1) as i:
                for b in range(2):
                    chunk(i, b, True)
            for b in range(2):
                chunk(KD // 2 - 1, b, False)
            for h in range(2):
                sp.wait_ge(stored[h], 16 * (KD + 1))

        @block.gpsimd
        def _(pool):
            pool.memset(zero[:, :], 0.0).then_inc(zeroed, 1)
            pool.wait_ge(zeroed, 1)
            with pool.Fori(0, KD // 2) as i:
                for b in range(2):
                    weight_splitter(nc, pool, i, b, 0, zeros, w_in, w_raw, w_hi, w_lo, hi_done, w_ready, mm_done)

        @block.tensor
        def _(pe):
            pe.sem_inc(mm_done, 2)
            with pe.Fori(0, KD // 2) as i:
                for b in range(2):
                    c = 2 * i + b
                    pe.wait_ge(w_ready, c + 1)
                    for h in range(2):
                        pe.wait_ge(evac, 2 * c + h + 1)
                        for n in range(2):
                            for g in range(HALF // BANK):
                                at = slice(HALF * h + BANK * g, HALF * h + BANK * (g + 1))
                                for k in range(KH):
                                    last = product(nc, acc[:, h, n, ds(BANK * g, BANK)], w_hi[:, b, KH * n + k, :], w_lo[:, b, KH * n + k, :],
                                                   act_hi[:, KH * n + k, at], act_lo[:, KH * n + k, at], k == 0, k == KH - 1)
                        last.then_inc(unit_mm, 1)
                    pe.wait_ge(unit_mm, 2 * c + 2)
                    pe.sem_inc(mm_done, 1)

        @block.vector
        def _(dve):
            dve.sem_inc(evac, 2)
            with dve.Fori(0, KD) as c:
                for h in range(2):
                    dve.wait_ge(unit_mm, 2 * c + h + 1)
                    dve.wait_ge(gate_in[h], 32 * c + 32)
                    nc.vector.tensor_tensor(gate[:, h, :, :], acc[:, h, :, :], gate[:, h, :, :], ALU.mult).then_inc(products, 1)
                    dve.wait_ge(products, 2 * c + h + 1)
                    dve.wait_ge(stored[h], 16 * c + 16)
                    nc.vector.tensor_tensor(out[:, h, :], gate[:, h, 0, :], gate[:, h, 1, :], ALU.add).then_inc(gated, 1)
                    dve.wait_ge(gated, 2 * c + h + 1)
                    dve.sem_inc(evac, 1)

        block_ctx.close()
        clear(nc, sems)


def down_phase(nc, core):
    d = core.d
    with ExitStack() as ctx:
        sb, ps, sem, sems = scope(nc, ctx, "down")
        w_hi = sb("w_hi", [P, FF_CHUNKS, D_MODEL], F32R)
        w_lo = sb("w_lo", [P, FF_CHUNKS, D_MODEL], F32R)
        raw = sb("raw", [P, 2, D_MODEL])
        g_raw = sb("g_raw", [P, 2, BANK])
        g_hi, g_lo = sb("g_hi", [P, 2, BANK], F32R), sb("g_lo", [P, 2, BANK], F32R)
        out = sb("out", [P, 2, BANK])
        acc = ps("acc", [P, KD, BANK])
        w_in = [sem(f"w_in{b}") for b in range(2)]
        g_in = [sem(f"g_in{b}") for b in range(2)]
        stored = [sem(f"stored{b}") for b in range(2)]
        w_hi_done, w_lo_done, g_hi_done, g_ready, mm_done, out_mm, evac = (
            sem(n) for n in ("w_hi_done", "w_lo_done", "g_hi_done", "g_ready", "mm_done", "out_mm", "evac"))
        GROUPS = SEQ // BANK
        block_ctx = ExitStack()
        block = block_ctx.enter_context(nc.Block())

        @block.sync
        def _(sp):
            def load(t, k):
                sp.wait_ge(g_ready, FF_CHUNKS * t + k + 1)
                sp.dma_start(g_raw[:, k % 2, :], d["hidden"][k, :, ds(BANK * t, BANK)]).then_inc(g_in[k % 2], 16)

            for k in range(FF_CHUNKS):
                if k >= 2:
                    sp.wait_ge(w_lo_done, k - 1)
                sp.dma_start(raw[:, k % 2, :], d["w_down"][k]).then_inc(w_in[k % 2], 16)
                load(0, k)
            with sp.Fori(1, GROUPS) as t:
                for k in range(FF_CHUNKS):
                    load(t, k)

        @block.tensor
        def _(pe):
            def group(t):
                for k in range(FF_CHUNKS):
                    if isinstance(t, int):
                        pe.wait_ge(w_lo_done, k + 1)
                    pe.wait_ge(g_ready, FF_CHUNKS * t + k + 3)
                    for n in range(KD):
                        if k == 0:
                            pe.wait_ge(evac, KD * t + n + 1)
                        w = slice(P * n, P * n + P)
                        last = product(nc, acc[:, n, :], w_hi[:, k, w], w_lo[:, k, w], g_hi[:, k % 2, :], g_lo[:, k % 2, :],
                                       k == 0, k == FF_CHUNKS - 1)
                        if k == FF_CHUNKS - 1:
                            last.then_inc(out_mm, 1)
                    if k < FF_CHUNKS - 1:
                        last.then_inc(mm_done, 1)
                    else:
                        pe.wait_ge(out_mm, KD * t + KD)
                        pe.sem_inc(mm_done, 1)

            group(0)
            with pe.Fori(1, GROUPS) as t:
                group(t)

        @block.scalar
        def _(act):
            def hidden_hi(t, k):
                act.wait_ge(g_in[k % 2], (16 * (FF_CHUNKS // 2)) * t + 16 * (k // 2 + 1))
                act.wait_ge(mm_done, FF_CHUNKS * t + k + 1)
                nc.scalar.activation(g_hi[:, k % 2, :], g_raw[:, k % 2, :], ACT.Copy).then_inc(g_hi_done, 1)

            def results(t):
                for n in range(KD):
                    act.wait_ge(out_mm, KD * t + n + 1)
                    act.wait_ge(stored[n % 2], (16 * (KD // 2)) * t + 16 * (n // 2 + 1))
                    nc.scalar.activation(out[:, n % 2, :], acc[:, n, :], ACT.Copy).then_inc(evac, 1)
                    act.wait_ge(evac, KD * t + n + 1 + KD)
                    act.dma_start(d["branch"][n, :, ds(BANK * t, BANK)], out[:, n % 2, :]).then_inc(stored[n % 2], 16)

            act.sem_inc(evac, KD)
            act.sem_inc(mm_done, 2)
            for b in range(2):
                act.sem_inc(stored[b], 16)
            for k in range(FF_CHUNKS):
                act.wait_ge(w_in[k % 2], 16 * (k // 2 + 1))
                nc.scalar.activation(w_hi[:, k, :], raw[:, k % 2, :], ACT.Copy).then_inc(w_hi_done, 1)
                hidden_hi(0, k)
            with act.Fori(0, GROUPS - 1) as t:
                hidden_hi(t + 1, 0)
                results(t)
                for k in range(1, FF_CHUNKS):
                    hidden_hi(t + 1, k)
            results(GROUPS - 1)
            for b in range(2):
                act.wait_ge(stored[b], 16 * (GROUPS * KD // 2 + 1))

        @block.vector
        def _(dve):
            def hidden_lo(t, k):
                dve.wait_ge(g_hi_done, FF_CHUNKS * t + k + 1)
                nc.vector.tensor_tensor(g_lo[:, k % 2, :], g_raw[:, k % 2, :], g_hi[:, k % 2, :].bitcast(F32), ALU.subtract).then_inc(g_ready, 1)

            dve.sem_inc(g_ready, 2)
            for k in range(FF_CHUNKS):
                dve.wait_ge(w_hi_done, k + 1)
                nc.vector.tensor_tensor(w_lo[:, k, :], raw[:, k % 2, :], w_hi[:, k, :].bitcast(F32), ALU.subtract).then_inc(w_lo_done, 1)
                hidden_lo(0, k)
            with dve.Fori(1, GROUPS) as t:
                for k in range(FF_CHUNKS):
                    hidden_lo(t, k)

        block_ctx.close()
        clear(nc, sems)


def layer_program(nc, d):
    core = Core(nc, d)
    for name, shape in (("proj", (IN_CHUNKS, P, SEQ)), ("ctx_kv", (2 * KH, P, CTX_LEN)), ("rotated", (V0, P, SEQ)), ("branches", (KD, P, SEQ)),
                        ("mixed", (KD, P, SEQ)), ("branch", (KD, P, SEQ)), ("x1", (KD, P, SEQ)), ("hidden", (FF_CHUNKS, P, SEQ)),
                        ("spec_k", (R, R, D_HYENA)), ("spec_u", (R, R, D_HYENA)), ("spec_y", (R, R, D_HYENA))):
        d[name] = nc.dram_tensor(f"scratch_{name}", shape, F32).ap()
    with ExitStack() as ctx:
        core.vec = ctx.enter_context(nc.sbuf_tensor("vec", [P, N_VEC], F32))
        core.mod = ctx.enter_context(nc.sbuf_tensor("mod", [P, MOD_CHUNKS, 2], F32))
        core.mean = ctx.enter_context(nc.sbuf_tensor("mean", [P, P], F32))
        core.ident = ctx.enter_context(nc.sbuf_tensor("ident", [P, P], F32))
        core.rnorm = ctx.enter_context(nc.sbuf_tensor("rnorm", [P, KH], F32))
        setup_phase(nc, core)
        filter_phase(nc, core)

        def operand(stack, tag, tokens):
            return (stack.enter_context(nc.sbuf_tensor(f"{tag}_hi", [P, KD, tokens], F32R)),
                    stack.enter_context(nc.sbuf_tensor(f"{tag}_lo", [P, KD, tokens], F32R)))

        with ExitStack() as s:
            hi, lo = operand(s, "ctx_act", CTX_LEN)
            norm_phase(nc, core, "norm_ctx", d["ctx"], CTX_LEN, hi, lo, VEC["mix_pre"], 1, SH_MIX, SC_MIX)
            projection_phase(nc, core, "proj_ctx", d["w_in"], [("bias", K0, 2 * KH, d["ctx_kv"], VEC["b_in"] + K0)], hi, lo, CTX_LEN)
        with ExitStack() as s:
            hi, lo = operand(s, "mix_act", SEQ)
            norm_phase(nc, core, "norm_mix", d["x"], SEQ, hi, lo, VEC["mix_pre"], 0, SH_MIX, SC_MIX)
            projection_phase(nc, core, "proj_mix", d["w_in"], [
                (kind, first, last - first, d["proj"][first:last], VEC["b_in"] + first)
                for kind, first, last in (("query", Q0, K0), ("bias", K0, HY0), ("conv", HY0, GATE0), ("sigmoid", GATE0, IN_CHUNKS))],
                hi, lo, SEQ, rotary=(d["rotated"], d["proj"][Q0:V0]))
        attention_phase(nc, core)
        hyena_phase(nc, core)
        with ExitStack() as s:
            hi, lo = operand(s, "branch_act", SEQ)
            split_phase(nc, core, "split_branches", d["branches"], hi, lo)
            merge_phase(nc, core, hi, lo)
            split_phase(nc, core, "split_mixed", d["mixed"], hi, lo)
            projection_phase(nc, core, "proj_out", d["w_out"], [("plain", 0, KD, d["branch"], None)], hi, lo, SEQ)
        with ExitStack() as s:
            hi, lo = operand(s, "ffn_act", SEQ)
            norm_phase(nc, core, "norm_ffn", d["x"], SEQ, hi, lo, VEC["ffn_pre"], 0, SH_FFN, SC_FFN,
                       add=(d["branch"], G_MIX, VEC["mix_post"], d["x1"]))
            projection_phase(nc, core, "proj_up", d["w_up"], [("ffn", 0, 2 * FF_CHUNKS, d["hidden"], None)], hi, lo, SEQ)
        down_phase(nc, core)
        norm_phase(nc, core, "norm_out", d["x1"], SEQ, None, None, None, 0, None, None,
                   add=(d["branch"], G_FFN, VEC["ffn_post"], d["out"]))


def frequencies(g):
    if g:
        return [(g + R * k2, part) for part in ("re", "im") for k2 in range(R)]
    return ([(R * k2, "re") for k2 in range(33)] + [(32 + R * k2, "re") for k2 in range(32)]
            + [(R * k2, "im") for k2 in range(1, 32)] + [(32 + R * k2, "im") for k2 in range(32)])


def root(e):
    return np.exp(-2j * np.pi * np.asarray(e) / NFFT)


def stage1(n1):
    m = np.zeros((len(n1), R))
    for g in range(R // 2):
        for c in range(2):
            if g == 0:
                m[:, c] = root(R * n1 * (32 * c)).real
            else:
                z = root(R * n1 * g)
                m[:, 2 * g + c] = z.imag if c else z.real
    return m


def inverse_stage1(n1):
    m = np.zeros((R, len(n1)))
    for g in range(R // 2):
        for c in range(2):
            if g == 0:
                m[c] = root(R * n1 * (32 * c)).real
            else:
                z = np.conj(root(R * n1 * g))
                m[2 * g + c] = -z.imag if c else z.real
    return m


def twiddles():
    n2 = np.arange(R)
    groups = []
    for g in range(R // 2):
        rows = frequencies(g)

        def forward(rows):
            m = np.zeros((P, P))
            for i, (k, part, sign) in enumerate(rows):
                z = root(n2 * k) * sign
                if g:
                    m[:R, i], m[R:, i] = (z.real, -z.imag) if part == "re" else (z.imag, z.real)
                else:
                    c = int(k % R != 0)
                    m[R * c:R * c + R, i] = z.real if part == "re" else z.imag
            return m

        other = {"re": "im", "im": "re"}
        real = lambda k: k % (NFFT // 2) == 0
        x = forward([(k, part, 1) for k, part in rows])
        xs = forward([(k, other[part], 0 if real(k) else (-1 if part == "re" else 1)) for k, part in rows])
        ka = forward([(k, "re", 1) for k, part in rows])
        kb = forward([(k, "im", 0 if real(k) else 1) for k, part in rows])
        inv = np.zeros((P, P))
        for i, (k, part) in enumerate(rows):
            z = np.conj(root(n2 * k)) * ((1 if real(k) else 2) / NFFT)
            v = z if part == "re" else 1j * z
            if g:
                inv[i, :R], inv[i, R:] = v.real, v.imag
            else:
                c = int(k % R != 0)
                inv[i, R * c:R * c + R] = v.real
        groups.append(np.stack([x, xs, ka, kb, inv], 1))
    return np.array(groups)


def shape_constants():
    f = np.float32
    c = {}
    c["ident"] = np.eye(P, dtype=f)
    c["fold"] = np.tile(np.eye(HEAD_DIM, dtype=f), (2, 1))
    c["mean"] = np.full((P, P), 1.0 / D_MODEL, f)
    j, side, g, n1 = np.meshgrid(np.arange(R // 2), np.arange(2), np.arange(2), np.arange(32), indexing="ij")
    n = (R * (32 * side + n1) + 2 * j + g).reshape(-1)
    pos = np.where(n <= SEQ, n, NFFT - n).astype(f)
    t = pos / f(SEQ - 1)
    bands = np.linspace(1e-4, POS_BANDS - 1, POS_BANDS, dtype=f)
    ang = (f(2.0 * np.pi / SEQ) * pos)[:, None] * bands[None, :]
    c["z"] = np.ascontiguousarray(np.concatenate([t[:, None], np.cos(ang), -np.sin(ang)], 1).astype(f).T)
    c["neg_t"] = np.ascontiguousarray(-t.reshape(-1, P).T)
    c["keep"] = np.ascontiguousarray((n != SEQ).astype(f).reshape(-1, P).T)
    s1 = stage1(np.arange(R))
    dft_k = np.zeros((2, 2, 32, 2, R))
    for gg in range(2):
        for side in range(2):
            dft_k[side, gg, :, gg, :] = s1[32 * side:32 * side + 32]
    c["dft_k"] = dft_k.reshape(P, P).astype(f)
    dft_u = np.zeros((4, 32, 2, 2, R))
    for gg in range(4):
        dft_u[gg, :, gg // 2, gg % 2, :] = s1[:32]
    c["dft_u"] = dft_u.reshape(P, 2, P).astype(f)
    idft = np.zeros((2, R, 2, 32))
    for gg in range(2):
        idft[gg, :, gg, :] = inverse_stage1(np.arange(32))
    c["idft"] = idft.reshape(P, R).astype(f)
    c["twiddle"] = twiddles().astype(f)
    tok = np.arange(SEQ)
    inv_freq = (f(10000.0) ** (-np.arange(16, dtype=f) / f(16))).astype(f)
    cos, sin = np.zeros((P, SEQ), f), np.zeros((P, SEQ), f)
    for i, ch in enumerate(np.tile(HEAD_ORDER, 2)):
        axis = (tok // GRID_W, tok % GRID_W)[ch // 32].astype(f)
        a = axis * inv_freq[ch % 16]
        cos[i], sin[i] = np.cos(a), np.sin(a) * (-1 if ch % 32 < 16 else 1)
    c["cos"], c["sin"] = cos.reshape(P, 2, SEQ // 2), sin.reshape(P, 2, SEQ // 2)
    qc, kc = np.arange(GRID_W)[:, None], np.arange(GRID_W)[None, :]
    start = np.clip(qc - WIN_COLS // 2, 0, GRID_W - WIN_COLS)
    mask = np.where((kc >= start) & (kc < start + WIN_COLS), 0.0, MASKED).astype(f)
    c["colmask"] = np.tile(mask, (2, 1))
    return c


def laid_out(x, c, ctx, c_ctx, w_mod, b_mod, norm_mix_pre, norm_mix_post, norm_ffn_pre, norm_ffn_post,
             w_in, b_in, na_rpb, hy_conv_w, hy_conv_b, hy_filt_w1, hy_filt_b1, hy_filt_w2, hy_filt_b2,
             hy_filt_w3, hy_filt_b3, hy_sin_freq, hy_decay, hy_skip, w_o_na, w_o_hy, w_out,
             ffn_w_up, ffn_conv_w, ffn_conv_b, ffn_w_down):
    def tiles(w):
        k, n = w.shape[0] // P, w.shape[1] // P
        return np.ascontiguousarray(w.reshape(k, P, n, P).transpose(2, 1, 0, 3))

    def cols(v):
        return np.asarray(v).reshape(-1, P).T

    def pairs(v):
        s = v.shape[:-1]
        return np.swapaxes(v.reshape(*s, 2, FF_CHUNKS, P), -3, -2).reshape(*s, 2 * D_FF)

    def head_order(v):
        n = 2 * D_ATTN
        qk = v[..., :n].reshape(*v.shape[:-1], n // HEAD_DIM, HEAD_DIM)[..., HEAD_ORDER]
        return np.concatenate([qk.reshape(*v.shape[:-1], n), v[..., n:]], -1)

    a = {}
    a["x"] = np.ascontiguousarray(x[0].T).reshape(KD, P, SEQ)
    a["ctx"] = np.ascontiguousarray(ctx[0].T).reshape(KD, P, CTX_LEN)
    a["cond"] = np.ascontiguousarray(np.stack([cols(c[0]), cols(c_ctx)], -1))
    a["w_mod"] = np.ascontiguousarray(w_mod[0].reshape(2, KD // 2, P, MOD_CHUNKS * P).transpose(2, 0, 1, 3))
    a["w_in"] = tiles(head_order(w_in[0]))
    a["w_o"] = tiles(np.concatenate([w_o_na[0], w_o_hy[0]]))
    a["w_out"] = tiles(w_out[0])
    a["w_up"] = tiles(pairs(ffn_w_up[0]))
    a["w_down"] = np.ascontiguousarray(ffn_w_down[0].reshape(FF_CHUNKS, P, D_MODEL))
    cw, fw = hy_conv_w[0], pairs(ffn_conv_w[0])
    a["vec"] = np.ascontiguousarray(np.concatenate([cols(v) for v in (
        head_order(b_in[0]), b_mod[0], norm_mix_pre[0], norm_mix_post[0], norm_ffn_pre[0], norm_ffn_post[0],
        cw[0], cw[1], cw[2], hy_conv_b[0], hy_skip[0], fw[0], fw[1], fw[2], pairs(ffn_conv_b[0]))], 1))
    a["filt_w1"], a["filt_w2"], a["filt_w3"] = hy_filt_w1[0], hy_filt_w2[0], hy_filt_w3[0]
    a["filt_hid"] = np.ascontiguousarray(np.stack([hy_filt_b1[0], hy_sin_freq[0, 0], hy_filt_b2[0], hy_sin_freq[0, 1]], 1))
    a["filt_b3"] = hy_filt_b3[0].reshape(2, D_HYENA)
    a["decay"] = hy_decay[0]
    qc, kc = np.arange(GRID_W)[:, None], np.arange(GRID_W)[None, :]
    dc = np.clip(kc - qc, 1 - WIN_COLS, WIN_COLS - 1) + WIN_COLS - 1
    rel = na_rpb[0][:, :, dc].transpose(0, 2, 1, 3)
    a["rpb"] = np.ascontiguousarray(np.stack([rel[:, :, 1 - qr:15 - qr] for qr in range(2)], 1)).reshape(N_HEADS, P, 14 * GRID_W)
    return a


def kernel(**inputs):
    import concourse.bacc as bacc
    from concourse.bass_utils import run_bass_kernel_spmd

    arrays = {**laid_out(**{k: np.asarray(v) for k, v in inputs.items()}), **shape_constants()}
    nc = bacc.Bacc("TRN2", target_bir_lowering=False, num_devices=1)
    d = {n: nc.dram_tensor(f"in_{n}", a.shape, mybir.dt.from_np(a.dtype), kind="ExternalInput").ap() for n, a in arrays.items()}
    d["out"] = nc.dram_tensor("out", (KD, P, SEQ), F32, kind="ExternalOutput").ap()
    layer_program(nc, d)
    result = run_bass_kernel_spmd(nc, [{f"in_{n}": np.ascontiguousarray(a) for n, a in arrays.items()}], core_ids=[0])
    return np.ascontiguousarray(result.results[0]["out"].reshape(D_MODEL, SEQ).T)[None]
```

```python
from contextlib import ExitStack

import concourse.bass as bass
import numpy as np
from concourse import mybir

F32 = mybir.dt.float32
F32R = mybir.dt.float32r
ALU = mybir.AluOpType
ACT = mybir.ActivationFunctionType
AX = mybir.AxisListType
ds = bass.ds

P = 128
D_MODEL, SEQ, CTX_LEN = 1024, 2048, 256
KD = D_MODEL // P
N_HEADS, HEAD_DIM, GRID_W = 8, 64, 64
ROWS = SEQ // GRID_W
D_ATTN, D_HYENA, D_FF = 512, 512, 2816
WIN_ROWS, WIN_COLS = 8, 16
KH = D_HYENA // P
FF_CHUNKS = D_FF // P
FILTER_HIDDEN, POS_BANDS = 64, 16
RMS_EPS = 1e-6
MASKED = -1e30
BANK = 512

Q0, K0, V0, HY0, GATE0, IN_CHUNKS = 0, 4, 8, 12, 24, 40
MOD_CHUNKS = 48
SH_MIX, SC_MIX, G_MIX, SH_FFN, SC_FFN, G_FFN = (KD * i for i in range(6))

NFFT = 2 * SEQ
R = 64

HEAD_ORDER = np.arange(HEAD_DIM).reshape(2, 2, 16).transpose(1, 0, 2).reshape(-1)

VEC = {}
_at = 0
for _name, _n in (("b_in", 40), ("b_mod", 48), ("mix_pre", 8), ("mix_post", 8), ("ffn_pre", 8), ("ffn_post", 8),
                  ("hy_w0", 12), ("hy_w1", 12), ("hy_w2", 12), ("hy_b", 12), ("skip", 4),
                  ("ff_w0", 44), ("ff_w1", 44), ("ff_w2", 44), ("ff_b", 44)):
    VEC[_name] = _at
    _at += _n
N_VEC = _at


class Core:

    def __init__(self, nc, dram):
        self.nc, self.d = nc, dram


def scope(nc, ctx, tag):
    sems = []

    def sb(name, shape, dt=F32):
        return ctx.enter_context(nc.sbuf_tensor(f"{tag}_{name}", shape, dt))

    def ps(name, shape):
        return ctx.enter_context(nc.psum_tensor(f"{tag}_{name}", shape, F32))

    def sem(name):
        s = ctx.enter_context(nc.semaphore(f"{tag}_{name}"))
        sems.append(s)
        return s

    return sb, ps, sem, sems


def clear(nc, sems):
    with nc.Block() as block:
        @block.gpsimd
        def _(pool):
            nums = sorted(s.num for s in sems)
            starts = [n for n in nums if n - 1 not in nums]
            ends = [n + 1 for n in nums if n + 1 not in nums]
            for a, b in zip(starts, ends):
                pool.sem_clear(range(a, b))


def setup_phase(nc, core):
    d = core.d
    with ExitStack() as ctx:
        sb, ps, sem, sems = scope(nc, ctx, "setup")
        const_in = sem("const_in")
        with nc.Block() as block:
            @block.sync
            def _(sp):
                sp.dma_start(core.vec[:, :], d["vec"]).then_inc(const_in, 16)
                sp.dma_start(core.ident[:, :], d["ident"]).then_inc(const_in, 16)
                sp.dma_start(core.mean[:, :], d["mean"]).then_inc(const_in, 16)
                sp.dma_start(core.pick[:, :, :], d["pick"]).then_inc(const_in, 16)
                sp.wait_ge(const_in, 64)
        clear(nc, sems)


def fold_mean_square(nc, core, out, squares):
    for g in range(SEQ // BANK):
        last = nc.tensor.matmul(out[32 * g:32 * g + 32, 0:BANK], core.mean[:, 0:32], squares[:, ds(BANK * g, BANK)], start=True, stop=True)
    return last


def spread_rs(nc, core, out):
    for g in range(SEQ // BANK):
        last = nc.tensor.matmul(out[:, ds(BANK * g, BANK)], core.pick[:, g, :], core.rs[:, :], start=True, stop=True)
    return last


def rs_on_dve(nc, core, dve, mean_sq, ms_done, eps_added, rooted, rs_done):
    dve.wait_ge(ms_done, 1)
    nc.vector.tensor_scalar(core.rs[:, :], mean_sq[:, 0:BANK], RMS_EPS, None, ALU.add).then_inc(eps_added, 1)
    dve.wait_ge(rooted, 1)
    nc.vector.reciprocal(core.rs[:, :], core.rs[:, :]).then_inc(rs_done, 1)
    dve.wait_ge(rs_done, 1)


def root_on_act(nc, core, act, eps_added, rooted):
    act.wait_ge(eps_added, 1)
    nc.scalar.activation(core.rs[:, :], core.rs[:, :], ACT.Sqrt).then_inc(rooted, 1)


def filter_phase(nc, core):
    d = core.d
    half = NFFT // 2
    two_pi_1, two_pi_2 = 6.28125, 0.0019350051879882812
    two_pi_3 = float(np.float64(2 * np.pi) - two_pi_1 - two_pi_2)
    magic = float(1.5 * 2 ** 23)
    pi_below = 3.1415925
    with ExitStack() as ctx:
        sb, ps, sem, sems = scope(nc, ctx, "filt")
        z = sb("z", [2 * POS_BANDS + 1, NFFT])
        w1 = sb("w1", [2 * POS_BANDS + 1, FILTER_HIDDEN])
        w2 = sb("w2", [P, FILTER_HIDDEN])
        w3 = sb("w3", [P, 2 * D_HYENA])
        hid = sb("hid", [P, 4])
        b3 = sb("b3", [P, D_HYENA])
        decay = sb("decay", [P, D_HYENA])
        neg_t = sb("neg_t", [P, NFFT // P])
        keep = sb("keep", [P, NFFT // P])
        dft = sb("dft", [P, P])
        ones = sb("ones", [P, 1])
        h1 = sb("h1", [P, half])
        h2 = sb("h2", [P, half])
        turns = sb("turns", [P, half])
        cond = sb("cond", [P, KD, 2])
        cond_s = sb("cond_s", [P, KD, 2])
        wm = sb("wm", [P, 4, KD // 2, BANK])
        mod_row = sb("mod_row", [2, MOD_CHUNKS * P])
        hs = sb("hs", [P, 2, P])
        dec = sb("dec", [P, 2, D_HYENA])
        kc = sb("kc", [P, 2, D_HYENA])
        kabs = sb("kabs", [P, 2, D_HYENA])
        ksum = sb("ksum", [P, D_HYENA])
        spec = sb("spec", [P, 2, D_HYENA])
        ps_h = ps("ps_h", [P, half])
        ps_s = ps("ps_s", [P, 2, BANK])
        ps_m = ps("ps_m", [P, MOD_CHUNKS, 2])
        ps_n = ps("ps_n", [P, BANK])
        xs = sb("xs", [P, 2, SEQ])
        xsum = sb("xsum", [P, SEQ])
        x_in = [sem(f"x_in{b}") for b in range(2)]
        x_sq, x_used, ms_done, eps_added, rooted, rs_done = (sem(n) for n in ("x_sq", "x_used", "ms_done", "eps_added", "rooted", "rs_done"))

        const_in, z_ready, mm_layer, layer, wrap = sem("const_in"), sem("z_ready"), sem("mm_layer"), sem("layer"), sem("wrap")
        wm_in = [sem(f"wm_in{m}") for m in range(4)]
        silu, wm_used, mod_mm, mod_out, mod_flip, mod_done = (sem(n) for n in ("silu", "wm_used", "mod_mm", "mod_out", "mod_flip", "mod_done"))
        hs_ready, tile_mm, dec_ready, kc_step, kc_ready = sem("hs_ready"), sem("tile_mm"), sem("dec_ready"), sem("kc_step"), sem("kc_ready")
        kabs_ready, ksum_done, spec_mm, spec_out = sem("kabs_ready"), sem("ksum_done"), sem("spec_mm"), sem("spec_out")
        stored = [sem(f"stored{s}") for s in range(2)]
        norm_mm, norm_done, tile_begun = sem("norm_mm"), sem("norm_done"), sem("tile_begun")
        tiles = NFFT // P // 2
        n_const = 16
        MOD_ROUNDS = MOD_CHUNKS * P // (2 * BANK)

        block_ctx = ExitStack()
        block = block_ctx.enter_context(nc.Block())

        @block.sync
        def _(sp):
            for dst, src in ((z, "z"), (w1, "filt_w1")):
                sp.dma_start(dst[:, :], d[src]).then_inc(const_in, 16)
            for h in range(2):
                sp.dma_start(w2[64 * h:64 * h + 64, :], d["filt_w2"]).then_inc(const_in, 16)
                sp.dma_start(w3[64 * h:64 * h + 64, :], d["filt_w3"]).then_inc(const_in, 16)
                sp.dma_start(hid[64 * h:64 * h + 64, :], d["filt_hid"]).then_inc(const_in, 16)
                sp.dma_start(b3[64 * h:64 * h + 64, :], d["filt_b3"][h:h + 1, :].partition_broadcast(64)).then_inc(const_in, 16)
                sp.dma_start(decay[64 * h:64 * h + 64, :], d["decay"][h:h + 1, :].partition_broadcast(64)).then_inc(const_in, 16)
            sp.dma_start(neg_t[:, :], d["neg_t"]).then_inc(const_in, 16)
            sp.dma_start(keep[:, :], d["keep"]).then_inc(const_in, 16)
            sp.dma_start(cond[:, :, :], d["cond"]).then_inc(const_in, 16)
            sp.dma_start(dft[:, :], d["dft_k"]).then_inc(const_in, 16)
            sp.sem_inc(stored[0], 16)
            sp.sem_inc(stored[1], 16)
            for b in range(2):
                sp.dma_start(xs[:, b, :], d["x"][b]).then_inc(x_in[b], 16)
            with sp.Fori(0, MOD_ROUNDS // 2) as i:
                for b in range(2):
                    r = 2 * i + b
                    for m in range(4):
                        sp.wait_ge(wm_used, 4 * r + m + 1)
                        sp.dma_start(wm[:, m, :, :], d["w_mod"][:, m % 2, :, ds((2 * BANK) * r + BANK * (m // 2), BANK)]).then_inc(wm_in[m], 16)
                    sp.wait_ge(x_used, r + 2)
                    sp.dma_start(xs[:, b, :], d["x"][ds(r + 2, 1)].rearrange("a p t -> (a p) t")).then_inc(x_in[b], 16)
            with sp.Fori(0, tiles) as i:
                for s in range(2):
                    sp.wait_ge(spec_out, 2 * i + s + 3)
                    sp.dma_start(d["spec_k"][ds((2 * i) + 2 * tiles * s, 2)].rearrange("g r c -> (g r) c"),
                                 spec[:, s, :]).then_inc(stored[s], 16)
            for s in range(2):
                sp.wait_ge(stored[s], 16 * (tiles + 1))

        @block.gpsimd
        def _(pool):
            pool.sem_inc(ksum_done, 2)
            pool.memset(ksum[:, :], 0.0).then_inc(ksum_done, 1)
            pool.memset(ones[:, :], 1.0).then_inc(z_ready, 1)
            pool.memset(xsum[:, :], 0.0).then_inc(x_used, 1)
            with pool.Fori(0, KD // 2) as i:
                for b in range(2):
                    pool.wait_ge(x_in[b], 16 * i + 16)
                    nc.gpsimd.tensor_tensor(xs[:, b, :], xs[:, b, :], xs[:, b, :], ALU.mult).then_inc(x_sq, 1)
                    pool.wait_ge(x_used, 2 * i + b + 1)
                    pool.wait_ge(x_sq, 2 * i + b + 1)
                    nc.gpsimd.tensor_tensor(xsum[:, :], xsum[:, :], xs[:, b, :], ALU.add).then_inc(x_used, 1)
            with pool.Fori(0, tiles) as i:
                for s in range(2):
                    pool.wait_ge(ksum_done, 2 * i + s + 3)
                    pool.wait_ge(kabs_ready, 2 * i + s + 1)
                    nc.gpsimd.tensor_tensor(ksum[:, :], ksum[:, :], kabs[:, s, :], ALU.add).then_inc(ksum_done, 1)

        @block.tensor
        def _(pe):
            def modulation(start, end):
                with pe.Fori(start, end) as i:
                    for g in range(2):
                        pe.wait_ge(mod_out, 2 * i + g + 1)
                        for h in range(2):
                            pe.wait_ge(wm_in[2 * g + h], 16 * i + 16)
                            for k in range(KD // 2):
                                last = nc.tensor.matmul(ps_s[0:2, g, :], cond_s[:, KD // 2 * h + k, :], wm[:, 2 * g + h, k, :],
                                                        start=(h == 0 and k == 0), stop=(h == 1 and k == KD // 2 - 1))
                            if h == 0:
                                last.then_inc(wm_used, 1)
                        last.then_inc(mod_mm, 1)
                        pe.wait_ge(mod_mm, 2 * i + g + 1)
                        pe.sem_inc(wm_used, 1)

            pe.sem_inc(wm_used, 4)
            pe.wait_ge(const_in, 16 * n_const)
            for h in range(2):
                for g in range(half // BANK):
                    last = nc.tensor.matmul(ps_h[64 * h:64 * h + 64, ds(BANK * g, BANK)], w1[:, :],
                                            z[:, ds(half * h + BANK * g, BANK)], start=True, stop=True)
            last.then_inc(mm_layer, 1)
            pe.wait_ge(silu, 1)
            modulation(0, 1)
            pe.wait_ge(layer, 1)
            for h in range(2):
                for g in range(half // BANK):
                    last = nc.tensor.matmul(ps_h[64 * h:64 * h + 64, ds(BANK * g, BANK)], w2[64 * h:64 * h + 64, :],
                                            h1[64 * h:64 * h + 64, ds(BANK * g, BANK)], start=True, stop=True)
            last.then_inc(mm_layer, 1)
            modulation(1, 2)
            pe.wait_ge(layer, 2)
            pe.wait_ge(z_ready, 2)
            modulation(2, MOD_ROUNDS)
            pe.wait_ge(mod_out, 2 * MOD_ROUNDS + 2)
            for c in range(MOD_CHUNKS):
                last = nc.tensor.transpose(ps_m[:, c, :], mod_row[:, P * c:P * c + P], core.ident[0:2, 0:2])
            last.then_inc(mod_flip, 1)
            pe.wait_ge(x_used, KD + 1)
            fold_mean_square(nc, core, ps_n, xsum).then_inc(ms_done, 1)

            with pe.Fori(0, tiles) as i:
                for s in range(2):
                    pe.wait_ge(hs_ready, 2 * i + s + 1)
                    pe.wait_ge(kc_ready, 2 * i + s + 1)
                    pe.sem_inc(tile_begun, 1)
                    for h in range(2):
                        last = nc.tensor.matmul(ps_h[64 * h:64 * h + 64, ds(BANK * s, BANK)],
                                                hs[64 * s:64 * s + 64, s, 64 * h:64 * h + 64],
                                                w3[64 * s:64 * s + 64, ds(D_HYENA * h, D_HYENA)], start=True, stop=True)
                    last.then_inc(tile_mm, 1)
                for s in range(2):
                    pe.wait_ge(kc_ready, 2 * i + s + 3)
                    nc.tensor.matmul(ps_s[:, s, :], dft[:, :], kc[:, s, :], start=True, stop=True).then_inc(spec_mm, 1)
            pe.wait_ge(tile_begun, 2 * tiles)
            pe.wait_ge(eps_added, 1)
            pe.wait_ge(ksum_done, 2 * tiles + 3)
            for q in range(KH):
                last = nc.tensor.matmul(ps_n[:, q:q + 1], ksum[:, ds(P * q, P)], ones[:, :], start=True, stop=True)
            last.then_inc(norm_mm, 1)

        @block.scalar
        def _(act):
            def modulation(start, end):
                with act.Fori(start, end) as i:
                    for g in range(2):
                        act.wait_ge(mod_mm, 2 * i + g + 1)
                        nc.scalar.activation(mod_row[:, ds((2 * BANK) * i + BANK * g, BANK)], ps_s[0:2, g, :], ACT.Copy).then_inc(mod_out, 1)

            act.sem_inc(spec_out, 2)
            act.sem_inc(mod_out, 2)
            act.wait_ge(const_in, 16 * n_const)
            nc.scalar.activation(cond_s[:, :, :], cond[:, :, :], ACT.Silu).then_inc(silu, 1)
            nc.scalar.activation(decay[:, :], decay[:, :], ACT.Abs).then_inc(z_ready, 1)
            for n in range(2):
                modulation(n, n + 1)
                act.wait_ge(wrap, 7 * n + 7)
                nc.scalar.activation((h1, h2)[n][:, :], turns[:, :], ACT.Sin).then_inc(layer, 1)
            modulation(2, MOD_ROUNDS)
            root_on_act(nc, core, act, eps_added, rooted)
            act.wait_ge(z_ready, 2)
            with act.Fori(0, tiles) as i:
                for s in range(2):
                    act.wait_ge(kc_ready, 2 * i + s + 1)
                    nc.scalar.activation(dec[:, s, :], decay[:, :], ACT.Exp,
                                         scale=neg_t[:, ds(i + tiles * s, 1)]).then_inc(dec_ready, 1)
                for s in range(2):
                    act.wait_ge(kc_ready, 2 * i + s + 3)
                    act.wait_ge(ksum_done, 2 * i + s + 2)
                    nc.scalar.activation(kabs[:, s, :], kc[:, s, :], ACT.Abs).then_inc(kabs_ready, 1)
                    act.wait_ge(spec_mm, 2 * i + s + 1)
                    act.wait_ge(stored[s], 16 * i + 16)
                    nc.scalar.activation(spec[:, s, :], ps_s[:, s, :], ACT.Copy).then_inc(spec_out, 1)

        @block.vector
        def _(dve):
            done = [0]

            def chain(ins):
                ins.then_inc(wrap, 1)
                done[0] += 1
                dve.wait_ge(wrap, done[0])

            dve.sem_inc(kc_ready, 2)
            dve.wait_ge(const_in, 16 * n_const)
            for n in range(2):
                dve.wait_ge(mm_layer, n + 1)
                chain(nc.vector.tensor_scalar(h2[:, :], ps_h[:, :], hid[:, 2 * n:2 * n + 1], hid[:, 2 * n + 1:2 * n + 2], ALU.add, ALU.mult))
                chain(nc.vector.tensor_scalar(turns[:, :], h2[:, :], float(1 / (2 * np.pi)), magic, ALU.mult, ALU.add))
                chain(nc.vector.tensor_scalar(turns[:, :], turns[:, :], -magic, None, ALU.add))
                chain(nc.vector.scalar_tensor_tensor(h2[:, :], turns[:, :], -two_pi_1, h2[:, :], ALU.mult, ALU.add))
                chain(nc.vector.scalar_tensor_tensor(h2[:, :], turns[:, :], -two_pi_2, h2[:, :], ALU.mult, ALU.add))
                chain(nc.vector.scalar_tensor_tensor(h2[:, :], turns[:, :], -two_pi_3, h2[:, :], ALU.mult, ALU.add))
                chain(nc.vector.tensor_scalar(turns[:, :], h2[:, :], pi_below, -pi_below, ALU.min, ALU.max))
            rs_on_dve(nc, core, dve, ps_n, ms_done, eps_added, rooted, rs_done)
            dve.wait_ge(layer, 2)

            with dve.Fori(0, tiles) as i:
                for s in range(2):
                    nc.vector.tensor_copy(hs[64 * s:64 * s + 64, s, :], h2[64 * s:64 * s + 64, ds(P * i, P)]).then_inc(hs_ready, 1)
                for s in range(2):
                    dve.wait_ge(tile_mm, 2 * i + s + 1)
                    dve.wait_ge(spec_out, 2 * i + s + 1)
                    nc.vector.tensor_tensor(kc[:, s, :], ps_h[:, ds(BANK * s, BANK)], b3[:, :], ALU.add).then_inc(kc_step, 1)
                    dve.wait_ge(kc_step, 2 * i + s + 1)
                    dve.wait_ge(dec_ready, 2 * i + s + 1)
                    nc.vector.scalar_tensor_tensor(kc[:, s, :], kc[:, s, :], keep[:, ds(i + tiles * s, 1)], dec[:, s, :],
                                                   ALU.mult, ALU.mult).then_inc(kc_ready, 1)
            dve.wait_ge(norm_mm, 1)
            nc.vector.reciprocal(core.rnorm[:, :], ps_n[:, 0:KH]).then_inc(norm_done, 1)
            dve.wait_ge(norm_done, 1)
            dve.wait_ge(mod_flip, 1)
            nc.vector.tensor_tensor(core.mod[:, :, :], ps_m[:, :, :],
                                    core.vec[:, VEC["b_mod"]:VEC["b_mod"] + MOD_CHUNKS].unsqueeze(2).broadcast_to((P, MOD_CHUNKS, 2)), ALU.add
                                    ).then_inc(mod_done, 1)
            dve.wait_ge(mod_done, 1)

        block_ctx.close()
        clear(nc, sems)


def mean_square(pe, core, out, sq):
    nc = core.nc
    for k in range(KD):
        last = nc.tensor.matmul(out, core.mean[:, :], sq[:, k, :], start=(k == 0), stop=(k == KD - 1))
    return last


def norm_phase(nc, core, tag, x_d, tokens, act_hi, act_lo, norm_w, cond_col, shift, scale, add=None):
    W = 256
    groups = tokens // W
    nb = min(2, groups)
    rounds = groups // nb
    with ExitStack() as ctx:
        sb, ps, sem, sems = scope(nc, ctx, tag)
        x = sb("x", [P, nb, KD, W])
        r = sb("r", [P, nb, KD, W]) if add else None
        sq = sb("sq", [P, KD, W])
        t = sb("t", [P, KD, W])
        rs = sb("rs", [P, 2, W])
        col = sb("col", [P, 3, KD])
        ms = ps("ms", [P, 2, BANK])
        x_in = [sem(f"x_in{b}") for b in range(nb)]
        r_in = [sem(f"r_in{b}") for b in range(nb)] if add else None
        stored = [sem(f"stored{b}") for b in range(nb)]
        cols, squared, ms_done, eps_added, rooted, rs_done = (sem(n) for n in ("cols", "squared", "ms_done", "eps_added", "rooted", "rs_done"))
        scaled, x1_step, x1_done, shifted, hi_done, lo_done = (sem(n) for n in ("scaled", "x1_step", "x1_done", "shifted", "hi_done", "lo_done"))
        want = act_hi is not None
        stats = int(want) + int(add is not None)
        freed = lo_done if want else x1_done

        def stat_base(i, b):
            return stats * (nb * i + b)

        block_ctx = ExitStack()
        block = block_ctx.enter_context(nc.Block())

        @block.sync
        def _(sp):
            for b in range(nb):
                sp.sem_inc(stored[b], 16)
            with sp.Fori(0, rounds) as i:
                for b in range(nb):
                    at = ds((nb * i + b) * W, W)
                    sp.wait_ge(freed, nb * i + b + 1)
                    sp.wait_ge(stored[b], 16 * i + 16)
                    sp.dma_start(x[:, b, :, :], x_d[:, :, at].rearrange("k p t -> p k t")).then_inc(x_in[b], 16)
                    if add:
                        sp.dma_start(r[:, b, :, :], add[0][:, :, at].rearrange("k p t -> p k t")).then_inc(r_in[b], 16)
                for b in range(nb):
                    at = ds((nb * i + b) * W, W)
                    if add:
                        sp.wait_ge(x1_done, nb * i + b + 1 + (0 if want else nb))
                        sp.dma_start(add[3][:, :, at].rearrange("k p t -> p k t"), x[:, b, :, :]).then_inc(stored[b], 16)
                    else:
                        sp.sem_inc(stored[b], 16)
            for b in range(nb):
                sp.wait_ge(stored[b], 16 * (rounds + 1))

        @block.gpsimd
        def _(pool):
            pass

        @block.tensor
        def _(pe):
            with pe.Fori(0, rounds) as i:
                for b in range(nb):
                    for n in range(stats):
                        pe.wait_ge(squared, stat_base(i, b) + n + 1)
                        mean_square(pe, core, ms[:, n, 0:W], sq).then_inc(ms_done, 1)

        @block.scalar
        def _(act):
            act.wait_ge(cols, 3 if want or add else 1)
            with act.Fori(0, rounds) as i:
                for b in range(nb):
                    for n in range(stats):
                        src = r if (add and n == 0) else x
                        if src is r:
                            act.wait_ge(r_in[b], 16 * i + 16)
                        elif add:
                            act.wait_ge(x1_done, nb * i + b + 1)
                        else:
                            act.wait_ge(x_in[b], 16 * i + 16)
                        nc.scalar.activation(sq[:, :, :], src[:, b, :, :], ACT.Square).then_inc(squared, 1)
                        act.wait_ge(eps_added, stat_base(i, b) + n + 1)
                        nc.scalar.activation(rs[:, n, :], rs[:, n, :], ACT.Sqrt).then_inc(rooted, 1)
                    if want:
                        act.wait_ge(scaled, nb * i + b + 1)
                        for k in range(KD):
                            last = nc.scalar.activation(t[:, k, :], t[:, k, :], ACT.Identity, bias=col[:, 1, k:k + 1], scale=col[:, 0, k:k + 1])
                        last.then_inc(shifted, 1)
                        act.wait_ge(shifted, nb * i + b + 1)
                        nc.scalar.activation(act_hi[:, :, ds((nb * i + b) * W, W)], t[:, :, :], ACT.Copy).then_inc(hi_done, 1)

        @block.vector
        def _(dve):
            dve.sem_inc(freed, nb)
            vec, mod = core.vec, core.mod
            if want:
                nc.vector.tensor_scalar(col[:, 2, :], mod[:, scale:scale + KD, cond_col], 1.0, None, ALU.add).then_inc(cols, 1)
                dve.wait_ge(cols, 1)
                nc.vector.tensor_tensor(col[:, 0, :], col[:, 2, :], vec[:, norm_w:norm_w + KD], ALU.mult).then_inc(cols, 1)
                nc.vector.tensor_copy(col[:, 1, :], mod[:, shift:shift + KD, cond_col]).then_inc(cols, 1)
                dve.wait_ge(cols, 3)
            else:
                dve.sem_inc(cols, 3)
            if add:
                nc.vector.tensor_tensor(col[:, 2, :], mod[:, add[1]:add[1] + KD, 0], vec[:, add[2]:add[2] + KD], ALU.mult).then_inc(x1_step, 1)
            with dve.Fori(0, rounds) as i:
                for b in range(nb):
                    for n in range(stats):
                        dve.wait_ge(ms_done, stat_base(i, b) + n + 1)
                        nc.vector.tensor_scalar(rs[:, n, :], ms[:, n, 0:W], RMS_EPS, None, ALU.add).then_inc(eps_added, 1)
                        dve.wait_ge(rooted, stat_base(i, b) + n + 1)
                        nc.vector.reciprocal(rs[:, n, :], rs[:, n, :]).then_inc(rs_done, 1)
                        dve.wait_ge(rs_done, stat_base(i, b) + n + 1)
                        rs_all = rs[:, n, :].unsqueeze(1).broadcast_to((P, KD, W))
                        if add and n == 0:
                            dve.wait_ge(x_in[b], 16 * i + 16)
                            nc.vector.tensor_tensor(r[:, b, :, :], r[:, b, :, :], rs_all, ALU.mult).then_inc(x1_step, 1)
                            dve.wait_ge(x1_step, nb * i + b + 2)
                            for k in range(KD):
                                last = nc.vector.scalar_tensor_tensor(x[:, b, k, :], r[:, b, k, :], col[:, 2, k:k + 1], x[:, b, k, :], ALU.mult, ALU.add)
                            last.then_inc(x1_done, 1)
                            if want:
                                dve.wait_ge(x1_done, nb * i + b + 1)
                        else:
                            nc.vector.tensor_tensor(t[:, :, :], x[:, b, :, :], rs_all, ALU.mult).then_inc(scaled, 1)
                    if want:
                        dve.wait_ge(hi_done, nb * i + b + 1)
                        at = ds((nb * i + b) * W, W)
                        nc.vector.tensor_tensor(act_lo[:, :, at], t[:, :, :], act_hi[:, :, at].bitcast(F32), ALU.subtract).then_inc(lo_done, 1)
                        dve.wait_ge(lo_done, nb * i + b + 1 + nb)

        block_ctx.close()
        clear(nc, sems)


def residual_phase(nc, core, x1):
    d = core.d
    NB = 3
    with ExitStack() as ctx:
        sb, ps, sem, sems = scope(nc, ctx, "res")
        x, r = sb("x", [P, NB, SEQ]), sb("r", [P, NB, SEQ])
        sq = sb("sq", [P, 2, SEQ])
        total = sb("total", [P, SEQ])
        gain = sb("gain", [P, KD])
        rs_all = ps("rs_all", [P, SEQ])
        ms = ps("ms", [P, BANK])
        x_in = [sem(f"x_in{b}") for b in range(NB)]
        spread, gained, scaled, x1_done, squared, summed, stored, ms_done, eps_added, rooted, rs_done = (sem(n) for n in (
            "spread", "gained", "scaled", "x1_done", "squared", "summed", "stored", "ms_done", "eps_added", "rooted", "rs_done"))
        block_ctx = ExitStack()
        block = block_ctx.enter_context(nc.Block())

        @block.sync
        def _(sp):
            for k in range(KD):
                if k >= NB:
                    sp.wait_ge(x1_done, k - NB + 1)
                sp.dma_start(r[:, k % NB, :], d["branch"][k]).then_inc(x_in[k % NB], 16)
                sp.dma_start(x[:, k % NB, :], d["x"][k]).then_inc(x_in[k % NB], 16)

        @block.tensor
        def _(pe):
            spread_rs(nc, core, rs_all).then_inc(spread, 1)
            pe.wait_ge(summed, KD)
            fold_mean_square(nc, core, ms, total).then_inc(ms_done, 1)

        @block.scalar
        def _(act):
            for k in range(KD):
                act.wait_ge(x1_done, k + 1)
                if k >= 2:
                    act.wait_ge(summed, k - 1)
                act.dma_start(d["x1"][k], x1[:, k, :]).then_inc(stored, 16)
                nc.scalar.activation(total[:, :] if k == 0 else sq[:, k % 2, :], x1[:, k, :], ACT.Square).then_inc(squared, 1)
            root_on_act(nc, core, act, eps_added, rooted)
            act.wait_ge(stored, 16 * KD)

        @block.gpsimd
        def _(pool):
            pool.wait_ge(squared, 1)
            pool.sem_inc(summed, 1)
            for k in range(1, KD):
                pool.wait_ge(squared, k + 1)
                pool.wait_ge(summed, k)
                nc.gpsimd.tensor_tensor(total[:, :], total[:, :], sq[:, k % 2, :], ALU.add).then_inc(summed, 1)

        @block.vector
        def _(dve):
            nc.vector.tensor_tensor(gain[:, :], core.mod[:, G_MIX:G_MIX + KD, 0], core.vec[:, VEC["mix_post"]:VEC["mix_post"] + KD], ALU.mult
                                    ).then_inc(gained, 1)
            dve.wait_ge(spread, 1)
            dve.wait_ge(gained, 1)
            for k in range(KD):
                b = k % NB
                dve.wait_ge(x_in[b], 32 * (k // NB) + 32)
                nc.vector.tensor_tensor(r[:, b, :], r[:, b, :], rs_all[:, :], ALU.mult).then_inc(scaled, 1)
                dve.wait_ge(scaled, k + 1)
                nc.vector.scalar_tensor_tensor(x1[:, k, :], r[:, b, :], gain[:, k:k + 1], x[:, b, :], ALU.mult, ALU.add).then_inc(x1_done, 1)
            rs_on_dve(nc, core, dve, ms, ms_done, eps_added, rooted, rs_done)

        block_ctx.close()
        clear(nc, sems)


def product(nc, out, w_hi, w_lo, x_hi, x_lo, first, last):
    nc.tensor.matmul(out, w_hi, x_hi, start=first, stop=False)
    nc.tensor.matmul(out, w_hi, x_lo, start=False, stop=False)
    return nc.tensor.matmul(out, w_lo, x_hi, start=False, stop=last)


def weight_splitter(nc, pool, i, b, count0, zero, w_in, w_raw, w_hi, w_lo, hi_done, w_ready, mm_done):
    pool.wait_ge(w_in[b], 16 * i + 16)
    pool.wait_ge(mm_done, 2 * i + b + 1 + count0)
    nc.gpsimd.tensor_tensor(w_hi[:, b, :, :], w_raw[:, b, :, :], zero, ALU.add).then_inc(hi_done, 1)
    pool.wait_ge(hi_done, 2 * i + b + 1)
    nc.gpsimd.tensor_tensor(w_lo[:, b, :, :], w_raw[:, b, :, :], w_hi[:, b, :, :].bitcast(F32), ALU.subtract).then_inc(w_ready, 1)


def projection_phase(nc, core, tag, w_d, segments, act_hi, act_lo, tokens, rotary=None, norm=None):
    vec = core.vec
    bank = min(BANK, tokens)
    kinds = [seg[0] for seg in segments]
    per_pair = "ffn" in kinds
    starts = [sum(seg[2] for seg in segments[:n]) for n in range(len(segments))]
    total_chunks = sum(seg[2] for seg in segments)
    rounds = total_chunks // 2
    with ExitStack() as ctx:
        sb, ps, sem, sems = scope(nc, ctx, tag)
        w_raw = sb("w_raw", [P, 2, KD, P])
        w_hi = sb("w_hi", [P, 2, KD, P], F32R)
        w_lo = sb("w_lo", [P, 2, KD, P], F32R)
        zero = sb("zero", [P, 1])
        zeros = zero[:, :].unsqueeze(1).broadcast_to((P, KD, P))
        q_bias = sb("q_bias", [P, KH]) if "query" in kinds else None
        n_out = 1 if per_pair else 2
        out = sb("out", [P, n_out, tokens])
        work = sb("work", [P, 2 if per_pair else 1, tokens]) if per_pair or "conv" in kinds else None
        acc = ps("acc", [P, 2, max(tokens, BANK)])
        if rotary:
            HALF = tokens // 2
            cos, sin = sb("cos", [P, 2, HALF]), sb("sin", [P, 2, HALF])
            qk, partner = sb("qk", [P, HALF]), sb("partner", [P, HALF])
            ROT_LOADS = 1 + 4
        rot_const, rot_in, rot_step, rot_done, rot_stored = (
            sem(n) for n in ("rot_const", "rot_in", "rot_step", "rot_done", "rot_stored")) if rotary else [None] * 5
        w_in = [sem(f"w_in{b}") for b in range(2)]
        stored = [sem(f"stored{b}") for b in range(n_out)]
        zeroed, q_scaled, hi_done, w_ready, mm_done, evac = (sem(n) for n in ("zeroed", "q_scaled", "hi_done", "w_ready", "mm_done", "evac"))
        act_out, conv_step, conv_done, gelu_done = (sem(n) for n in ("act_out", "conv_step", "conv_done", "gelu_done"))
        if norm:
            x_d, norm_w, shift, scale, x_on_chip = norm
            scratch = [out[:, 0, :]] + ([work[:, 0, :], work[:, 1, :]] if per_pair else [out[:, 1, :], work[:, 0, :]])
            NS = len(scratch)
            col = sb("col", [P, 3, KD])
            x_in = [sem(f"x_in{n}") for n in range(NS)]
            cols, spread, scaled, shifted, act_hi_done, act_lo_done = (
                sem(n) for n in ("cols", "spread", "scaled", "shifted", "act_hi_done", "act_lo_done"))
        block_ctx = ExitStack()
        block = block_ctx.enter_context(nc.Block())

        @block.sync
        def _(sp):
            for s in stored:
                sp.sem_inc(s, 16)
            for b in range(2):
                sp.dma_start(w_raw[:, b, :, :], w_d[segments[0][1] + b]).then_inc(w_in[b], 16)
            if norm and not x_on_chip:
                for k in range(KD):
                    if k >= NS:
                        sp.wait_ge(act_lo_done, k - NS + 1)
                    sp.dma_start(scratch[k % NS], x_d[k]).then_inc(x_in[k % NS], 16)

            def rot_load(i, b):
                sp.wait_ge(rot_stored, 32 * i + (16 * b + 16))
                at = slice(HALF * b, HALF * (b + 1))
                sp.dma_start(qk[:, :], rotary[1][ds(i, 1), :, at].rearrange("a p t -> (a p) t")).then_inc(rot_in, 16)
                for blk in range(4):
                    row = 32 * (blk ^ 1)
                    sp.dma_start(partner[32 * blk:32 * blk + 32, :], rotary[1][ds(i, 1), row:row + 32, at].rearrange("a p t -> (a p) t")
                                 ).then_inc(rot_in, 16)

            def rot_store(i, b):
                sp.wait_ge(rot_done, 2 * i + b + 1)
                sp.dma_start(rotary[0][ds(i, 1), :, HALF * b:HALF * (b + 1)].rearrange("a p t -> (a p) t"), qk[:, :]).then_inc(rot_stored, 16)

            if rotary:
                sp.dma_start(cos[:, :, :], core.d["cos"]).then_inc(rot_const, 16)
                sp.dma_start(sin[:, :, :], core.d["sin"]).then_inc(rot_const, 16)
                sp.sem_inc(rot_stored, 16)

            def chunk(start, kind, out_d, i, b, source):
                c = 2 * i + b + start
                if source is not None:
                    sp.wait_ge(w_ready, c + 1)
                    sp.dma_start(w_raw[:, b, :, :], w_d[ds(source, 1)].rearrange("a p k n -> (a p) k n")).then_inc(w_in[b], 16)
                if kind == "ffn":
                    if b == 0:
                        return
                    sp.wait_ge(conv_done, i + 2)
                    sp.dma_start(out_d[ds(i, 1)].rearrange("a p t -> (a p) t"), out[:, 0, :]).then_inc(stored[0], 16)
                    return
                rotate = rotary and kind == "sigmoid"
                if rotate:
                    rot_load(i, b)
                if kind == "conv":
                    sp.wait_ge(conv_done, 2 * i + b + 2)
                else:
                    sp.wait_ge(evac, c + 3)
                sp.dma_start(out_d[ds(2 * i + b, 1)].rearrange("a p t -> (a p) t"), out[:, b, :]).then_inc(stored[b], 16)
                if rotate:
                    rot_store(i, b)

            for n, (kind, first, count, out_d, _bias) in enumerate(segments):
                if rotary and kind == "sigmoid":
                    for b in range(2):
                        sp.wait_ge(stored[b], 8 * starts[n] + 16)
                if count > 2:
                    with sp.Fori(0, count // 2 - 1) as i:
                        for b in range(2):
                            chunk(starts[n], kind, out_d, i, b, 2 * i + (first + b + 2))
                for b in range(2):
                    nxt = segments[n + 1][1] + b if n + 1 < len(segments) else None
                    chunk(starts[n], kind, out_d, count // 2 - 1, b, nxt)
            for s in stored:
                sp.wait_ge(s, 16 * (rounds + 1))
            if rotary:
                sp.wait_ge(rot_stored, 16 * 17)

        @block.gpsimd
        def _(pool):
            pool.memset(zero[:, :], 0.0).then_inc(zeroed, 1)
            pool.wait_ge(zeroed, 1)
            plain_rounds = starts[kinds.index("sigmoid")] // 2 if rotary else rounds
            with pool.Fori(0, plain_rounds) as i:
                for b in range(2):
                    weight_splitter(nc, pool, i, b, 0, zeros, w_in, w_raw, w_hi, w_lo, hi_done, w_ready, mm_done)
            if rotary:
                pool.wait_ge(rot_const, 32)
                tt = nc.gpsimd.tensor_tensor

                def split(i, b):
                    weight_splitter(nc, pool, i + plain_rounds, b, 0, zeros, w_in, w_raw, w_hi, w_lo, hi_done, w_ready, mm_done)

                def rotate(u, b):
                    pool.wait_ge(rot_in, (16 * ROT_LOADS) * u + 16 * ROT_LOADS)
                    tt(qk[:, :], qk[:, :], cos[:, b, :], ALU.mult).then_inc(rot_step, 1)
                    tt(partner[:, :], partner[:, :], sin[:, b, :], ALU.mult).then_inc(rot_step, 1)
                    pool.wait_ge(rot_step, 2 * u + 2)
                    tt(qk[:, :], qk[:, :], partner[:, :], ALU.add).then_inc(rot_done, 1)

                split(0, 0)
                with pool.Fori(0, rounds - plain_rounds - 1) as i:
                    split(i, 1)
                    rotate(2 * i, 0)
                    split(i + 1, 0)
                    rotate(2 * i + 1, 1)
                last = rounds - plain_rounds - 1
                split(last, 1)
                rotate(2 * last, 0)
                rotate(2 * last + 1, 1)

        @block.tensor
        def _(pe):
            def chunk(i, b):
                pe.wait_ge(w_ready, 2 * i + b + 1)
                pe.wait_ge(evac, 2 * i + b + 1)
                for g in range(tokens // bank):
                    at = slice(bank * g, bank * (g + 1))
                    for k in range(KD):
                        last = product(nc, acc[:, b, at], w_hi[:, b, k, :], w_lo[:, b, k, :],
                                       act_hi[:, k, at], act_lo[:, k, at], k == 0, k == KD - 1)
                last.then_inc(mm_done, 1)

            pe.sem_inc(mm_done, 2)
            if norm:
                spread_rs(nc, core, acc[:, 1, :]).then_inc(spread, 1)
                pe.wait_ge(w_ready, 1)
                pe.wait_ge(evac, 1)
                for k in range(KD):
                    pe.wait_ge(act_lo_done, k + 1)
                    for g in range(tokens // bank):
                        at = slice(bank * g, bank * (g + 1))
                        last = product(nc, acc[:, 0, at], w_hi[:, 0, k, :], w_lo[:, 0, k, :],
                                       act_hi[:, k, at], act_lo[:, k, at], k == 0, k == KD - 1)
                last.then_inc(mm_done, 1)
                chunk(0, 1)
            with pe.Fori(1 if norm else 0, rounds) as i:
                for b in range(2):
                    chunk(i, b)
        @block.scalar
        def _(act):
            if not per_pair:
                act.sem_inc(evac, 2)
            if norm:
                act.wait_ge(cols, 3)
                for k in range(KD):
                    t = scratch[k % NS]
                    act.wait_ge(scaled, k + 1)
                    nc.scalar.activation(t, t, ACT.Identity, bias=col[:, 1, k:k + 1], scale=col[:, 0, k:k + 1]).then_inc(shifted, 1)
                    act.wait_ge(shifted, k + 1)
                    nc.scalar.activation(act_hi[:, k, :], t, ACT.Copy).then_inc(act_hi_done, 1)
            if "query" in kinds:
                act.wait_ge(q_scaled, 1)
            for n, (kind, first, count, out_d, bias) in enumerate(segments):
                with act.Fori(0, count // 2) as i:
                    for b in range(2):
                        m = 2 * i + b
                        act.wait_ge(mm_done, m + starts[n] + 3)
                        if kind in ("bias", "sigmoid", "query"):
                            act.wait_ge(stored[b], 16 * i + (8 * starts[n] + 16))
                        if kind in ("bias", "sigmoid"):
                            nc.scalar.activation(out[:, b, :], acc[:, b, 0:tokens], ACT.Sigmoid if kind == "sigmoid" else ACT.Identity,
                                                 bias=vec[:, ds(m + bias, 1)]).then_inc(evac, 1)
                        elif kind == "query":
                            nc.scalar.activation(out[:, b, :], acc[:, b, 0:tokens], ACT.Identity, bias=q_bias[:, ds(m, 1)],
                                                 scale=HEAD_DIM ** -0.5).then_inc(evac, 1)
                        elif kind == "conv":
                            act.wait_ge(conv_done, m + 1)
                            nc.scalar.activation(work[:, 0, :], acc[:, b, :], ACT.Identity, bias=vec[:, ds(m + bias, 1)]).then_inc(evac, 1)
                        else:
                            act.wait_ge(conv_done, i + 1)
                            nc.scalar.activation(work[:, b, :], acc[:, b, :], ACT.Identity, bias=vec[:, ds(m + VEC["ff_b"], 1)],
                                                 scale=vec[:, ds(m + VEC["ff_w1"], 1)]).then_inc(act_out, 1)
                            if b == 0:
                                act.wait_ge(evac, m + 3)
                                nc.scalar.activation(work[:, 0, :], work[:, 0, :], ACT.Gelu_apprx_tanh).then_inc(gelu_done, 1)

        @block.vector
        def _(dve):
            if norm:
                nc.vector.tensor_scalar(col[:, 2, :], core.mod[:, scale:scale + KD, 0], 1.0, None, ALU.add).then_inc(cols, 1)
                dve.wait_ge(cols, 1)
                nc.vector.tensor_tensor(col[:, 0, :], col[:, 2, :], vec[:, norm_w:norm_w + KD], ALU.mult).then_inc(cols, 1)
                nc.vector.tensor_copy(col[:, 1, :], core.mod[:, shift:shift + KD, 0]).then_inc(cols, 1)

                def scale_chunk(k):
                    t = scratch[k % NS]
                    if x_on_chip:
                        x = x_d[:, k, :]
                    else:
                        x = t
                        dve.wait_ge(x_in[k % NS], 16 * (k // NS) + 16)
                    nc.vector.tensor_tensor(t, x, acc[:, 1, :], ALU.mult).then_inc(scaled, 1)

                dve.wait_ge(spread, 1)
                scale_chunk(0)
                for k in range(KD):
                    if k + 1 < KD:
                        if k + 1 >= NS:
                            dve.wait_ge(act_lo_done, k + 2 - NS)
                        scale_chunk(k + 1)
                    dve.wait_ge(act_hi_done, k + 1)
                    if x_on_chip:
                        dve.wait_ge(scaled, k + 1)
                    nc.vector.tensor_tensor(act_lo[:, k, :], scratch[k % NS], act_hi[:, k, :].bitcast(F32), ALU.subtract).then_inc(act_lo_done, 1)
            if "query" in kinds:
                bias = segments[kinds.index("query")][4]
                nc.vector.tensor_scalar(q_bias[:, :], vec[:, bias:bias + KH], HEAD_DIM ** -0.5, None, ALU.mult).then_inc(q_scaled, 1)
            if "conv" in kinds:
                start, count = starts[kinds.index("conv")], segments[kinds.index("conv")][2]
                dve.sem_inc(conv_done, 1)
                with dve.Fori(0, count // 2) as i:
                    for b in range(2):
                        m = 2 * i + b
                        o, u = out[:, b, :], work[:, 0, :]
                        dve.wait_ge(evac, m + start + 3)
                        dve.wait_ge(stored[b], 16 * i + (8 * start + 16))
                        nc.vector.tensor_scalar(o, u, vec[:, ds(m + VEC["hy_w1"], 1)], vec[:, ds(m + VEC["hy_b"], 1)], ALU.mult, ALU.add
                                                ).then_inc(conv_step, 1)
                        dve.wait_ge(conv_step, 2 * m + 1)
                        nc.vector.scalar_tensor_tensor(o[:, 1:], u[:, :-1], vec[:, ds(m + VEC["hy_w0"], 1)], o[:, 1:], ALU.mult, ALU.add
                                                       ).then_inc(conv_step, 1)
                        dve.wait_ge(conv_step, 2 * m + 2)
                        nc.vector.scalar_tensor_tensor(o[:, :-1], u[:, 1:], vec[:, ds(m + VEC["hy_w2"], 1)], o[:, :-1], ALU.mult, ALU.add
                                                       ).then_inc(conv_done, 1)
            if per_pair:
                dve.sem_inc(evac, 2)
                dve.sem_inc(conv_done, 1)
                with dve.Fori(0, rounds) as i:
                    for b in range(2):
                        c = 2 * i + b
                        o, u = work[:, b, :], acc[:, b, :]
                        dve.wait_ge(act_out, c + 1)
                        nc.vector.scalar_tensor_tensor(o[:, 1:], u[:, :-1], vec[:, ds(c + VEC["ff_w0"], 1)], o[:, 1:], ALU.mult, ALU.add
                                                       ).then_inc(conv_step, 1)
                        dve.wait_ge(conv_step, c + 1)
                        nc.vector.scalar_tensor_tensor(o[:, :-1], u[:, 1:], vec[:, ds(c + VEC["ff_w2"], 1)], o[:, :-1], ALU.mult, ALU.add
                                                       ).then_inc(evac, 1)
                    dve.wait_ge(gelu_done, i + 1)
                    dve.wait_ge(evac, 2 * i + 4)
                    dve.wait_ge(stored[0], 16 * i + 16)
                    nc.vector.tensor_tensor(out[:, 0, :], work[:, 0, :], work[:, 1, :], ALU.mult).then_inc(conv_done, 1)

        block_ctx.close()
        clear(nc, sems)


def attention_phase(nc, core):
    d = core.d
    PAIRS = ROWS // 2
    BLOCKS = PAIRS // 2
    NB = (WIN_ROWS + 1) * GRID_W
    EDGE = WIN_ROWS * GRID_W
    CX = CTX_LEN
    CXT = CX // P
    TAB = 14 * GRID_W
    TILES = SEQ // P
    E_BUFS = 4
    UNITS = 2 * PAIRS

    def window(p):
        if p < 2:
            return EDGE, 0, (6 - 2 * p) * GRID_W
        if p >= PAIRS - 2:
            return EDGE, ROWS - WIN_ROWS, (2 - 2 * (p - PAIRS + 2)) * GRID_W
        return NB, 2 * p - WIN_ROWS // 2, None

    def slots(m):
        if m in (0, BLOCKS - 1):
            row = window(2 * m)[1]
            nb = [(3 + i, row // 2 + i) for i in range(4)]
        else:
            nb = [(2 + i, 2 * m - 2 + i) for i in range(6)]
        return [(0, TILES), (1, TILES + 1)] + nb

    with ExitStack() as ctx:
        sb, ps, sem, sems = scope(nc, ctx, "att")
        colmask = sb("colmask", [P, GRID_W])
        fold = sb("fold", [P, HEAD_DIM])
        zero = sb("zero", [P, 1])
        q, qr, k = (sb(n, [P, SEQ]) for n in ("q", "qr", "k"))
        kx = sb("kx", [P, CX])
        v, vx = sb("v", [P, SEQ]), sb("vx", [P, CX])
        q_rot, q_plain = sb("q_rot", [P, 2, SEQ], F32R), sb("q_plain", [P, 2, SEQ], F32R)
        k_hh, k_ll = sb("k_hh", [P, 2, SEQ], F32R), sb("k_ll", [P, 2, SEQ], F32R)
        kx_hh, kx_ll = sb("kx_hh", [P, 2, CX], F32R), sb("kx_ll", [P, 2, CX], F32R)
        table = sb("table", [P, 2, TAB])
        inner = sb("inner", [P, 2, CX + NB])
        vt = sb("vt", [P, TILES + CXT, 2, 2, HEAD_DIM], F32R)
        e = sb("e", [P, E_BUFS, 7 * P])
        pt_hi, pt_lo = sb("pt_hi", [P, 2, 8, 2 * P], F32R), sb("pt_lo", [P, 2, 8, 2 * P], F32R)
        stat = sb("stat", [P, E_BUFS, 8])
        o_sb = sb("o_sb", [P, 2 * P])
        y = sb("y", [HEAD_DIM, 2, 2 * P])
        s_ps = ps("s_ps", [P, 2, 2 * BANK])
        t_ps = ps("t_ps", [P, 2, BANK])
        o_ps = ps("o_ps", [P, BANK])
        y_ps = ps("y_ps", [P, BANK])

        const_in, loaded, v_in, zeroed = sem("const_in"), sem("loaded"), sem("v_in"), sem("zeroed")
        step, prepared, raw_used, head_done = sem("step"), sem("prepared"), sem("raw_used"), sem("head_done")
        v_flip, v_hi, v_lo, inner_ready = sem("v_flip"), sem("v_hi"), sem("v_lo"), sem("inner_ready")
        scores, row_max, logits, neg_max, exp_done, sums, inverse, normed = (
            sem(n) for n in ("scores", "row_max", "logits", "neg_max", "exp_done", "sums", "inverse", "normed"))
        flip_a, flip_b, hi_a, hi_b, lo_a, lo_b = (sem(n) for n in ("flip_a", "flip_b", "hi_a", "hi_b", "lo_a", "lo_b"))
        pv, o_out, y_mm, y_out = sem("pv"), sem("o_out"), sem("y_mm"), sem("y_out")
        stored = [sem(f"stored{b}") for b in range(2)]
        LOADS = 4 * 2 + 1
        V_GROUPS = -(-(TILES + CXT) // 4)
        STEPS_P = 7
        block_ctx = ExitStack()
        block = block_ctx.enter_context(nc.Block())

        def head(j, hb):
            return 2 * j + hb

        def tile_groups():
            return [(g, 4 * g, min(4, TILES + CXT - 4 * g)) for g in range(V_GROUPS)]

        def v_bank(g):
            return s_ps[:, g % 4 // 2, ds(BANK * (g % 2), BANK)]

        @block.sync
        def _(sp):
            sp.dma_start(colmask[:, :], d["colmask"]).then_inc(const_in, 16)
            sp.dma_start(fold[:, :], d["fold"]).then_inc(const_in, 16)
            with sp.Fori(0, N_HEADS // 2) as j:
                for hb in range(2):
                    if hb == 0:
                        sp.wait_ge(v_flip, V_GROUPS * j + 1)
                        sp.dma_start(v[:, :], d["proj"][ds(j + V0, 1)].rearrange("a p t -> (a p) t")).then_inc(v_in, 16)
                        sp.dma_start(vx[:, :], d["ctx_kv"][ds(j + KH, 1)].rearrange("a p t -> (a p) t")).then_inc(v_in, 16)
                    sp.wait_ge(raw_used, head(j, hb) + 1)
                    for half in range(2):
                        at = 64 * half
                        for dst, src, c in ((q, "proj", Q0), (qr, "rotated", Q0), (k, "rotated", K0)):
                            sp.dma_start(dst[at:at + 64, :], d[src][ds(j + c, 1), 64 * hb:64 * hb + 64, :].rearrange("a p t -> (a p) t")
                                         ).then_inc(loaded, 16)
                        sp.dma_start(kx[at:at + 64, :], d["ctx_kv"][ds(j, 1), 64 * hb:64 * hb + 64, :].rearrange("a p t -> (a p) t")
                                     ).then_inc(loaded, 16)
                    sp.wait_ge(head_done, head(j, hb) + 1)
                    sp.dma_start(table[:, hb, :], d["rpb"][ds(2 * j + hb, 1)].rearrange("h p t -> (h p) t")).then_inc(loaded, 16)
            for b in range(2):
                sp.wait_ge(stored[b], 16 * (N_HEADS * BLOCKS // 2 + 1))

        @block.gpsimd
        def _(pool):
            nc.gpsimd.memset(zero[:, :], 0.0).then_inc(zeroed, 1)
            nc.gpsimd.memset(inner[:, :, 0:CX], 0.0).then_inc(zeroed, 1)
            nc.gpsimd.memset(e[:, :, CX + NB:7 * P], 0.0).then_inc(zeroed, 1)
            for pt in (pt_hi, pt_lo):
                nc.gpsimd.memset(pt[:, :, 7, 0:P].bitcast(F32), 0.0).then_inc(zeroed, 1)
                nc.gpsimd.memset(pt[:, :, 2, P:2 * P].bitcast(F32), 0.0).then_inc(zeroed, 1)
            pool.sem_inc(raw_used, 1)
            pool.wait_ge(const_in, 32)
            pool.wait_ge(zeroed, 7)
            tt = nc.gpsimd.tensor_tensor
            wide = zero[:, :].broadcast_to((P, SEQ))
            mask = colmask[:, :].unsqueeze(1).broadcast_to((P, TAB // GRID_W, GRID_W))
            low = slice(64, 128)
            with pool.Fori(0, N_HEADS // 2) as j:
                for hb in range(2):
                    base = STEPS_P * head(j, hb)
                    pool.wait_ge(head_done, head(j, hb) + 1)
                    pool.wait_ge(loaded, (16 * LOADS) * head(j, hb) + 16 * LOADS)
                    tab = table[:, hb, :].rearrange("p (r c) -> p r c", c=GRID_W)
                    tt(tab, tab, mask, ALU.add).then_inc(step, 1)
                    for hi, raw in ((kx_hh, kx), (q_plain, q), (q_rot, qr), (k_hh, k)):
                        tt(hi[:, hb, :], raw[:, :], wide[:, 0:raw.shape[1]], ALU.add).then_inc(step, 1)
                    pool.wait_ge(step, base + 5)
                    tt(kx_ll[:, hb, :], kx[:, :], kx_hh[:, hb, :].bitcast(F32), ALU.subtract).then_inc(step, 1)
                    tt(k_ll[:, hb, :], k[:, :], k_hh[:, hb, :].bitcast(F32), ALU.subtract).then_inc(step, 1)
                    pool.wait_ge(step, base + 7)
                    tt(q_plain[low, hb, :], q[low, :], q_plain[low, hb, :].bitcast(F32), ALU.subtract)
                    tt(q_rot[low, hb, :], qr[low, :], q_rot[low, hb, :].bitcast(F32), ALU.subtract).then_inc(prepared, 1)
                    pool.wait_ge(prepared, head(j, hb) + 1)
                    pool.sem_inc(raw_used, 1)

        @block.tensor
        def _(pe):
            def score(j, u):
                hb, s = divmod(u, PAIRS)
                nk, row, _ = window(s)
                if u >= 2:
                    pe.wait_ge(exp_done, UNITS * j + u - 1)
                out, at = s_ps[:, u % 2, :], ds(P * s, P)
                nc.tensor.matmul(out[:, 0:CX], q_plain[:, hb, at], kx_hh[:, hb, :], start=True, stop=False)
                nc.tensor.matmul(out[:, 0:CX], q_plain[:, hb, at], kx_ll[:, hb, :], start=False, stop=True)
                for lo, n in ((0, CX), (CX, nk - CX)):
                    keys, to = ds(GRID_W * row + lo, n), out[:, CX + lo:CX + lo + n]
                    nc.tensor.matmul(to, q_rot[:, hb, at], k_hh[:, hb, keys], start=True, stop=False)
                    last = nc.tensor.matmul(to, q_rot[:, hb, at], k_ll[:, hb, keys], start=False, stop=True)
                last.then_inc(scores, 1)

            def flip(j, u):
                nk = window(u % PAIRS)[0]
                pe.wait_ge(normed, UNITS * j + u + 1)
                if u >= 1:
                    pe.wait_ge(lo_a, UNITS * j + u)
                for t in range(4):
                    last = nc.tensor.transpose(t_ps[:, 0, ds(P * t, P)], e[:, u % E_BUFS, ds(P * t, P)], core.ident[:, :])
                last.then_inc(flip_a, 1)
                if u >= 1:
                    pe.wait_ge(lo_b, UNITS * j + u)
                for t in range(4, 7 if nk == NB else 6):
                    last = nc.tensor.transpose(t_ps[:, 1, ds(P * (t - 4), P)], e[:, u % E_BUFS, ds(P * t, P)], core.ident[:, :])
                last.then_inc(flip_b, 1)

            def values(j, m):
                pe.wait_ge(lo_a, UNITS * j + 2 * m + 2)
                pe.wait_ge(lo_b, UNITS * j + 2 * m + 2)
                if m >= 1:
                    pe.wait_ge(o_out, (2 * BLOCKS) * j + m)
                hb, todo = m // BLOCKS, slots(m % BLOCKS)
                for n, (slot, tile) in enumerate(todo):
                    w = vt[:, tile, hb, :, :].rearrange("p a c -> p (a c)")
                    nc.tensor.matmul(o_ps[:, 0:2 * P], w, pt_hi[:, m % 2, slot, :], start=(n == 0), stop=False)
                    last = nc.tensor.matmul(o_ps[:, 0:2 * P], w, pt_lo[:, m % 2, slot, :], start=False, stop=(n == len(todo) - 1))
                last.then_inc(pv, 1)

            def fold_halves(j, m):
                pe.wait_ge(o_out, (2 * BLOCKS) * j + m + 1)
                if m >= 1:
                    pe.wait_ge(y_out, (2 * BLOCKS) * j + m)
                nc.tensor.matmul(y_ps[0:HEAD_DIM, 0:2 * P], fold[:, :], o_sb[:, :], start=True, stop=True).then_inc(y_mm, 1)

            pe.sem_inc(v_flip, 1)
            pe.wait_ge(const_in, 32)
            pe.wait_ge(zeroed, 7)
            with pe.Fori(0, N_HEADS // 2) as j:
                pe.wait_ge(v_in, 32 * j + 32)
                for g, first, n in tile_groups():
                    if g >= 4:
                        pe.wait_ge(v_lo, V_GROUPS * j + g - 3)
                    for t in range(first, first + n):
                        src = v[:, ds(P * t, P)] if t < TILES else vx[:, ds(P * (t - TILES), P)]
                        last = nc.tensor.transpose(v_bank(g)[:, ds(P * (t - first), P)], src, core.ident[:, :])
                    last.then_inc(v_flip, 1)
                pe.wait_ge(v_lo, V_GROUPS * j + V_GROUPS)
                for t in range(UNITS + 4):
                    if t in (0, PAIRS):
                        pe.wait_ge(prepared, head(j, t // PAIRS) + 1)
                    if t < UNITS:
                        score(j, t)
                    if 2 <= t < UNITS + 2:
                        flip(j, t - 2)
                    if t >= 4 and t % 2 == 0:
                        values(j, (t - 4) // 2)
                    if t >= 5 and t % 2:
                        fold_halves(j, (t - 5) // 2)

        def dest(pt, m, a, nk, bank):
            cols = slice(P * a, P * a + P)
            buf = pt[:, m % 2, :, :]
            if nk == NB and a == 0:
                return buf[:, 0:4, cols] if bank == 0 else buf[:, 4:7, cols]
            if bank == 0:
                return buf[:, 0:6, cols].rearrange("p (x c) q -> p x c q", c=3)[:, :, 0:2, :]
            return buf[:, 5:8, cols] if nk == NB else buf[:, 5:7, cols]

        def source(nk, a, bank):
            if bank == 0:
                t = t_ps[:, 0, :].rearrange("p (c q) -> p c q", q=P)
                return t if nk == NB and a == 0 else t_ps[:, 0, :].rearrange("p (x c q) -> p x c q", c=2, q=P)
            n = 3 if nk == NB else 2
            return t_ps[:, 1, 0:n * P].rearrange("p (c q) -> p c q", q=P)

        @block.scalar
        def _(act):
            def hi(j, u, bank):
                m, a = divmod(u, 2)
                nk = window(u % PAIRS)[0]
                if bank == 0 and a == 0 and m >= 2:
                    act.wait_ge(pv, (2 * BLOCKS) * j + m - 1)
                act.wait_ge((flip_a, flip_b)[bank], UNITS * j + u + 1)
                nc.scalar.activation(dest(pt_hi, m, a, nk, bank), source(nk, a, bank), ACT.Copy).then_inc((hi_a, hi_b)[bank], 1)

            def exps(j, u):
                nk, _, col = window(u % PAIRS)
                st, ee, b = stat[:, u % E_BUFS, :], e[:, u % E_BUFS, :], u % 2
                act.wait_ge(neg_max, UNITS * j + u + 1)
                if col is None:
                    nc.scalar.activation(ee[:, 0:CX + nk], ee[:, 0:CX + nk], ACT.Exp, bias=st[:, 2:3], accum_out=st[:, 5:6]).then_inc(exp_done, 1)
                else:
                    nc.scalar.activation(ee[:, 0:CX], s_ps[:, b, 0:CX], ACT.Exp, bias=st[:, 2:3], accum_out=st[:, 3:4])
                    nc.scalar.activation(ee[:, CX:CX + nk], ee[:, CX:CX + nk], ACT.Exp, bias=st[:, 2:3], accum_out=st[:, 4:5]).then_inc(exp_done, 1)

            act.sem_inc(head_done, 2)
            for b in range(2):
                act.sem_inc(stored[b], 16)
            with act.Fori(0, N_HEADS // 2) as j:
                for g, first, n in tile_groups():
                    act.wait_ge(v_flip, V_GROUPS * j + g + 2)
                    act_in = v_bank(g)[:, 0:P * n].rearrange("p (t h c) -> p t h c", h=2, c=HEAD_DIM)
                    nc.scalar.activation(vt[:, first:first + n, :, 0, :], act_in, ACT.Copy).then_inc(v_hi, 1)
                for t in range(UNITS + 4):
                    if 2 <= t < UNITS + 2:
                        hi(j, t - 2, 0)
                        hi(j, t - 2, 1)
                    if t < UNITS:
                        exps(j, t)
                    if t % PAIRS == PAIRS - 1 and t < UNITS:
                        act.sem_inc(head_done, 1)
                    if t >= 4 and t % 2 == 0:
                        act.wait_ge(pv, (2 * BLOCKS) * j + (t - 4) // 2 + 1)
                        nc.scalar.activation(o_sb[:, :], o_ps[:, 0:2 * P], ACT.Copy).then_inc(o_out, 1)
                    if t >= 5 and t % 2:
                        m = (t - 5) // 2
                        act.wait_ge(y_mm, (2 * BLOCKS) * j + m + 1)
                        act.wait_ge(stored[m % 2], (16 * BLOCKS) * j + 16 * (m // 2) + 16)
                        nc.scalar.activation(y[:, m % 2, :], y_ps[0:HEAD_DIM, 0:2 * P], ACT.Copy).then_inc(y_out, 1)
                        act.wait_ge(y_out, (2 * BLOCKS) * j + m + 1)
                        hb, at = 64 * (m // BLOCKS), 2 * P * (m % BLOCKS)
                        act.dma_start(d["branches"][ds(j, 1), hb:hb + 64, at:at + 2 * P].rearrange("a p t -> (a p) t"), y[:, m % 2, :]
                                      ).then_inc(stored[m % 2], 16)

        @block.vector
        def _(dve):
            def edge(j, u):
                hb, s = divmod(u, PAIRS)
                return 8 * j + 4 * hb + (s if s < 2 else s - PAIRS + 4) + 1

            def logit(j, u):
                hb, s = divmod(u, PAIRS)
                nk, _, col = window(s)
                st, ee, b = stat[:, u % E_BUFS, :], e[:, u % E_BUFS, :], u % 2
                dve.wait_ge(scores, UNITS * j + u + 1)
                if u >= E_BUFS:
                    dve.wait_ge(flip_b, UNITS * j + u - E_BUFS + 1)
                if col is None:
                    nc.vector.memset(st[:, 7:8], 0.0)
                    nc.vector.tensor_tensor_reduce(out=ee[:, 0:CX + nk], in0=s_ps[:, b, 0:CX + nk], in1=inner[:, hb, :], scale=1.0,
                                                   scalar=MASKED, op0=ALU.add, op1=ALU.max, accum_out=st[:, 1:2]).then_inc(logits, 1)
                    dve.wait_ge(logits, UNITS * j + u + 1)
                    nc.vector.tensor_scalar(st[:, 2:3], st[:, 1:2], -1.0, None, ALU.mult).then_inc(neg_max, 1)
                else:
                    nc.vector.reduce_max(st[:, 0:1], s_ps[:, b, 0:CX], AX.X).then_inc(row_max, 1)
                    nc.vector.tensor_tensor_reduce(out=ee[:, CX:CX + nk], in0=s_ps[:, b, CX:CX + nk], in1=table[:, hb, ds(col, nk)], scale=1.0,
                                                   scalar=MASKED, op0=ALU.add, op1=ALU.max, accum_out=st[:, 1:2]).then_inc(logits, 1)
                    dve.wait_ge(row_max, edge(j, u))
                    dve.wait_ge(logits, UNITS * j + u + 1)
                    nc.vector.tensor_scalar(st[:, 2:3], st[:, 1:2], st[:, 0:1], -1.0, ALU.max, ALU.mult).then_inc(neg_max, 1)

            def normalise(j, u):
                nk, _, col = window(u % PAIRS)
                st, ee = stat[:, u % E_BUFS, :], e[:, u % E_BUFS, :]
                dve.wait_ge(exp_done, UNITS * j + u + 1)
                if col is not None:
                    nc.vector.tensor_tensor(st[:, 5:6], st[:, 3:4], st[:, 4:5], ALU.add).then_inc(sums, 1)
                    dve.wait_ge(sums, edge(j, u))
                nc.vector.reciprocal(st[:, 6:7], st[:, 5:6]).then_inc(inverse, 1)
                dve.wait_ge(inverse, UNITS * j + u + 1)
                nc.vector.tensor_scalar(ee[:, 0:CX + nk], ee[:, 0:CX + nk], st[:, 6:7], None, ALU.mult).then_inc(normed, 1)

            def lo(j, u, bank):
                m, a = divmod(u, 2)
                nk = window(u % PAIRS)[0]
                dve.wait_ge((hi_a, hi_b)[bank], UNITS * j + u + 1)
                nc.vector.tensor_tensor(dest(pt_lo, m, a, nk, bank), source(nk, a, bank), dest(pt_hi, m, a, nk, bank).bitcast(F32), ALU.subtract
                                        ).then_inc((lo_a, lo_b)[bank], 1)

            dve.wait_ge(zeroed, 7)
            with dve.Fori(0, N_HEADS // 2) as j:
                for g, first, n in tile_groups():
                    dve.wait_ge(v_hi, V_GROUPS * j + g + 1)
                    nc.vector.tensor_tensor(vt[:, first:first + n, :, 1, :], v_bank(g)[:, 0:P * n].rearrange("p (t h c) -> p t h c", h=2, c=HEAD_DIM),
                                            vt[:, first:first + n, :, 0, :].bitcast(F32), ALU.subtract).then_inc(v_lo, 1)
                for t in range(UNITS + 2):
                    if t % PAIRS == 0 and t < UNITS:
                        hb = t // PAIRS
                        dve.wait_ge(prepared, head(j, hb) + 1)
                        nc.vector.tensor_copy(inner[:, hb, CX:CX + NB], table[:, hb, 2 * GRID_W:2 * GRID_W + NB]).then_inc(inner_ready, 1)
                        dve.wait_ge(inner_ready, 3 * head(j, hb) + 1)
                        nc.vector.memset(inner[0:64, hb, CX + NB - GRID_W:CX + NB], MASKED).then_inc(inner_ready, 1)
                        nc.vector.memset(inner[64:128, hb, CX:CX + GRID_W], MASKED).then_inc(inner_ready, 1)
                        dve.wait_ge(inner_ready, 3 * head(j, hb) + 3)
                    if t < UNITS:
                        logit(j, t)
                    if t >= 2:
                        lo(j, t - 2, 0)
                    if 1 <= t < UNITS + 1:
                        normalise(j, t - 1)
                    if t >= 2:
                        lo(j, t - 2, 1)

        block_ctx.close()
        clear(nc, sems)


def hyena_phase(nc, core):
    d = core.d
    with ExitStack() as ctx:
        sb, ps, sem, sems = scope(nc, ctx, "hy")
        x1 = sb("x1", [P, KH, SEQ])
        vv = sb("vv", [P, KH, SEQ])
        dft = sb("dft", [P, 2, P])
        idft = sb("idft", [P, R])
        ua = sb("ua", [P, 2, KH, P])
        ut = sb("ut", [P, 2, D_HYENA])
        spec = sb("spec", [P, 2, 2, D_HYENA])
        const_in, u_in, u_ready, skip_done = sem("const_in"), sem("u_in"), sem("u_ready"), sem("skip_done")
        ua_ready, flip, ut_ready, s1_mm, s1_out = (sem(n) for n in ("ua_ready", "flip", "ut_ready", "s1_mm", "s1_out"))
        s1_stored = [sem(f"s1_stored{b}") for b in range(2)]
        with ExitStack() as inner_ctx:
            ps1 = inner_ctx.enter_context(nc.psum_tensor("hy_flip_ps", [P, 2, BANK], F32))
            ps2 = inner_ctx.enter_context(nc.psum_tensor("hy_s1_ps", [P, 2, 2, BANK], F32))
            block_ctx = ExitStack()
            block = block_ctx.enter_context(nc.Block())
            TILES = R // 4

            @block.sync
            def _(sp):
                sp.dma_start(dft[:, :, :], d["dft_u"]).then_inc(const_in, 16)
                sp.dma_start(idft[:, :], d["idft"]).then_inc(const_in, 16)
                for q in range(KH):
                    sp.dma_start(x1[:, q, :], d["proj"][HY0 + KH + q]).then_inc(u_in, 16)
                    sp.dma_start(vv[:, q, :], d["proj"][HY0 + 2 * KH + q]).then_inc(u_in, 16)
                for b in range(2):
                    sp.sem_inc(s1_stored[b], 16)
                with sp.Fori(0, TILES // 2) as i:
                    for b in range(2):
                        sp.wait_ge(s1_out, 2 * i + b + 1)
                        for h in range(2):
                            sp.dma_start(d["spec_u"][ds(8 * i + 4 * b + 2 * h, 2)].rearrange("g r c -> (g r) c"),
                                         spec[:, b, h, :]).then_inc(s1_stored[b], 16)
                for b in range(2):
                    sp.wait_ge(s1_stored[b], 16 + 32 * (TILES // 2))

            @block.vector
            def _(dve):
                dve.wait_ge(u_in, 32 * KH)
                nc.vector.tensor_tensor(vv[:, :, :], x1[:, :, :], vv[:, :, :], ALU.mult).then_inc(u_ready, 1)
                dve.wait_ge(u_ready, 1)
                tokens = vv[:, :, :].rearrange("p q (a b) -> p q b a", b=R)
                dve.sem_inc(flip, 2)
                with dve.Fori(0, TILES // 2) as i:
                    for b in range(2):
                        dve.wait_ge(flip, 2 * i + b + 1)
                        for q in range(KH):
                            last = nc.vector.tensor_copy(ua[:, b, q, :].rearrange("p (g a) -> p g a", g=4),
                                                         tokens[:, q, ds(8 * i + 4 * b, 4), :])
                        last.then_inc(ua_ready, 1)
                for q in range(KH):
                    last = nc.vector.tensor_scalar(x1[:, q, :], vv[:, q, :], core.vec[:, VEC["skip"] + q:VEC["skip"] + q + 1], None, ALU.mult)
                last.then_inc(skip_done, 1)
                dve.wait_ge(skip_done, 1)

            @block.tensor
            def _(pe):
                pe.wait_ge(const_in, 32)
                with pe.Fori(0, TILES // 2) as i:
                    for b in range(2):
                        pe.wait_ge(ua_ready, 2 * i + b + 1)
                        for q in range(KH):
                            last = nc.tensor.transpose(ps1[:, b, ds(P * q, P)], ua[:, b, q, :], core.ident[:, :])
                        last.then_inc(flip, 1)
                    for b in range(2):
                        pe.wait_ge(ut_ready, 2 * i + b + 1)
                        for h in range(2):
                            last = nc.tensor.matmul(ps2[:, b, h, :], dft[:, h, :], ut[:, b, :], start=True, stop=True)
                        last.then_inc(s1_mm, 1)

            @block.scalar
            def _(act):
                with act.Fori(0, TILES // 2) as i:
                    for b in range(2):
                        act.wait_ge(flip, 2 * i + b + 3)
                        nc.scalar.activation(ut[:, b, :], ps1[:, b, :], ACT.Copy).then_inc(ut_ready, 1)
                    for b in range(2):
                        act.wait_ge(s1_mm, 2 * i + b + 1)
                        act.wait_ge(s1_stored[b], 32 * i + 16)
                        nc.scalar.activation(spec[:, b, :, :], ps2[:, b, :, :], ACT.Copy).then_inc(s1_out, 1)

            block_ctx.close()

        G = R // 2
        NB = 4
        ROUNDS = G // NB
        with ExitStack() as inner_ctx:
            isb = lambda n, s: inner_ctx.enter_context(nc.sbuf_tensor(f"hy_{n}", s, F32))
            tw = isb("tw", [P, NB, 5, P])
            au, ak = isb("au", [P, NB, D_HYENA]), isb("ak", [P, NB, D_HYENA])
            ka, kb = isb("ka", [P, 2, D_HYENA]), isb("kb", [P, 2, D_HYENA])
            prod = isb("prod", [P, 2, 2, D_HYENA])
            yy = isb("yy", [P, 2, D_HYENA])
            bo = isb("bo", [P, 2, D_HYENA])
            psg = inner_ctx.enter_context(nc.psum_tensor("hy_g_ps", [P, 2, 4, BANK], F32))
            g_in = [sem(f"g_in{b}") for b in range(NB)]
            b_stored = [sem(f"b_stored{b}") for b in range(2)]
            fwd_k, fwd_u, k_out, prods, y_ready, inv, b_out = (sem(n) for n in ("fwd_k", "fwd_u", "k_out", "prods", "y_ready", "inv", "b_out"))
            block_ctx = ExitStack()
            block = block_ctx.enter_context(nc.Block())
            FWD_LOADS = 5

            def staggered(engine, first, second):
                first(0, 0)
                with engine.Fori(0, ROUNDS - 1) as i:
                    for b in range(NB):
                        first(i + (b + 1) // NB, (b + 1) % NB)
                        second(i, b)
                for b in range(NB):
                    if b + 1 < NB:
                        first(ROUNDS - 1, b + 1)
                    second(ROUNDS - 1, b)

            @block.sync
            def _(sp):
                with sp.Fori(0, ROUNDS) as i:
                    for b in range(NB):
                        g = NB * i + b
                        sp.wait_ge(inv, g + 1)
                        sp.dma_start(tw[:, b, :, :], d["twiddle"][ds(g, 1)].rearrange("a p m n -> (a p) m n")).then_inc(g_in[b], 16)
                        for dst, src in ((ak, "spec_k"), (au, "spec_u")):
                            for c in range(2):
                                sp.dma_start(dst[64 * c:64 * c + 64, b, :], d[src][:, ds(2 * g + c, 1), :].rearrange("n a c -> n (a c)")
                                             ).then_inc(g_in[b], 16)

            @block.tensor
            def _(pe):
                def forward(i, b):
                    g = NB * i + b
                    pe.wait_ge(g_in[b], (16 * FWD_LOADS) * i + 16 * FWD_LOADS)
                    pe.wait_ge(k_out, g + 1)
                    nc.tensor.matmul(psg[:, b % 2, 2, :], tw[:, b, 2, :], ak[:, b, :], start=True, stop=True)
                    nc.tensor.matmul(psg[:, b % 2, 3, :], tw[:, b, 3, :], ak[:, b, :], start=True, stop=True).then_inc(fwd_k, 1)
                    pe.wait_ge(prods, g + 1)
                    nc.tensor.matmul(psg[:, b % 2, 1, :], tw[:, b, 1, :], au[:, b, :], start=True, stop=True)
                    pe.wait_ge(b_out, g + 1)
                    nc.tensor.matmul(psg[:, b % 2, 0, :], tw[:, b, 0, :], au[:, b, :], start=True, stop=True).then_inc(fwd_u, 1)

                def inverse(i, b):
                    pe.wait_ge(y_ready, NB * i + b + 1)
                    nc.tensor.matmul(psg[:, b % 2, 0, :], tw[:, b, 4, :], yy[:, b % 2, :], start=True, stop=True).then_inc(inv, 1)

                pe.sem_inc(inv, NB)
                staggered(pe, forward, inverse)

            @block.scalar
            def _(act):
                def copy_k(i, b):
                    act.wait_ge(fwd_k, NB * i + b + 1)
                    nc.scalar.activation(ka[:, b % 2, :], psg[:, b % 2, 2, :], ACT.Copy)
                    nc.scalar.activation(kb[:, b % 2, :], psg[:, b % 2, 3, :], ACT.Copy).then_inc(k_out, 1)

                def store(i, b):
                    g = NB * i + b
                    act.wait_ge(inv, g + NB + 1)
                    act.wait_ge(b_stored[b % 2], (16 * NB) * i + 32 * (b // 2) + 16)
                    nc.scalar.activation(bo[:, b % 2, :], psg[:, b % 2, 0, :], ACT.Copy).then_inc(b_out, 1)
                    act.wait_ge(b_out, g + 3)
                    for c in range(2):
                        act.dma_start(d["spec_y"][:, ds(2 * g + c, 1), :].rearrange("n a c -> n (a c)"),
                                      bo[64 * c:64 * c + 64, b % 2, :]).then_inc(b_stored[b % 2], 16)

                act.sem_inc(k_out, 2)
                act.sem_inc(b_out, 2)
                for b in range(2):
                    act.sem_inc(b_stored[b], 16)
                staggered(act, copy_k, store)
                for b in range(2):
                    act.wait_ge(b_stored[b], 16 + 16 * G)

            @block.vector
            def _(dve):
                dve.sem_inc(prods, 2)
                with dve.Fori(0, G // 2) as i:
                    for b in range(2):
                        dve.wait_ge(k_out, 2 * i + b + 3)
                        dve.wait_ge(fwd_u, 2 * i + b + 1)
                        nc.vector.tensor_tensor(prod[:, b, 1, :], psg[:, b, 1, :], kb[:, b, :], ALU.mult)
                        nc.vector.tensor_tensor(prod[:, b, 0, :], psg[:, b, 0, :], ka[:, b, :], ALU.mult).then_inc(prods, 1)

            @block.gpsimd
            def _(pool):
                with pool.Fori(0, G // 2) as i:
                    for b in range(2):
                        pool.wait_ge(prods, 2 * i + b + 3)
                        nc.gpsimd.tensor_tensor(yy[:, b, :], prod[:, b, 0, :], prod[:, b, 1, :], ALU.add).then_inc(y_ready, 1)

            block_ctx.close()

        with ExitStack() as inner_ctx:
            bt = inner_ctx.enter_context(nc.sbuf_tensor("hy_bt", [P, 2, 8, D_HYENA], F32))
            x0 = inner_ctx.enter_context(nc.sbuf_tensor("hy_x0", [P, KH, SEQ], F32))
            psy = inner_ctx.enter_context(nc.psum_tensor("hy_y_ps", [P, 2, KH, BANK], F32))
            bt_in = [sem(f"bt_in{b}") for b in range(2)]
            x0_in, y_mm, y_sum, y_done, y_stored = (sem(n) for n in ("x0_in", "y_mm", "y_sum", "y_done", "y_stored"))
            block_ctx = ExitStack()
            block = block_ctx.enter_context(nc.Block())
            TG = R // 16

            @block.sync
            def _(sp):
                sp.sem_inc(y_mm, 2)
                with sp.Fori(0, TG // 2) as i:
                    for b in range(2):
                        sp.wait_ge(y_mm, 2 * i + b + 1)
                        sp.dma_start(bt[:, b, :, :], d["spec_y"][ds(32 * i + 16 * b, 16)].rearrange("(t g) r c -> (g r) t c", g=2)
                                     ).then_inc(bt_in[b], 16)
                for q in range(KH):
                    sp.wait_ge(y_done, q + 1)
                    sp.dma_start(d["branches"][KH + q], x1[:, q, :]).then_inc(y_stored, 16)
                sp.wait_ge(y_stored, 16 * KH)

            @block.scalar
            def _(act):
                for q in range(KH):
                    act.dma_start(x0[:, q, :], d["proj"][HY0 + q]).then_inc(x0_in, 16)

            @block.tensor
            def _(pe):
                pe.wait_ge(const_in, 32)
                with pe.Fori(0, TG // 2) as i:
                    for b in range(2):
                        pe.wait_ge(bt_in[b], 16 * i + 16)
                        pe.wait_ge(y_sum, 2 * i + b + 1)
                        for t in range(8):
                            for q in range(KH):
                                last = nc.tensor.matmul(psy[:, b, q, ds(R * t, R)], bt[:, b, t, ds(P * q, P)], idft[:, :], start=True, stop=True)
                        last.then_inc(y_mm, 1)

            @block.vector
            def _(dve):
                dve.sem_inc(y_sum, 2)
                tokens = x1[:, :, :].rearrange("p q (a b) -> p q b a", b=R)
                with dve.Fori(0, TG // 2) as i:
                    for b in range(2):
                        dve.wait_ge(y_mm, 2 * i + b + 3)
                        for q in range(KH):
                            at = tokens[:, q, ds(32 * i + 16 * b, 16), :]
                            last = nc.vector.scalar_tensor_tensor(at, psy[:, b, q, :].rearrange("p (n a) -> p n a", a=SEQ // R),
                                                                  core.rnorm[:, q:q + 1], at, ALU.mult, ALU.add)
                        last.then_inc(y_sum, 1)
                dve.wait_ge(y_sum, TG + 2)
                dve.wait_ge(x0_in, 16 * KH)
                for q in range(KH):
                    nc.vector.tensor_tensor(x1[:, q, :], x1[:, q, :], x0[:, q, :], ALU.mult).then_inc(y_done, 1)

            block_ctx.close()
        clear(nc, sems)


def merge_phase(nc, core):
    d = core.d
    HALF = SEQ // 2
    ROUNDS = KD // 2
    with ExitStack() as ctx:
        sb, ps, sem, sems = scope(nc, ctx, "merge")
        act_hi, act_lo = sb("act_hi", [P, KD, HALF], F32R), sb("act_lo", [P, KD, HALF], F32R)
        mix_hi, mix_lo = sb("mix_hi", [P, KD, HALF], F32R), sb("mix_lo", [P, KD, HALF], F32R)
        w_raw = sb("w_raw", [P, 2, KD, P])
        w_hi = sb("w_hi", [P, 2, KD, P], F32R)
        w_lo = sb("w_lo", [P, 2, KD, P], F32R)
        zero = sb("zero", [P, 1])
        zeros = zero[:, :].unsqueeze(1).broadcast_to((P, KD, P))
        raw = sb("raw", [P, 2, HALF])
        gate = sb("gate", [P, 2, 2, HALF])
        out = sb("out", [P, 2, HALF])
        sq = sb("sq", [P, HALF])
        total = sb("total", [P, SEQ])
        acc = ps("acc", [P, 2, 2, HALF])
        w_in = [sem(f"w_in{b}") for b in range(2)]
        raw_in = [sem(f"raw_in{b}") for b in range(2)]
        gate_in = [sem(f"gate_in{b}") for b in range(2)]
        stored = [sem(f"stored{b}") for b in range(2)]
        zeroed, hi_done, w_ready, mm_done, split_hi, split_lo = (sem(n) for n in ("zeroed", "hi_done", "w_ready", "mm_done", "split_hi", "split_lo"))
        gated, merged, mix_hi_done, mix_lo_done, evac = (sem(n) for n in ("gated", "merged", "mix_hi_done", "mix_lo_done", "evac"))
        squared, summed, ms_done, eps_added, rooted, rs_done = (sem(n) for n in ("squared", "summed", "ms_done", "eps_added", "rooted", "rs_done"))
        block_ctx = ExitStack()
        block = block_ctx.enter_context(nc.Block())

        @block.sync
        def _(sp):
            def load_w(h, stage, i, b):
                c = 2 * KD * h + KD * stage + 2 * i + b
                if not isinstance(c, int) or c >= 2:
                    sp.wait_ge(w_ready, c - 1)
                sp.dma_start(w_raw[:, b, :, :], d["w_merge"][ds(2 * i + b + KD * stage, 1)].rearrange("a p k n -> (a p) k n")).then_inc(w_in[b], 16)

            def load_gates(h, i, b):
                n = 2 * i + b
                if not isinstance(n, int) or KD * h + n >= 2:
                    sp.wait_ge(merged, KD * h + n - 1)
                for m in range(2):
                    sp.dma_start(gate[:, b, m, :], d["proj"][ds(n + (GATE0 + KD * m), 1), :, HALF * h:HALF * (h + 1)].rearrange("a p t -> (a p) t")
                                 ).then_inc(gate_in[b], 16)

            def load_raw(h, i, b):
                n = 2 * i + b
                if not isinstance(n, int) or KD * h + n >= 2:
                    sp.wait_ge(split_lo, KD * h + n - 1)
                sp.dma_start(raw[:, b, :], d["branches"][ds(n, 1), :, HALF * h:HALF * (h + 1)].rearrange("a p t -> (a p) t")).then_inc(raw_in[b], 16)

            for b in range(2):
                load_w(0, 0, 0, b)
                load_raw(0, 0, b)
            for b in range(2):
                load_gates(0, 0, b)
            for i in range(1, ROUNDS):
                for b in range(2):
                    load_raw(0, i, b)
            for h in range(2):
                with sp.Fori(1 - h, ROUNDS) as i:
                    for b in range(2):
                        load_w(h, 0, i, b)
                        load_gates(h, i, b)
                with sp.Fori(0, ROUNDS) as i:
                    for b in range(2):
                        load_w(h, 1, i, b)
                        if h == 0:
                            load_raw(1, i, b)

        @block.gpsimd
        def _(pool):
            pool.memset(zero[:, :], 0.0).then_inc(zeroed, 1)
            pool.wait_ge(zeroed, 1)
            with pool.Fori(0, 4 * ROUNDS) as i:
                for b in range(2):
                    weight_splitter(nc, pool, i, b, 0, zeros, w_in, w_raw, w_hi, w_lo, hi_done, w_ready, mm_done)

        @block.tensor
        def _(pe):
            def mix(h, i, b):
                n = 2 * i + b
                pe.wait_ge(w_ready, 2 * KD * h + n + 1)
                if not isinstance(n, int) or n >= 2:
                    pe.wait_ge(gated, KD * h + n - 1)
                elif h:
                    pe.wait_ge(evac, KD * (h - 1) + KD - 1 + b)
                for m in range(2):
                    for g in range(HALF // BANK):
                        at = ds(BANK * g, BANK)
                        for k in range(KH * m, KH * m + KH):
                            if isinstance(n, int) and n == 0 and g == 0:
                                pe.wait_ge(split_lo, KD * h + k + 1)
                            last = product(nc, acc[:, b, m, at], w_hi[:, b, k, :], w_lo[:, b, k, :],
                                           act_hi[:, k, at], act_lo[:, k, at], k == KH * m, k == KH * m + KH - 1)
                last.then_inc(mm_done, 1)

            def project(h, i, b):
                n = 2 * i + b
                pe.wait_ge(w_ready, 2 * KD * h + KD + n + 1)
                if isinstance(n, int) and n < 2:
                    pe.wait_ge(gated, KD * h + KD - 1 + b)
                else:
                    pe.wait_ge(evac, KD * h + n - 1)
                for g in range(HALF // BANK):
                    at = ds(BANK * g, BANK)
                    for k in range(KD):
                        if isinstance(n, int) and n == 0 and g == 0:
                            pe.wait_ge(mix_lo_done, KD * h + k + 1)
                        last = product(nc, acc[:, b, 0, at], w_hi[:, b, k, :], w_lo[:, b, k, :], mix_hi[:, k, at], mix_lo[:, k, at], k == 0, k == KD - 1)
                last.then_inc(mm_done, 1)

            pe.sem_inc(mm_done, 2)
            for h in range(2):
                for stage in (mix, project):
                    for b in range(2):
                        stage(h, 0, b)
                    with pe.Fori(1, ROUNDS) as i:
                        for b in range(2):
                            stage(h, i, b)
            pe.wait_ge(summed, 2 * KD + 1)
            fold_mean_square(nc, core, acc[:, 0, 0, :], total).then_inc(ms_done, 1)

        @block.scalar
        def _(act):
            def split(h, i, b):
                act.wait_ge(raw_in[b], (8 * KD) * h + 16 * i + 16)
                nc.scalar.activation(act_hi[:, ds(2 * i + b, 1), :].rearrange("p a t -> p (a t)"), raw[:, b, :], ACT.Copy).then_inc(split_hi, 1)

            for b in range(2):
                act.sem_inc(stored[b], 16)
            for i in range(ROUNDS):
                for b in range(2):
                    split(0, i, b)
            for h in range(2):
                with act.Fori(0, ROUNDS) as i:
                    for b in range(2):
                        act.wait_ge(merged, 2 * i + b + (KD * h + 1))
                        nc.scalar.activation(mix_hi[:, ds(2 * i + b, 1), :].rearrange("p a t -> p (a t)"), out[:, b, :], ACT.Copy).then_inc(mix_hi_done, 1)
                with act.Fori(0, ROUNDS) as i:
                    for b in range(2):
                        n = 2 * i + b
                        act.wait_ge(mm_done, n + (2 * KD * h + KD + 3))
                        act.wait_ge(squared, n + (KD * h + 1))
                        act.wait_ge(stored[b], 16 * i + (8 * KD * h + 16))
                        nc.scalar.activation(out[:, b, :], acc[:, b, 0, :], ACT.Copy).then_inc(evac, 1)
                        act.wait_ge(evac, n + (KD * h + 1))
                        act.dma_start(d["branch"][ds(n, 1), :, HALF * h:HALF * (h + 1)].rearrange("a p t -> (a p) t"), out[:, b, :]
                                      ).then_inc(stored[b], 16)
                        if h == 0:
                            split(1, i, b)
            root_on_act(nc, core, act, eps_added, rooted)
            for b in range(2):
                act.wait_ge(stored[b], 16 * (KD + 1))

        @block.vector
        def _(dve):
            def split(h, i, b):
                at = ds(2 * i + b, 1)
                dve.wait_ge(split_hi, KD * h + 2 * i + b + 1)
                nc.vector.tensor_tensor(act_lo[:, at, :].rearrange("p a t -> p (a t)"), raw[:, b, :],
                                        act_hi[:, at, :].rearrange("p a t -> p (a t)").bitcast(F32), ALU.subtract).then_inc(split_lo, 1)

            nc.vector.memset(total[:, :], 0.0).then_inc(summed, 1)
            dve.sem_inc(squared, 2)
            for i in range(ROUNDS):
                for b in range(2):
                    split(0, i, b)
            for h in range(2):
                if h:
                    for b in range(2):
                        dve.wait_ge(stored[b], 8 * KD * h + 16)
                with dve.Fori(0, ROUNDS) as i:
                    for b in range(2):
                        n, at = 2 * i + b, ds(2 * i + b, 1)
                        dve.wait_ge(gate_in[b], (16 * KD) * h + 32 * i + 32)
                        dve.wait_ge(mm_done, n + (2 * KD * h + 3))
                        nc.vector.tensor_tensor(gate[:, b, :, :], acc[:, b, :, :], gate[:, b, :, :], ALU.mult).then_inc(gated, 1)
                        dve.wait_ge(gated, n + (KD * h + 1))
                        nc.vector.tensor_tensor(out[:, b, :], gate[:, b, 0, :], gate[:, b, 1, :], ALU.add).then_inc(merged, 1)
                        dve.wait_ge(mix_hi_done, n + (KD * h + 1))
                        nc.vector.tensor_tensor(mix_lo[:, at, :].rearrange("p a t -> p (a t)"), out[:, b, :],
                                                mix_hi[:, at, :].rearrange("p a t -> p (a t)").bitcast(F32), ALU.subtract).then_inc(mix_lo_done, 1)
                dve.wait_ge(mix_lo_done, KD * h + KD)
                with dve.Fori(0, ROUNDS) as i:
                    for b in range(2):
                        n, part = 2 * i + b, total[:, HALF * h:HALF * (h + 1)]
                        dve.wait_ge(summed, n + (KD * h + 1))
                        dve.wait_ge(evac, n + (KD * h + 1))
                        nc.vector.tensor_tensor(sq[:, :], out[:, b, :], out[:, b, :], ALU.mult).then_inc(squared, 1)
                        dve.wait_ge(squared, n + (KD * h + 3))
                        nc.vector.tensor_tensor(part, part, sq[:, :], ALU.add).then_inc(summed, 1)
                        if h == 0:
                            split(1, i, b)
            rs_on_dve(nc, core, dve, acc[:, 0, 0, :], ms_done, eps_added, rooted, rs_done)

        block_ctx.close()
        clear(nc, sems)


def down_phase(nc, core):
    d = core.d
    with ExitStack() as ctx:
        sb, ps, sem, sems = scope(nc, ctx, "down")
        w_hi = sb("w_hi", [P, FF_CHUNKS, D_MODEL], F32R)
        w_lo = sb("w_lo", [P, FF_CHUNKS, D_MODEL], F32R)
        raw = sb("raw", [P, 2, D_MODEL])
        r_raw, x_raw = raw[:, :, 0:BANK], raw[:, :, BANK:2 * BANK]
        g_raw = sb("g_raw", [P, 2, BANK])
        g_hi, g_lo = sb("g_hi", [P, 2, BANK], F32R), sb("g_lo", [P, 2, BANK], F32R)
        out = sb("out", [P, 2, BANK])
        total, rs = sb("total", [P, BANK]), sb("rs", [P, BANK])
        gain = sb("gain", [P, KD])
        acc = ps("acc", [P, KD, BANK])
        w_in = [sem(f"w_in{b}") for b in range(2)]
        g_in = [sem(f"g_in{b}") for b in range(2)]
        stored = [sem(f"stored{b}") for b in range(2)]
        rx_in = [sem(f"rx_in{b}") for b in range(2)]
        final_stored = [sem(f"final_stored{b}") for b in range(2)]
        w_hi_done, w_lo_done, g_hi_done, g_ready, mm_done, out_mm, evac = (
            sem(n) for n in ("w_hi_done", "w_lo_done", "g_hi_done", "g_ready", "mm_done", "out_mm", "evac"))
        gained, squared, summed, ms_done, ms_read, rooted, rs_done, scaled, final = (
            sem(n) for n in ("gained", "squared", "summed", "ms_done", "ms_read", "rooted", "rs_done", "scaled", "final"))
        GROUPS = SEQ // BANK
        last_x = [x_raw[:, 0, :], x_raw[:, 1, :], g_raw[:, 0, :], g_raw[:, 1, :]]
        last_in = [sem(f"last_in{b}") for b in range(4)]
        last_stored = [sem(f"last_stored{b}") for b in range(4)]
        FIRST = 4
        block_ctx = ExitStack()
        block = block_ctx.enter_context(nc.Block())

        @block.sync
        def _(sp):
            def load(t, k):
                sp.wait_ge(g_ready, FF_CHUNKS * t + k + 1)
                sp.dma_start(g_raw[:, k % 2, :], d["hidden"][k, :, ds(BANK * t, BANK)]).then_inc(g_in[k % 2], 16)

            def load_rx(t, n):
                b = n % 2
                at = ds(BANK * t - BANK, BANK)
                in_order = (8 * KD) * (t - 1) + 16 * (n // 2 + 2)
                if n < 2:
                    sp.wait_ge(summed, (KD - 1) * t)
                sp.wait_ge(final_stored[b], in_order)
                sp.wait_ge(stored[b], in_order)
                if n >= 2:
                    sp.wait_ge(final, KD * t + n - 1)
                sp.dma_start(r_raw[:, b, :], d["branch"][n, :, at]).then_inc(rx_in[b], 16)
                sp.dma_start(x_raw[:, b, :], d["x1"][n, :, at]).then_inc(rx_in[b], 16)

            def store(t, n):
                at = ds(BANK * t - BANK, BANK)
                sp.wait_ge(final, KD * t + n + 1)
                sp.dma_start(d["out"][n, :, at], x_raw[:, n % 2, :]).then_inc(final_stored[n % 2], 16)

            for b in range(2):
                sp.sem_inc(final_stored[b], 32)
            for k in range(FF_CHUNKS):
                if k >= 2:
                    sp.wait_ge(w_lo_done, k - 1)
                sp.dma_start(raw[:, k % 2, :], d["w_down"][k]).then_inc(w_in[k % 2], 16)
                load(0, k)
            with sp.Fori(1, GROUPS) as t:
                for k in range(FF_CHUNKS):
                    load(t, k)
                    if FIRST + 2 <= k < FIRST + 2 + KD:
                        store(t, k - FIRST - 2)
                    if FIRST <= k < FIRST + KD:
                        load_rx(t, k - FIRST)
            at = slice(SEQ - BANK, SEQ)
            for n in range(KD + 2):
                if n >= 2:
                    sp.wait_ge(final, KD * GROUPS + n - 1)
                    sp.dma_start(d["out"][n - 2, :, at], last_x[(n - 2) % 4]).then_inc(last_stored[(n - 2) % 4], 16)
                if n < KD:
                    if n < 2:
                        sp.wait_ge(final_stored[n], 8 * KD * (GROUPS - 1) + 32)
                    elif n < 4:
                        sp.wait_ge(g_ready, FF_CHUNKS * GROUPS + 2)
                    else:
                        sp.wait_ge(last_stored[n % 4], 16 * (n // 4))
                    sp.dma_start(last_x[n % 4], d["x1"][n, :, at]).then_inc(last_in[n % 4], 16)
            for b in range(4):
                sp.wait_ge(last_stored[b], 16 * KD // 4)

        @block.gpsimd
        def _(pool):
            with pool.Fori(0, GROUPS) as t:
                for n in range(1, KD):
                    pool.wait_ge(squared, KD * t + n + 3)
                    if n > 1:
                        pool.wait_ge(summed, (KD - 1) * t + n - 1)
                    nc.gpsimd.tensor_tensor(total[:, :], total[:, :], r_raw[:, n % 2, :], ALU.add).then_inc(summed, 1)

        @block.tensor
        def _(pe):
            def mean_square(t):
                pe.wait_ge(summed, (KD - 1) * t)
                pe.wait_ge(evac, KD * t + KD)
                nc.tensor.matmul(acc[:, KD - 1, :], core.mean[:, :], total[:, :], start=True, stop=True).then_inc(ms_done, 1)

            def group(t):
                for k in range(FF_CHUNKS):
                    if isinstance(t, int):
                        pe.wait_ge(w_lo_done, k + 1)
                    pe.wait_ge(g_ready, FF_CHUNKS * t + k + 3)
                    for n in range(KD):
                        if k == 0:
                            if n == KD - 1 and not isinstance(t, int):
                                mean_square(t)
                                pe.wait_ge(ms_read, t)
                            else:
                                pe.wait_ge(evac, KD * t + n + 1)
                        w = slice(P * n, P * n + P)
                        last = product(nc, acc[:, n, :], w_hi[:, k, w], w_lo[:, k, w], g_hi[:, k % 2, :], g_lo[:, k % 2, :],
                                       k == 0, k == FF_CHUNKS - 1)
                        if k == FF_CHUNKS - 1:
                            last.then_inc(out_mm, 1)
                    if k < FF_CHUNKS - 1:
                        last.then_inc(mm_done, 1)
                    else:
                        pe.wait_ge(out_mm, KD * t + KD)
                        pe.sem_inc(mm_done, 1)

            group(0)
            with pe.Fori(1, GROUPS) as t:
                group(t)
            mean_square(GROUPS)

        @block.scalar
        def _(act):
            def hidden_hi(t, k):
                act.wait_ge(g_in[k % 2], (16 * (FF_CHUNKS // 2)) * t + 16 * (k // 2 + 1))
                act.wait_ge(mm_done, FF_CHUNKS * t + k + 1)
                nc.scalar.activation(g_hi[:, k % 2, :], g_raw[:, k % 2, :], ACT.Copy).then_inc(g_hi_done, 1)

            def results(t, to_dram=True):
                for n in range(KD):
                    act.wait_ge(out_mm, KD * t + n + 1)
                    act.wait_ge(squared, KD * t + n + 1)
                    if to_dram or n < 2:
                        act.wait_ge(stored[n % 2], (16 * (KD // 2)) * t + 16 * (n // 2 + 1))
                    nc.scalar.activation(out[:, n % 2, :], acc[:, n, :], ACT.Copy).then_inc(evac, 1)
                    if not to_dram:
                        continue
                    act.wait_ge(evac, KD * t + n + 1 + KD)
                    act.dma_start(d["branch"][n, :, ds(BANK * t, BANK)], out[:, n % 2, :]).then_inc(stored[n % 2], 16)

            def root(t):
                act.wait_ge(ms_read, t)
                nc.scalar.activation(rs[:, :], rs[:, :], ACT.Sqrt).then_inc(rooted, 1)

            act.sem_inc(evac, KD)
            act.sem_inc(mm_done, 2)
            for b in range(2):
                act.sem_inc(stored[b], 16)
            for k in range(FF_CHUNKS):
                act.wait_ge(w_in[k % 2], 16 * (k // 2 + 1))
                nc.scalar.activation(w_hi[:, k, :], raw[:, k % 2, :], ACT.Copy).then_inc(w_hi_done, 1)
                hidden_hi(0, k)
            with act.Fori(1, GROUPS) as t:
                hidden_hi(t, 0)
                results(t - 1)
                hidden_hi(t, 1)
                root(t)
                for k in range(2, FF_CHUNKS):
                    hidden_hi(t, k)
            results(GROUPS - 1, to_dram=False)
            root(GROUPS)

        @block.vector
        def _(dve):
            def hidden_lo(t, k):
                dve.wait_ge(g_hi_done, FF_CHUNKS * t + k + 1)
                nc.vector.tensor_tensor(g_lo[:, k % 2, :], g_raw[:, k % 2, :], g_hi[:, k % 2, :].bitcast(F32), ALU.subtract).then_inc(g_ready, 1)

            def squares(t):
                dve.wait_ge(final, KD * t)
                for n in range(KD):
                    dve.wait_ge(evac, KD * t + n + 1)
                    if n > 2:
                        dve.wait_ge(summed, (KD - 1) * (t - 1) + n - 2)
                    nc.vector.tensor_tensor(r_raw[:, n % 2, :] if n else total[:, :], out[:, n % 2, :], out[:, n % 2, :], ALU.mult
                                            ).then_inc(squared, 1)

            def inverse_rms(t):
                dve.wait_ge(ms_done, t)
                nc.vector.tensor_scalar(rs[:, :], acc[:, KD - 1, :], RMS_EPS, None, ALU.add).then_inc(ms_read, 1)
                dve.wait_ge(rooted, t)
                nc.vector.reciprocal(rs[:, :], rs[:, :]).then_inc(rs_done, 1)
                dve.wait_ge(rs_done, t)

            def residual(t, n):
                b = n % 2
                dve.wait_ge(rx_in[b], (16 * KD) * (t - 1) + 32 * (n // 2 + 1))
                nc.vector.tensor_tensor(r_raw[:, b, :], r_raw[:, b, :], rs[:, :], ALU.mult).then_inc(scaled, 1)
                dve.wait_ge(scaled, KD * (t - 1) + n + 1)
                nc.vector.scalar_tensor_tensor(x_raw[:, b, :], r_raw[:, b, :], gain[:, n:n + 1], x_raw[:, b, :], ALU.mult, ALU.add).then_inc(final, 1)

            nc.vector.tensor_tensor(gain[:, :], core.mod[:, G_FFN:G_FFN + KD, 0], core.vec[:, VEC["ffn_post"]:VEC["ffn_post"] + KD], ALU.mult
                                    ).then_inc(gained, 1)
            dve.wait_ge(gained, 1)
            dve.sem_inc(g_ready, 2)
            dve.sem_inc(final, KD)
            dve.sem_inc(squared, 2)
            for k in range(FF_CHUNKS):
                dve.wait_ge(w_hi_done, k + 1)
                nc.vector.tensor_tensor(w_lo[:, k, :], raw[:, k % 2, :], w_hi[:, k, :].bitcast(F32), ALU.subtract).then_inc(w_lo_done, 1)
                hidden_lo(0, k)
            dve.wait_ge(w_lo_done, FF_CHUNKS)
            with dve.Fori(1, GROUPS) as t:
                hidden_lo(t, 0)
                squares(t)
                hidden_lo(t, 1)
                inverse_rms(t)
                for k in range(2, FF_CHUNKS):
                    hidden_lo(t, k)
                    if FIRST + 1 <= k < FIRST + 1 + KD:
                        residual(t, k - FIRST - 1)
            squares(GROUPS)
            inverse_rms(GROUPS)
            for n in range(KD):
                src = acc[:, n, :] if n < KD - 1 else out[:, n % 2, :]
                x, done = last_x[n % 4], KD * (GROUPS - 1) + n
                if n >= 2:
                    dve.wait_ge(final, KD + done - 1)
                nc.vector.tensor_tensor(r_raw[:, n % 2, :], src, rs[:, :], ALU.mult).then_inc(scaled, 1)
                dve.wait_ge(scaled, done + 1)
                dve.wait_ge(last_in[n % 4], 16 * (n // 4 + 1))
                nc.vector.scalar_tensor_tensor(x, r_raw[:, n % 2, :], gain[:, n:n + 1], x, ALU.mult, ALU.add).then_inc(final, 1)

        block_ctx.close()
        clear(nc, sems)


def layer_program(nc, d):
    core = Core(nc, d)
    for name, shape in (("proj", (IN_CHUNKS, P, SEQ)), ("ctx_kv", (2 * KH, P, CTX_LEN)), ("rotated", (V0, P, SEQ)), ("branches", (KD, P, SEQ)),
                        ("branch", (KD, P, SEQ)), ("x1", (KD, P, SEQ)), ("hidden", (FF_CHUNKS, P, SEQ)),
                        ("spec_k", (R, R, D_HYENA)), ("spec_u", (R, R, D_HYENA)), ("spec_y", (R, R, D_HYENA))):
        d[name] = nc.dram_tensor(f"scratch_{name}", shape, F32).ap()
    with ExitStack() as ctx:
        core.vec = ctx.enter_context(nc.sbuf_tensor("vec", [P, N_VEC], F32))
        core.mod = ctx.enter_context(nc.sbuf_tensor("mod", [P, MOD_CHUNKS, 2], F32))
        core.mean = ctx.enter_context(nc.sbuf_tensor("mean", [P, P], F32))
        core.rnorm = ctx.enter_context(nc.sbuf_tensor("rnorm", [P, KH], F32))
        before_down = ctx.enter_context(ExitStack())
        core.pick = before_down.enter_context(nc.sbuf_tensor("pick", [P, SEQ // BANK, P], F32))
        core.rs = before_down.enter_context(nc.sbuf_tensor("rs", [P, BANK], F32))
        core.ident = before_down.enter_context(nc.sbuf_tensor("ident", [P, P], F32))
        setup_phase(nc, core)
        filter_phase(nc, core)

        def operand(stack, tag, tokens):
            return (stack.enter_context(nc.sbuf_tensor(f"{tag}_hi", [P, KD, tokens], F32R)),
                    stack.enter_context(nc.sbuf_tensor(f"{tag}_lo", [P, KD, tokens], F32R)))

        with ExitStack() as s:
            hi, lo = operand(s, "ctx_act", CTX_LEN)
            norm_phase(nc, core, "norm_ctx", d["ctx"], CTX_LEN, hi, lo, VEC["mix_pre"], 1, SH_MIX, SC_MIX)
            projection_phase(nc, core, "proj_ctx", d["w_in"], [("bias", K0, 2 * KH, d["ctx_kv"], VEC["b_in"] + K0)], hi, lo, CTX_LEN)
        with ExitStack() as s:
            hi, lo = operand(s, "mix_act", SEQ)
            projection_phase(nc, core, "proj_mix", d["w_in"], [
                (kind, first, last - first, d["proj"][first:last], VEC["b_in"] + first)
                for kind, first, last in (("query", Q0, K0), ("bias", K0, HY0), ("conv", HY0, GATE0), ("sigmoid", GATE0, IN_CHUNKS))],
                hi, lo, SEQ, rotary=(d["rotated"], d["proj"][Q0:V0]), norm=(d["x"], VEC["mix_pre"], SH_MIX, SC_MIX, False))
        attention_phase(nc, core)
        hyena_phase(nc, core)
        merge_phase(nc, core)
        with nc.sbuf_tensor("x1", [P, KD, SEQ], F32) as x1:
            residual_phase(nc, core, x1)
        with ExitStack() as s:
            lo = s.enter_context(nc.sbuf_tensor("ffn_act_lo", [P, KD, SEQ], F32R))
            hi = s.enter_context(nc.sbuf_tensor("ffn_act_hi", [P, KD, SEQ], F32R))
            projection_phase(nc, core, "proj_up", d["w_up"], [("ffn", 0, 2 * FF_CHUNKS, d["hidden"], None)], hi, lo, SEQ,
                             norm=(x1, VEC["ffn_pre"], SH_FFN, SC_FFN, True))
        before_down.close()
        down_phase(nc, core)


def frequencies(g):
    if g:
        return [(g + R * k2, part) for part in ("re", "im") for k2 in range(R)]
    return ([(R * k2, "re") for k2 in range(33)] + [(32 + R * k2, "re") for k2 in range(32)]
            + [(R * k2, "im") for k2 in range(1, 32)] + [(32 + R * k2, "im") for k2 in range(32)])


def root(e):
    return np.exp(-2j * np.pi * np.asarray(e) / NFFT)


def stage1(n1):
    m = np.zeros((len(n1), R))
    for g in range(R // 2):
        for c in range(2):
            if g == 0:
                m[:, c] = root(R * n1 * (32 * c)).real
            else:
                z = root(R * n1 * g)
                m[:, 2 * g + c] = z.imag if c else z.real
    return m


def inverse_stage1(n1):
    m = np.zeros((R, len(n1)))
    for g in range(R // 2):
        for c in range(2):
            if g == 0:
                m[c] = root(R * n1 * (32 * c)).real
            else:
                z = np.conj(root(R * n1 * g))
                m[2 * g + c] = -z.imag if c else z.real
    return m


def twiddles():
    n2 = np.arange(R)
    groups = []
    for g in range(R // 2):
        rows = frequencies(g)

        def forward(rows):
            m = np.zeros((P, P))
            for i, (k, part, sign) in enumerate(rows):
                z = root(n2 * k) * sign
                if g:
                    m[:R, i], m[R:, i] = (z.real, -z.imag) if part == "re" else (z.imag, z.real)
                else:
                    c = int(k % R != 0)
                    m[R * c:R * c + R, i] = z.real if part == "re" else z.imag
            return m

        other = {"re": "im", "im": "re"}
        real = lambda k: k % (NFFT // 2) == 0
        x = forward([(k, part, 1) for k, part in rows])
        xs = forward([(k, other[part], 0 if real(k) else (-1 if part == "re" else 1)) for k, part in rows])
        ka = forward([(k, "re", 1) for k, part in rows])
        kb = forward([(k, "im", 0 if real(k) else 1) for k, part in rows])
        inv = np.zeros((P, P))
        for i, (k, part) in enumerate(rows):
            z = np.conj(root(n2 * k)) * ((1 if real(k) else 2) / NFFT)
            v = z if part == "re" else 1j * z
            if g:
                inv[i, :R], inv[i, R:] = v.real, v.imag
            else:
                c = int(k % R != 0)
                inv[i, R * c:R * c + R] = v.real
        groups.append(np.stack([x, xs, ka, kb, inv], 1))
    return np.array(groups)


def shape_constants():
    f = np.float32
    c = {}
    c["ident"] = np.eye(P, dtype=f)
    c["fold"] = np.tile(np.eye(HEAD_DIM, dtype=f), (2, 1))
    c["mean"] = np.full((P, P), 1.0 / D_MODEL, f)
    pick = np.zeros((P, SEQ // BANK, P), f)
    for g in range(SEQ // BANK):
        pick[32 * g, g] = 1.0
    c["pick"] = pick
    j, side, g, n1 = np.meshgrid(np.arange(R // 2), np.arange(2), np.arange(2), np.arange(32), indexing="ij")
    n = (R * (32 * side + n1) + 2 * j + g).reshape(-1)
    pos = np.where(n <= SEQ, n, NFFT - n).astype(f)
    t = pos / f(SEQ - 1)
    bands = np.linspace(1e-4, POS_BANDS - 1, POS_BANDS, dtype=f)
    ang = (f(2.0 * np.pi / SEQ) * pos)[:, None] * bands[None, :]
    c["z"] = np.ascontiguousarray(np.concatenate([t[:, None], np.cos(ang), -np.sin(ang)], 1).astype(f).T)
    c["neg_t"] = np.ascontiguousarray(-t.reshape(-1, P).T)
    c["keep"] = np.ascontiguousarray((n != SEQ).astype(f).reshape(-1, P).T)
    s1 = stage1(np.arange(R))
    dft_k = np.zeros((2, 2, 32, 2, R))
    for gg in range(2):
        for side in range(2):
            dft_k[side, gg, :, gg, :] = s1[32 * side:32 * side + 32]
    c["dft_k"] = dft_k.reshape(P, P).astype(f)
    dft_u = np.zeros((4, 32, 2, 2, R))
    for gg in range(4):
        dft_u[gg, :, gg // 2, gg % 2, :] = s1[:32]
    c["dft_u"] = dft_u.reshape(P, 2, P).astype(f)
    idft = np.zeros((2, R, 2, 32))
    for gg in range(2):
        idft[gg, :, gg, :] = inverse_stage1(np.arange(32))
    c["idft"] = idft.reshape(P, R).astype(f)
    c["twiddle"] = twiddles().astype(f)
    tok = np.arange(SEQ)
    inv_freq = (f(10000.0) ** (-np.arange(16, dtype=f) / f(16))).astype(f)
    cos, sin = np.zeros((P, SEQ), f), np.zeros((P, SEQ), f)
    for i, ch in enumerate(np.tile(HEAD_ORDER, 2)):
        axis = (tok // GRID_W, tok % GRID_W)[ch // 32].astype(f)
        a = axis * inv_freq[ch % 16]
        cos[i], sin[i] = np.cos(a), np.sin(a) * (-1 if ch % 32 < 16 else 1)
    c["cos"], c["sin"] = cos.reshape(P, 2, SEQ // 2), sin.reshape(P, 2, SEQ // 2)
    qc, kc = np.arange(GRID_W)[:, None], np.arange(GRID_W)[None, :]
    start = np.clip(qc - WIN_COLS // 2, 0, GRID_W - WIN_COLS)
    mask = np.where((kc >= start) & (kc < start + WIN_COLS), 0.0, MASKED).astype(f)
    c["colmask"] = np.tile(mask, (2, 1))
    return c


def laid_out(x, c, ctx, c_ctx, w_mod, b_mod, norm_mix_pre, norm_mix_post, norm_ffn_pre, norm_ffn_post,
             w_in, b_in, na_rpb, hy_conv_w, hy_conv_b, hy_filt_w1, hy_filt_b1, hy_filt_w2, hy_filt_b2,
             hy_filt_w3, hy_filt_b3, hy_sin_freq, hy_decay, hy_skip, w_o_na, w_o_hy, w_out,
             ffn_w_up, ffn_conv_w, ffn_conv_b, ffn_w_down):
    def tiles(w):
        k, n = w.shape[0] // P, w.shape[1] // P
        return np.ascontiguousarray(w.reshape(k, P, n, P).transpose(2, 1, 0, 3))

    def cols(v):
        return np.asarray(v).reshape(-1, P).T

    def pairs(v):
        s = v.shape[:-1]
        return np.swapaxes(v.reshape(*s, 2, FF_CHUNKS, P), -3, -2).reshape(*s, 2 * D_FF)

    def head_order(v):
        n = 2 * D_ATTN
        qk = v[..., :n].reshape(*v.shape[:-1], n // HEAD_DIM, HEAD_DIM)[..., HEAD_ORDER]
        return np.concatenate([qk.reshape(*v.shape[:-1], n), v[..., n:]], -1)

    a = {}
    a["x"] = np.ascontiguousarray(x[0].T).reshape(KD, P, SEQ)
    a["ctx"] = np.ascontiguousarray(ctx[0].T).reshape(KD, P, CTX_LEN)
    a["cond"] = np.ascontiguousarray(np.stack([cols(c[0]), cols(c_ctx)], -1))
    a["w_mod"] = np.ascontiguousarray(w_mod[0].reshape(2, KD // 2, P, MOD_CHUNKS * P).transpose(2, 0, 1, 3))
    a["w_in"] = tiles(head_order(w_in[0]))
    a["w_merge"] = np.concatenate([tiles(np.concatenate([w_o_na[0], w_o_hy[0]])), tiles(w_out[0])])
    a["w_up"] = tiles(pairs(ffn_w_up[0]))
    a["w_down"] = np.ascontiguousarray(ffn_w_down[0].reshape(FF_CHUNKS, P, D_MODEL))
    cw, fw = hy_conv_w[0], pairs(ffn_conv_w[0])
    a["vec"] = np.ascontiguousarray(np.concatenate([cols(v) for v in (
        head_order(b_in[0]), b_mod[0], norm_mix_pre[0], norm_mix_post[0], norm_ffn_pre[0], norm_ffn_post[0],
        cw[0], cw[1], cw[2], hy_conv_b[0], hy_skip[0], fw[0], fw[1], fw[2], pairs(ffn_conv_b[0]))], 1))
    a["filt_w1"], a["filt_w2"], a["filt_w3"] = hy_filt_w1[0], hy_filt_w2[0], hy_filt_w3[0]
    a["filt_hid"] = np.ascontiguousarray(np.stack([hy_filt_b1[0], hy_sin_freq[0, 0], hy_filt_b2[0], hy_sin_freq[0, 1]], 1))
    a["filt_b3"] = hy_filt_b3[0].reshape(2, D_HYENA)
    a["decay"] = hy_decay[0]
    qc, kc = np.arange(GRID_W)[:, None], np.arange(GRID_W)[None, :]
    dc = np.clip(kc - qc, 1 - WIN_COLS, WIN_COLS - 1) + WIN_COLS - 1
    rel = na_rpb[0][:, :, dc].transpose(0, 2, 1, 3)
    a["rpb"] = np.ascontiguousarray(np.stack([rel[:, :, 1 - qr:15 - qr] for qr in range(2)], 1)).reshape(N_HEADS, P, 14 * GRID_W)
    return a


def kernel(**inputs):
    import concourse.bacc as bacc
    from concourse.bass_utils import run_bass_kernel_spmd

    arrays = {**laid_out(**{k: np.asarray(v) for k, v in inputs.items()}), **shape_constants()}
    nc = bacc.Bacc("TRN2", target_bir_lowering=False, num_devices=1)
    d = {n: nc.dram_tensor(f"in_{n}", a.shape, mybir.dt.from_np(a.dtype), kind="ExternalInput").ap() for n, a in arrays.items()}
    d["out"] = nc.dram_tensor("out", (KD, P, SEQ), F32, kind="ExternalOutput").ap()
    layer_program(nc, d)
    result = run_bass_kernel_spmd(nc, [{f"in_{n}": np.ascontiguousarray(a) for n, a in arrays.items()}], core_ids=[0])
    return np.ascontiguousarray(result.results[0]["out"].reshape(D_MODEL, SEQ).T)[None]
```
